# Optimizing a Trainium2 kernel written in Bass

```python
import math
import jax
import jax.numpy as jnp
from jax import lax
import numpy as np

D_MODEL = 1024
BATCH = 1
SEQ = 256
DEPTH = 2

CTX_LEN = 256
GRID_W = 64
N_MIXERS = 2
N_HGRN = (DEPTH + 1) // 2
N_MAMBA = DEPTH // 2
EPS = 1e-6

HG_HEADS = 8
HG_KDIM = 128
HG_VDIM = D_MODEL // HG_HEADS
HG_KEY = HG_HEADS * HG_KDIM
HG_CHUNK = 16
HG_IN = 3 * HG_KEY + 2 * D_MODEL
HG_SPLITS = [HG_KEY, HG_KEY + D_MODEL, 2 * HG_KEY + D_MODEL, 3 * HG_KEY + D_MODEL]

MB_EXPAND = 2
MB_INNER = MB_EXPAND * D_MODEL
MB_HEADDIM = 64
MB_HEADS = MB_INNER // MB_HEADDIM
MB_GROUPS = 8
MB_HPG = MB_HEADS // MB_GROUPS
MB_STATE = 128
MB_GN = MB_GROUPS * MB_STATE
MB_CONV = 3
MB_CONV_CH = MB_INNER + 2 * MB_GN
MB_CHUNK = 64
MB_IN = MB_INNER + MB_CONV_CH + 2 * MB_HEADS

D_FF = 2816

kernel_name = 'hybrid_hgrn2_mamba2_prefix_dit'

def rmsnorm(x, w):
    xf = x.astype(jnp.float32)
    y = xf * lax.rsqrt(jnp.mean(xf * xf, axis=-1, keepdims=True) + EPS)
    return (y * w.astype(jnp.float32)).astype(x.dtype)

def modulate(h, shift, scale):
    return h * (1 + scale) + shift

def flip(t):
    return jnp.flip(t, axis=1)

def dwconv1d(a, w, bias):
    ap = jnp.pad(a, ((0, 0), (1, 1), (0, 0)))
    return ap[:, :-2] * w[0] + ap[:, 1:-1] * w[1] + ap[:, 2:] * w[2] + bias

def dwconv2d_grid(a, w, bias, rows):
    b, L, ch = a.shape
    img = a.reshape(b, rows, GRID_W, ch)
    out = lax.conv_general_dilated(img, w[:, :, None, :].astype(a.dtype), (1, 1), ((1, 1), (1, 1)),
                                   dimension_numbers=('NHWC', 'HWIO', 'NHWC'), feature_group_count=ch)
    return (out + bias).reshape(b, L, ch)

def gla_chunk(q, k, v, logf, s0):
    b, L, h, dk = q.shape
    dv = v.shape[-1]
    n = L // HG_CHUNK
    r = lambda t: t.astype(jnp.float32).reshape(b, n, HG_CHUNK, h, t.shape[-1])
    q, k, v, logf = r(q), r(k), r(v), r(logf)
    bc = jnp.cumsum(logf, axis=2)
    blast = bc[:, :, -1]
    q_dec = q * jnp.exp(bc)
    att = jnp.einsum('bnthd,bnshd->bnhts', q_dec, k * jnp.exp(-bc))
    att = jnp.where(jnp.tril(jnp.ones((HG_CHUNK, HG_CHUNK), bool)), att, 0.0)
    o_intra = jnp.einsum('bnhts,bnshv->bnthv', att, v)
    k_end = k * jnp.exp(blast[:, :, None] - bc)

    def step(S, inp):
        qd, ke, vv, dec = inp
        o_int = jnp.einsum('bthd,bhdv->bthv', qd, S)
        S = dec[..., None] * S + jnp.einsum('bshd,bshv->bhdv', ke, vv)
        return S, o_int

    mv = lambda t: jnp.moveaxis(t, 1, 0)
    s_fin, o_inter = lax.scan(step, s0, (mv(q_dec), mv(k_end), mv(v), mv(jnp.exp(blast))))
    o = o_intra + mv(o_inter)
    return o.reshape(b, L, h, dv), s_fin

def hgrn2_mixer(hx, hc, w_in, w_out, norm_w, lb, need_ctx):
    def prep(h):
        b, L = h.shape[:2]
        q, v, f_fw, f_bw, g = jnp.split(h @ w_in, HG_SPLITS, axis=-1)
        return (q.reshape(b, L, HG_HEADS, HG_KDIM), v.reshape(b, L, HG_HEADS, HG_VDIM), (f_fw, f_bw), g)

    def forget(fz, lbd):
        b, L = fz.shape[:2]
        f = lbd + (1 - lbd) * jax.nn.sigmoid(fz.astype(jnp.float32).reshape(b, L, HG_HEADS, HG_KDIM))
        return jnp.log(f), 1 - f

    def readout(o, g):
        b, L = o.shape[:2]
        o = o * lax.rsqrt(jnp.mean(o * o, axis=-1, keepdims=True) + EPS)
        o = (o * norm_w.astype(jnp.float32).reshape(HG_HEADS, HG_VDIM)).reshape(b, L, D_MODEL)
        return (o * jax.nn.silu(g.astype(jnp.float32))).astype(g.dtype) @ w_out

    qx, vx, fx, gx = prep(hx)
    qc, vc, fc, gc = prep(hc)
    s_zero = jnp.zeros((hc.shape[0], HG_HEADS, HG_KDIM, HG_VDIM), jnp.float32)
    ox = 0.0
    oc = 0.0
    for d in range(2):
        lbd = lb[d].reshape(HG_HEADS, HG_KDIM)
        logf_c, k_c = forget(fc[d], lbd)
        logf_x, k_x = forget(fx[d], lbd)
        seq_c = (qc, k_c, vc, logf_c)
        seq_x = (qx, k_x, vx, logf_x)
        if d == 1:
            seq_c = tuple(flip(t) for t in seq_c)
            seq_x = tuple(flip(t) for t in seq_x)
        o_c, s_c = gla_chunk(*seq_c, s_zero)
        o_x, _ = gla_chunk(*seq_x, s_c)
        if d == 1:
            o_c, o_x = flip(o_c), flip(o_x)
        ox = ox + o_x
        oc = oc + o_c
    yx = readout(ox, gx)
    yc = readout(oc, gc) if need_ctx else None
    return yx, yc

def ssd_chunk(xs, dt, bm, cm, a, h0):
    b, L = xs.shape[:2]
    n = L // MB_CHUNK
    Q = MB_CHUNK
    xs = xs.astype(jnp.float32).reshape(b, n, Q, MB_GROUPS, MB_HPG, MB_HEADDIM)
    dt = dt.reshape(b, n, Q, MB_GROUPS, MB_HPG)
    bm = bm.astype(jnp.float32).reshape(b, n, Q, MB_GROUPS, MB_STATE)
    cm = cm.astype(jnp.float32).reshape(b, n, Q, MB_GROUPS, MB_STATE)
    acs = jnp.cumsum(dt * a, axis=2)
    alast = acs[:, :, -1]
    at = jnp.moveaxis(acs, 2, -1)
    seg = at[..., :, None] - at[..., None, :]
    decay = jnp.exp(jnp.where(jnp.tril(jnp.ones((Q, Q), bool)), seg, -jnp.inf))
    cb = jnp.einsum('bnlgk,bnsgk->bngls', cm, bm)
    w = cb[:, :, :, None] * decay * jnp.moveaxis(dt, 2, -1)[..., None, :]
    y_diag = jnp.einsum('bngjls,bnsgjp->bnlgjp', w, xs)
    wst = jnp.exp(alast[:, :, None] - acs) * dt

    def step(h, inp):
        c_, b_, x_, ws_, ei_, cd_ = inp
        y_off = jnp.einsum('blgk,bgjpk,blgj->blgjp', c_, h, ei_)
        h = cd_[..., None, None] * h + jnp.einsum('bsgk,bsgj,bsgjp->bgjpk', b_, ws_, x_)
        return h, y_off

    mv = lambda t: jnp.moveaxis(t, 1, 0)
    h_fin, y_off = lax.scan(step, h0, (mv(cm), mv(bm), mv(xs), mv(wst), mv(jnp.exp(acs)), mv(jnp.exp(alast))))
    y = y_diag + mv(y_off)
    return y.reshape(b, L, MB_GROUPS, MB_HPG, MB_HEADDIM), h_fin

def mamba2_mixer(hx, hc, w_in, conv_w, conv_b, dt_bias, a_log, d_skip, norm_w, w_out, need_ctx):
    def prep(h):
        b, L = h.shape[:2]
        z, xbc, dt_raw = jnp.split(h @ w_in, [MB_INNER, MB_INNER + MB_CONV_CH], axis=-1)
        xbc = jax.nn.silu(dwconv1d(xbc, conv_w, conv_b))
        xs, bm, cm = jnp.split(xbc, [MB_INNER, MB_INNER + MB_GN], axis=-1)
        return (z, xs.reshape(b, L, MB_GROUPS, MB_HPG, MB_HEADDIM), bm.reshape(b, L, MB_GROUPS, MB_STATE),
                cm.reshape(b, L, MB_GROUPS, MB_STATE), dt_raw.reshape(b, L, 2, MB_GROUPS, MB_HPG))

    def readout(y, xs, z):
        b, L = y.shape[:2]
        y = y + d_skip.astype(jnp.float32).reshape(MB_GROUPS, MB_HPG)[..., None] * xs.astype(jnp.float32)
        y = (y.reshape(b, L, MB_INNER) * jax.nn.silu(z.astype(jnp.float32))).reshape(b, L, MB_GROUPS, -1)
        y = y * lax.rsqrt(jnp.mean(y * y, axis=-1, keepdims=True) + EPS)
        y = y.reshape(b, L, MB_INNER) * norm_w.astype(jnp.float32)
        return y.astype(z.dtype) @ w_out

    zx, xx, bx, cx, dtx = prep(hx)
    zc, xc, bc_, cc, dtc = prep(hc)
    h_zero = jnp.zeros((hc.shape[0], MB_GROUPS, MB_HPG, MB_HEADDIM, MB_STATE), jnp.float32)
    yx = 0.0
    yc = 0.0
    for d in range(2):
        a = -jnp.exp(a_log[d].astype(jnp.float32)).reshape(MB_GROUPS, MB_HPG)
        bias = dt_bias[d].astype(jnp.float32).reshape(MB_GROUPS, MB_HPG)
        dt_c = jax.nn.softplus(dtc[:, :, d].astype(jnp.float32) + bias)
        dt_x = jax.nn.softplus(dtx[:, :, d].astype(jnp.float32) + bias)
        seq_c = (xc, dt_c, bc_, cc)
        seq_x = (xx, dt_x, bx, cx)
        if d == 1:
            seq_c = tuple(flip(t) for t in seq_c)
            seq_x = tuple(flip(t) for t in seq_x)
        y_c, h_c = ssd_chunk(*seq_c, a, h_zero)
        y_x, _ = ssd_chunk(*seq_x, a, h_c)
        if d == 1:
            y_c, y_x = flip(y_c), flip(y_x)
        yx = yx + y_x
        yc = yc + y_c
    out_x = readout(yx, xx, zx)
    out_c = readout(yc, xc, zc) if need_ctx else None
    return out_x, out_c

def conv_ffn(h, w_up, w_down, conv):
    a, v = jnp.split(h @ w_up, 2, axis=-1)
    return (jax.nn.silu(conv(a)) * v) @ w_down

def setup_inputs(seed: int = 0) -> dict:
    key = jax.random.key(seed)
    ks = jax.random.split(key, 24)
    nrm = lambda k, shape, s: jax.random.normal(k, shape, jnp.float32) * s
    D = D_MODEL
    dt0 = jnp.exp(jax.random.uniform(ks[15], (N_MAMBA, 2, MB_HEADS), jnp.float32)
                  * (math.log(0.1) - math.log(0.001)) + math.log(0.001))
    return {
        'x': nrm(ks[0], (BATCH, SEQ, D), 1.0),
        'c': nrm(ks[1], (BATCH, D), 1.0),
        'ctx': nrm(ks[2], (BATCH, CTX_LEN, D), 1.0),
        'c_ctx': nrm(ks[3], (D,), 1.0),
        'ada_w': nrm(ks[4], (DEPTH, D, 6 * D), D ** -0.5),
        'ada_b': nrm(ks[5], (DEPTH, 6 * D), 0.02),
        'pre_norm': 1.0 + nrm(ks[6], (DEPTH, 2, D), 0.05),
        'post_norm': 1.0 + nrm(ks[7], (DEPTH, 2, D), 0.05),
        'hg_w_in': nrm(ks[8], (N_HGRN, D, HG_IN), D ** -0.5),
        'hg_w_out': nrm(ks[9], (N_HGRN, D, D), D ** -0.5),
        'hg_norm': 1.0 + nrm(ks[10], (N_HGRN, D), 0.05),
        'hg_lb_logits': nrm(ks[11], (2, N_HGRN + 1, HG_KEY), 0.5),
        'mb_w_in': nrm(ks[12], (N_MAMBA, D, MB_IN), D ** -0.5),
        'mb_conv_w': nrm(ks[13], (N_MAMBA, MB_CONV, MB_CONV_CH), MB_CONV ** -0.5),
        'mb_conv_b': nrm(ks[14], (N_MAMBA, MB_CONV_CH), 0.02),
        'mb_dt_bias': dt0 + jnp.log(-jnp.expm1(-dt0)),
        'mb_a_log': jnp.log(jax.random.uniform(ks[16], (N_MAMBA, 2, MB_HEADS), jnp.float32, 1.0, 16.0)),
        'mb_d': 1.0 + nrm(ks[17], (N_MAMBA, MB_HEADS), 0.1),
        'mb_norm': 1.0 + nrm(ks[18], (N_MAMBA, MB_INNER), 0.05),
        'mb_w_out': nrm(ks[19], (N_MAMBA, MB_INNER, D), MB_INNER ** -0.5),
        'ffn_w_up': nrm(ks[20], (DEPTH, D, 2 * D_FF), D ** -0.5),
        'ffn_conv_w': nrm(ks[21], (DEPTH, 3, 3, D_FF), 1.0 / 3.0),
        'ffn_conv_b': nrm(ks[22], (DEPTH, D_FF), 0.02),
        'ffn_w_down': nrm(ks[23], (DEPTH, D_FF, D), D_FF ** -0.5),
    }

def reference(x, c, ctx, c_ctx, ada_w, ada_b, pre_norm, post_norm, hg_w_in, hg_w_out, hg_norm, hg_lb_logits,
              mb_w_in, mb_conv_w, mb_conv_b, mb_dt_bias, mb_a_log, mb_d, mb_norm, mb_w_out,
              ffn_w_up, ffn_conv_w, ffn_conv_b, ffn_w_down):
    rows = x.shape[1] // GRID_W
    lb_all = jnp.cumsum(jax.nn.softmax(hg_lb_logits.astype(jnp.float32), axis=1), axis=1)
    sc = jax.nn.silu(c)
    scc = jax.nn.silu(c_ctx)
    for l in range(DEPTH):
        last = l == DEPTH - 1
        mx = jnp.split((sc @ ada_w[l] + ada_b[l])[:, None, :], 6, axis=-1)
        mc = jnp.split(scc @ ada_w[l] + ada_b[l], 6, axis=-1)
        hx = modulate(rmsnorm(x, pre_norm[l, 0]), mx[0], mx[1])
        hc = modulate(rmsnorm(ctx, pre_norm[l, 0]), mc[0], mc[1])
        j = l // N_MIXERS
        if l % N_MIXERS == 0:
            yx, yc = hgrn2_mixer(hx, hc, hg_w_in[j], hg_w_out[j], hg_norm[j], lb_all[:, j], not last)
        else:
            yx, yc = mamba2_mixer(hx, hc, mb_w_in[j], mb_conv_w[j], mb_conv_b[j], mb_dt_bias[j], mb_a_log[j],
                                  mb_d[j], mb_norm[j], mb_w_out[j], not last)
        x = x + mx[2] * rmsnorm(yx, post_norm[l, 0])
        if not last:
            ctx = ctx + mc[2] * rmsnorm(yc, post_norm[l, 0])
        hx = modulate(rmsnorm(x, pre_norm[l, 1]), mx[3], mx[4])
        yx = conv_ffn(hx, ffn_w_up[l], ffn_w_down[l],
                      lambda a: dwconv2d_grid(a, ffn_conv_w[l], ffn_conv_b[l], rows))
        x = x + mx[5] * rmsnorm(yx, post_norm[l, 1])
        if not last:
            hc = modulate(rmsnorm(ctx, pre_norm[l, 1]), mc[3], mc[4])
            yc = conv_ffn(hc, ffn_w_up[l], ffn_w_down[l],
                          lambda a: dwconv1d(a, ffn_conv_w[l][1], ffn_conv_b[l]))
            ctx = ctx + mc[5] * rmsnorm(yc, post_norm[l, 1])
    return x


_drawn_inputs = setup_inputs


def setup_inputs(seed=0):
    import zlib

    import numpy as np

    out = dict(_drawn_inputs(seed))
    spreads = {}
    factors = {'mb_conv_b': 6.017, 'mb_d': 19.395, 'ffn_conv_b': 5.205}
    for name, (base, spread) in spreads.items():
        noise = np.random.default_rng([zlib.crc32(name.encode()), seed]).standard_normal(out[name].shape)
        drawn = base * np.exp(spread * noise) if base else spread * noise
        out[name] = jnp.asarray(drawn.astype(out[name].dtype))
    for name, factor in factors.items():
        out[name] = (out[name] * factor).astype(out[name].dtype)
    return out
```

```python
from contextlib import ExitStack

import concourse.bass as bass
from concourse import mybir

F32 = mybir.dt.float32
F32R = mybir.dt.float32r
U32 = mybir.dt.uint32
ALU = mybir.AluOpType
ACT = mybir.ActivationFunctionType

P = 128
D = 1024
SEQ = 256
T = 2 * SEQ
KT = D // P
EPS = 1e-6
DVE_LO = 1024
HEADS = 8
CH = 32
NCH = T // CH
MB_INNER = 2048
MB_HEADS = 32
MB_GROUPS = 8
HD = 64
FF = 2816
FT = FF // P
FH = (12, 10)
CLAMP = 2.0 ** 62


class Steps:

    def __init__(self, eng, sem):
        self.eng, self.sem, self.n = eng, sem, 0

    def __call__(self, ins):
        self.n += 1
        ins.then_inc(self.sem, 1)
        return self.n

    def wait(self, n=None):
        self.eng.wait_ge(self.sem, self.n if n is None else n)


class PsumPlan:

    def __init__(self, ready, freed):
        self.ready, self.freed = ready, freed
        self.index, self.prev, self.by, self.last = {}, {}, {}, {}
        self.total, self.count = 0, {e: 0 for e in freed}
        self.filled, self.read = 0, {e: 0 for e in freed}

    def add(self, key, bank, by):
        self.prev[key] = self.last.get(bank)
        self.total += 1
        self.index[key] = (self.total, bank)
        self.count[by] += 1
        self.by[key] = (by, self.count[by])
        self.last[bank] = key

    def loop(self, fills, reads):
        before = (self.total, dict(self.count))
        self.total += fills
        for by, n in reads.items():
            self.count[by] += n
        return before

    def passed(self, fills=0, by=None, reads=0):
        self.filled += fills
        if by:
            self.read[by] += reads

    def done(self, ins, key):
        self.filled += 1
        assert self.index[key][0] == self.filled, key
        ins.then_inc(self.ready, 1)

    def empty(self, ins, by, key):
        self.read[by] += 1
        assert self.by[key] == (by, self.read[by]), key
        ins.then_inc(self.freed[by], 1)

    def wait_emptied(self, eng, key):
        by, n = self.by[key]
        eng.wait_ge(self.freed[by], n)

    def bank(self, key):
        return self.index[key][1]

    def wait_free(self, pe, key):
        if self.prev[key] is not None:
            by, n = self.by[self.prev[key]]
            pe.wait_ge(self.freed[by], n)

    def wait_ready(self, eng, key):
        eng.wait_ge(self.ready, self.index[key][0])

    def wait_empty(self, eng):
        for by, n in self.count.items():
            if n:
                eng.wait_ge(self.freed[by], n)


def rows(*groups):
    at, out = 0, {}
    for name, n in groups:
        out[name] = at
        at += n
    return out, at


PROWS, NPROWS = rows(("c", 8), ("c_ctx", 8), ("ada_b", 96), ("pre", 32), ("post", 32), ("hg_norm", 8),
                     ("lb", 32), ("mb_cw", 96), ("mb_cb", 32), ("mb_norm", 16), ("ff_cb", 44), ("ff_cw", 396))
PSLOTS = -(-NPROWS // P)


def program(nc, a, out):
    ctx = ExitStack()
    sems = {}

    def sem(name):
        if name not in sems:
            sems[name] = ctx.enter_context(nc.semaphore(name))
        return sems[name]

    def sb(stack, name, shape, dt=F32):
        return stack.enter_context(nc.sbuf_tensor(name, shape, dt))

    xT = sb(ctx, "xT", [P, KT, T])
    yT = sb(ctx, "yT", [P, KT, T])
    hh = sb(ctx, "hh", [P, KT, T], F32R)
    hl = sb(ctx, "hl", [P, KT, T], F32R)
    wraw = sb(ctx, "wraw", [P, 2, 2048])
    wh = sb(ctx, "wh", [P, 2, 2048], F32R)
    wl = sb(ctx, "wl", [P, 2, 2048], F32R)
    pv = sb(ctx, "pv", [P, NPROWS])
    mod = sb(ctx, "mod", [P, 2, 48, 2])
    nsc = sb(ctx, "nsc", [P, 2, 2, KT, 2])
    gsc = sb(ctx, "gsc", [P, 2, 2, KT, 2])
    ident = sb(ctx, "ident", [P, P])
    ones = sb(ctx, "ones", [P, P])
    eps = sb(ctx, "eps", [P, 1])
    sq = sb(ctx, "sq", [P, 2, T])
    tmp = sb(ctx, "tmp", [P, 2, T])
    rstd = sb(ctx, "rstd", [P, T])
    mbs = sb(ctx, "mbs", [64, 3])
    bank = [ctx.enter_context(nc.psum_tensor(f"bank{i}", [P, 512], F32)) for i in range(8)]
    xrow = yT[:, :, :].rearrange("p a b -> p (a b)").rearrange("p (t c) -> p t c", t=4)

    ff = ExitStack()
    fh = sb(ff, "fh", [P, FH[0], T], F32R)
    fl = sb(ff, "fl", [P, FH[0], T], F32R)
    conv = sb(ff, "conv", [P, 2, T])
    gated = sb(ff, "gated", [P, 2, T])
    prod = sb(ff, "prod", [P, 2, T])
    rows_out = sb(ff, "rows_out", [P, 2, D])
    ff.close()

    hg = ExitStack()
    araw = sb(hg, "araw", [P, 2, 4, 512])
    scc = sb(hg, "scc", [P, KT, 32])
    asum = sb(hg, "asum", [P, 512])
    ared = sb(hg, "ared", [P, 4, 2])
    osm = sb(hg, "osm", [P, 2, 4])
    gA = [sb(hg, f"gA{d}", [P, T]) for d in range(2)]
    gB = [sb(hg, f"gB{d}", [P, T]) for d in range(2)]
    gC = [sb(hg, f"gC{d}", [P, T]) for d in range(2)]
    gD = [[sb(hg, f"gD{d}{i}", [P, T]) for i in range(2)] for d in range(2)]
    sm = sb(hg, "sm", [P, 2, 2, 3, NCH])
    gs = sb(hg, "gs", [P, 3, T])
    vtok = sb(hg, "vtok", [P, 2, 4, P])
    vm = sb(hg, "vm", [P, 2, 4, 4, P])
    st = [sb(hg, f"st{d}", [P, NCH - 1, P]) for d in range(2)]
    ket = [sb(hg, f"ket{d}", [P, 4, P]) for d in range(2)]
    attm = [sb(hg, f"attm{d}", [P, 4, P]) for d in range(2)]
    mask = sb(hg, "mask", [P, 2, P], U32)
    lb = sb(hg, "lb", [P, 2, KT])
    omlb = sb(hg, "omlb", [P, 2, 2, KT])
    lbt = sb(hg, "lbt", [P, 3, 2, KT])
    keep = sb(hg, "keep", [P, NCH + 1, CH])
    hg.close()

    mb = ExitStack()
    dtw = sb(mb, "dtw", [64, 3, T])
    dtf = sb(mb, "dtf", [64, T])
    atf = sb(mb, "atf", [64, T])
    elf = sb(mb, "elf", [64, T])
    acol = sb(mb, "acol", [64, 2])
    dg = sb(mb, "dg", [64, 96])
    bc = sb(mb, "bc", [P, 96])
    dtk = sb(mb, "dtk", [P, 4, 64])
    wtk = sb(mb, "wtk", [P, 4, 64])
    atk = sb(mb, "atk", [P, 2, 64])
    eik = sb(mb, "eik", [P, 2, 64])
    tri = sb(mb, "tri", [P, 2, P])
    xf = sb(mb, "xf", [P, 2, T])
    bf = sb(mb, "bf", [P, 2, T])
    cf = sb(mb, "cf", [P, 2, SEQ])
    xtok = sb(mb, "xtok", [P, 4, 256])
    btok = sb(mb, "btok", [P, 4, P])
    wx = [sb(mb, f"wx{d}", [P, 3, 256]) for d in range(2)]
    dx = [sb(mb, f"dx{d}", [P, 2, 256]) for d in range(2)]
    skip = sb(mb, "skip", [P, 2, 256])
    sz = sb(mb, "sz", [P, 2, 2, 256])
    hs = sb(mb, "hs", [P, 2, 256])
    h1 = sb(mb, "h1", [P, 2, 256])
    cbm = sb(mb, "cbm", [P, 2, 2, P])
    wd = [[sb(mb, f"wd{d}{i}", [P, 2, 2, P]) for i in range(2)] for d in range(2)]
    ysum = sb(mb, "ysum", [P, 2, T])
    yg = sb(mb, "yg", [P, T])
    msq = sb(mb, "msq", [P, 2, 2])
    mb.close()
    qt = tmp[:, 1, :]
    maskf = sq[:, 1, 0:2 * P].rearrange("p (d s) -> p d s", d=2)
    prow = st[0][:, :, :].rearrange("p a b -> p (a b)")[:, 0:PSLOTS * P].rearrange("p (s c) -> p s c", s=PSLOTS)

    psum_ready = sem("psum_ready")
    plan = PsumPlan(psum_ready, {"act": sem("psum_freed_by_act"), "dve": sem("psum_freed_by_dve")})

    ADA_FIRST = 4
    ada_of = [3, 3, 3, 3, 2, 2, 2, 2]
    ada_start = [ADA_FIRST + sum(ada_of[:h]) for h in range(HEADS + 1)]
    for s in range(PSLOTS):
        plan.add(("pv", s), s % 3, "dve")
    for k in range(KT):
        plan.add(("xt", k), (PSLOTS + k) % 3, "act" if k % 2 else "dve")
    for n in range(ADA_FIRST):
        plan.add(("am", n), 3, "act")
        plan.add(("at", n), 3, "dve")
    plan.add(("ss", "pre", 0, 0), 7, "act")
    ring = {"g": 0, "s": 0}

    def gkey(key, by):
        plan.add(key, ring["g"] % 3, by)
        ring["g"] += 1

    def skey(key, by):
        plan.add(key, 4 + ring["s"] % 3, by)
        ring["s"] += 1

    TILES = ([2, 3, 0, 1], [3, 2, 1, 0])
    def ada_key(h, slot):
        if h < HEADS:
            if 1 <= slot <= ada_of[h]:
                plan.add(("at", ada_start[h] + slot - 1), 3, "dve")
            if slot < ada_of[h]:
                plan.add(("am", ada_start[h] + slot), 3, "act")

    for h in range(HEADS + 2):
        p = h - 1
        G, S = h < HEADS, 0 <= p < HEADS
        if G:
            gkey(("v", h), "act")
        if S:
            skey(("att", p, 0), "dve")
            skey(("ke", p, 0), "act")
        if G:
            gkey(("g", h), "dve")
            skey(("vt", h), "act")
        ada_key(h, 0)
        if S:
            skey(("kv", p, 0, 0), "dve")
            skey(("kv", p, 0, 1), "dve")
        if G:
            gkey(("q", h), "act")
        ada_key(h, 1)
        if p >= 1:
            skey(("ot", p - 1), "dve")
        if S:
            skey(("kv", p, 0, 2), "dve")
            skey(("kv", p, 0, 3), "dve")
            skey(("att", p, 1), "dve")
            skey(("ke", p, 1), "act")
        if G:
            gkey(("f", h, 0), "act")
        ada_key(h, 2)
        if S:
            skey(("kv", p, 1, 0), "dve")
            skey(("kv", p, 1, 1), "dve")
        if G:
            gkey(("f", h, 1), "act")
        ada_key(h, 3)
        if S:
            skey(("kv", p, 1, 2), "dve")
            skey(("kv", p, 1, 3), "dve")
    for m in range(KT):
        plan.add(("y", 0, m), m % 3, "act")

    plan.add(("ss", 0, 0), 7, "act")
    plan.add(("ss2", 0, 0), 7, "act")
    ffp = {}

    def plan_ffn(l):
        for half in range(2):
            ffp[l, half, "up"] = plan.loop(2 * FH[half], {"dve": 2 * FH[half]})
            if half == 0:
                ffp[l, half, "down"] = plan.loop(KT, {"act": KT})
            else:
                for m in range(KT):
                    plan.add(("fy", l, m), 4 + m % 2, "dve")
        plan.add(("ss", l, 1), 7, "act")

    plan_ffn(0)
    plan.add(("ss2", 0, 1), 7, "act")
    plan.add(("dt",), 3, "dve")
    ring = {"g": 0, "s": 0}

    def mkey(key, by):
        plan.add(key, 3 + ring["s"] % 4, by)
        ring["s"] += 1

    GROUPS = MB_GROUPS
    for g in range(GROUPS + 2):
        p, q = g - 1, g - 2
        G, S, Q = g < GROUPS, 0 <= p < GROUPS, q >= 0
        if G:
            gkey(("xs", g, 0), "dve")
        if S:
            mkey(("tx", p, 0), "act")
            mkey(("tx", p, 1), "act")
            mkey(("tb", p), "act")
            mkey(("cb", p), "dve")
        if G:
            gkey(("xs", g, 1), "dve")
        if g == 0:
            mkey(("tk", 0), "dve")
            mkey(("tk", 1), "dve")
            mkey(("cd",), "dve")
        if S:
            mkey(("row", p, 0, 0), "dve")
            mkey(("row", p, 0, 1), "dve")
        if G:
            gkey(("b", g), "dve")
        if S:
            mkey(("st", p, 0), "dve")
            mkey(("st", p, 1), "dve")
            mkey(("row", p, 1, 0), "dve")
            mkey(("row", p, 1, 1), "dve")
        if Q:
            mkey(("yt", q), "act")
        if G:
            gkey(("c", g), "dve")
        if S:
            mkey(("off", p, 0), "dve")
            mkey(("off", p, 1), "dve")
        if G:
            gkey(("z", g), "act")
        if S:
            plan.add(("dg", p), 7, "dve")
    for m in range(KT):
        plan.add(("y", 1, m), m % 3, "act")
    plan.add(("ss", 1, 0), 7, "act")
    plan.add(("ss2", 1, 0), 7, "act")
    plan_ffn(1)
    for t in range(2):
        plan.add(("out", t, 0), 2 * t, "act")
        plan.add(("out", t, 1), 2 * t + 1, "dve")

    slabs = []

    def slab(key, n, parts, last):
        slabs.append((key, n, parts, last))

    def cols(w, kts, c0, n):
        return w[kts[0] * P:kts[1] * P, c0:c0 + n].rearrange("(k p) c -> p k c", p=P)

    def pair(key, w, c0, c1, last):
        slab(key, 2048, [(lambda r: r.rearrange("p (k c) -> p k c", c=256)[:, :, 0:128], cols(w, (0, KT), c0, 128)),
                         (lambda r: r.rearrange("p (k c) -> p k c", c=256)[:, :, 128:256], cols(w, (0, KT), c1, 128))], last)

    def wide(key, w, c0, last, k0=0):
        slab(key, 2048, [(lambda r: r.rearrange("p (k c) -> p k c", c=256)[:, 0:4, :], cols(w, (k0, k0 + 4), c0, 256)),
                         (lambda r: r.rearrange("p (k c) -> p k c", c=256)[:, 4:8, :], cols(w, (k0 + 4, k0 + 8), c0, 256))], last)

    w_in = a["hg_w_in"][0]
    for h in range(HEADS):
        c = h * P
        slab(("V", h), 1024, [(lambda r: r[:, 0:1024].rearrange("p (k c) -> p k c", c=128)[:, 0:4, :], cols(w_in, (0, 4), D + c, P)),
                              (lambda r: r[:, 0:1024].rearrange("p (k c) -> p k c", c=128)[:, 4:8, :], cols(w_in, (4, 8), D + c, P))], ("v", h))
        pair(("GQ", h), w_in, 4 * D + c, c, ("q", h))
        pair(("F", h), w_in, 2 * D + c, 3 * D + c, ("f", h, 1))
    for i in range(4):
        wide(("O", i), a["hg_w_out"][0], 256 * i, ("y", 0, 2 * i + 1))
    slab0 = {}

    def plan_ffn_slabs(l):
        for half in range(2):
            slab0[l, half, "up"] = len(slabs)
            slabs.extend([None] * FH[half])
            slab0[l, half, "down"] = len(slabs)
            slabs.extend([(None, FH[half] * P, None, ("fy", l, m) if half else None) for m in range(KT)])

    plan_ffn_slabs(0)
    m_in = a["mb_w_in"][0]
    MB0 = len(slabs)
    XS0, B0 = MB_INNER, 2 * MB_INNER
    C0, DT0 = B0 + MB_GROUPS * P, B0 + 2 * MB_GROUPS * P
    for half in range(2):
        v = lambda r, k0: r[:, 0:256].rearrange("p (k c) -> p k c", c=64)[:, k0:k0 + 2, :]
        slab(("DT", half), 256, [(lambda r, v=v: v(r, 0), cols(m_in, (4 * half, 4 * half + 2), DT0, 64)),
                                 (lambda r, v=v: v(r, 2), cols(m_in, (4 * half + 2, 4 * half + 4), DT0, 64))], ("dt",))
    for g in range(MB_GROUPS):
        wide(("XS", g), m_in, XS0 + 256 * g, ("xs", g, 1))
        pair(("BC", g), m_in, B0 + P * g, C0 + P * g, ("c", g))
        wide(("Z", g), m_in, 256 * g, ("z", g))
    for m in range(KT):
        v = lambda r, k0: r.rearrange("p (k c) -> p k c", c=P)[:, k0:k0 + 8, :]
        slab(("M", m), 2048, [(lambda r, v=v: v(r, 0), cols(a["mb_w_out"][0], (0, 8), P * m, P)),
                              (lambda r, v=v: v(r, 8), cols(a["mb_w_out"][0], (8, 16), P * m, P))], ("y", 1, m))
    OM0 = len(slabs) - KT
    plan_ffn_slabs(1)

    w_landed = [sem("w_landed0"), sem("w_landed1")]
    w_hi, w_lo, w_lo_pool = sem("w_hi"), sem("w_lo"), sem("w_lo_pool")
    w_hi_pool = sem("w_hi_pool")
    a_landed = [sem("a_landed0"), sem("a_landed1")]
    a_used = sem("a_used")
    mbs_landed = sem("mbs_landed")
    x_landed, p_landed, stored = sem("x_landed"), sem("p_landed"), sem("stored")
    consts = sem("consts")
    silu_c, lb_step = sem("silu_c"), sem("lb_step")
    sq_ready, sq_used = sem("sq_ready"), sem("sq_used")
    rstd_ready = sem("rstd_ready")
    x_new = sem("x_new")
    hf_ready, hh_ready, hl_ready = sem("hf_ready"), sem("hh_ready"), sem("hl_ready")
    y_ready = sem("y_ready")
    q_ready = sem("q_ready")
    eg_ready, eg_clamped, sg_ready = sem("eg_ready"), sem("eg_clamped"), sem("sg_ready")
    e_ready, e_clamped, sig_ready, logf_ready = sem("e_ready"), sem("e_clamped"), sem("sig_ready"), sem("logf_ready")
    d_ready, small_ready, en_ready = sem("d_ready"), sem("small_ready"), sem("en_ready")
    qk_ready, qin_ready = sem("qk_ready"), sem("qin_ready")
    v_ready, ket_ready, att_ready = sem("v_ready"), sem("ket_ready"), sem("att_ready")
    state_ready = sem("state_ready")
    intra_done, inter_done = sem("intra_done"), sem("inter_done")
    osq_ready, oms_ready, or_ready = sem("osq_ready"), sem("oms_ready"), sem("or_ready")
    on_ready = sem("on_ready")
    vf_ready = sem("vf_ready")
    conv_start, silu_done = sem("conv_start"), sem("silu_done")
    fh_ready, fl_ready, tap_done = sem("fh_ready"), sem("fl_ready"), sem("tap_done")
    centre_ready, conv_silu = sem("centre_ready"), sem("conv_silu")
    dt_act, dt_dve = sem("dt_act"), sem("dt_dve")
    tri_ready, scaled_ready = sem("tri_ready"), sem("scaled_ready")
    decay_ready, w_ready, hs_ready = sem("decay_ready"), sem("w_ready"), sem("hs_ready")
    off_done, seg_ready = sem("off_done"), sem("seg_ready")
    yg_ready, ygsq_ready, ygms_ready, ygr_ready, yn_ready = sem("yg_ready"), sem("ygsq_ready"), sem("ygms_ready"), sem("ygr_ready"), sem("yn_ready")
    rows_act, rows_dve = sem("rows_act"), sem("rows_dve")
    act_step, dve_step, pool_step = sem("act_step"), sem("dve_step"), sem("pool_step")
    ss_prev = {}

    N_PDMA = [0]
    pgroups = [("c", a["c"].rearrange("b (n q) -> (b n) q", q=P)),
               ("c_ctx", a["c_ctx"].rearrange("(n q) -> n q", q=P)),
               ("ada_b", a["ada_b"].rearrange("l (n q) -> (l n) q", q=P)),
               ("pre", a["pre_norm"].rearrange("l s (n q) -> (l s n) q", q=P)),
               ("post", a["post_norm"].rearrange("l s (n q) -> (l s n) q", q=P)),
               ("hg_norm", a["hg_norm"].rearrange("l (n q) -> (l n) q", q=P)),
               ("lb", a["hg_lb_logits"].rearrange("d i (n q) -> (d i n) q", q=P)),
               ("mb_cw", a["mb_conv_w"].rearrange("l t (n q) -> (l t n) q", q=P)),
               ("mb_cb", a["mb_conv_b"].rearrange("l (n q) -> (l n) q", q=P)),
               ("mb_norm", a["mb_norm"].rearrange("l (n q) -> (l n) q", q=P)),
               ("ff_cb", a["ffn_conv_b"].rearrange("l (n q) -> (l n) q", q=P)),
               ("ff_cw", a["ffn_conv_w"].rearrange("l i j (n q) -> (l i j n) q", q=P))]
    pdma = []
    for name, src in pgroups:
        r, n, done = PROWS[name], src.shape[0], 0
        while done < n:
            k = min(n - done, P - (r + done) % P)
            pdma.append(((r + done) // P, (r + done) % P, k, src[done:done + k, :]))
            done += k

    def prm(name, i, n=1):
        r = PROWS[name] + i
        return pv[:, r:r + n]

    block = ctx.enter_context(nc.Block())

    @block.sync
    def _(sp):
        def load_params():
            for slot, r, k, src in pdma:
                sp.dma_start(prow[r:r + k, slot, :], src).then_inc(p_landed, 16)
            for i, name in enumerate(("mb_dt_bias", "mb_a_log")):
                sp.dma_start(mbs[:, i:i + 1], a[name].rearrange("l d (h o) -> (l d h) o", o=1)).then_inc(mbs_landed, 16)
            for d in range(2):
                sp.dma_start(mbs[32 * d:32 * d + 32, 2:3], a["mb_d"].rearrange("l (h o) -> (l h) o", o=1)).then_inc(mbs_landed, 16)

        def load_tokens():
            sp.dma_start(xrow[:, 0:2, :], a["x"][0].rearrange("(t p) c -> p t c", p=P)).then_inc(x_landed, 16)
            sp.dma_start(xrow[:, 2:4, :], a["ctx"][0].rearrange("(t p) c -> p t c", p=P)).then_inc(x_landed, 16)

        def load_slab(i):
            key, n, parts, last = slabs[i]
            if i >= 2:
                sp.wait_ge(w_lo, i - 1)
            for view, src in parts:
                sp.dma_start(view(wraw[:, i % 2, :]), src).then_inc(w_landed[i % 2], 16)

        def load_ada(n):
            l, c = n // 12, 512 * (n % 12)
            for half in range(2):
                if n >= 1:
                    if half == 0:
                        sp.wait_ge(a_used, n)
                    else:
                        plan.wait_ready(sp, ("am", n - 1))
                sp.dma_start(araw[:, half, :, :],
                             a["ada_w"][l][half * 512:half * 512 + 512, c:c + 512].rearrange("(k p) c -> p k c", p=P))\
                    .then_inc(a_landed[half], 16)

        load_params()
        load_tokens()
        for n in range(ADA_FIRST):
            load_ada(n)
        load_slab(0)
        load_slab(1)
        for h in range(HEADS):
            for n in range(3):
                load_slab(3 * h + n + 2)
                if n < ada_of[h]:
                    load_ada(ada_start[h] + n)
        for i in range(3 * HEADS + 2, 3 * HEADS + 4):
            load_slab(i)

        def raw(i):
            return wraw[:, i % 2, :]

        def load_ffn(l):
            for half in range(2):
                nf, f0 = FH[half], half * FH[0]
                s0 = slab0[l, half, "up"]
                with sp.Fori(0, nf // 2) as i:
                    for u in range(2):
                        sp.wait_ge(w_lo, i * 2 + (s0 + u - 1))
                        for part in range(2):
                            c = i * (2 * P) + ((f0 + u) * P + part * FF)
                            sp.dma_start(raw(s0 + u).rearrange("p (k c) -> p k c", c=256)[:, :, part * P:(part + 1) * P],
                                         a["ffn_w_up"][l][:, bass.ds(c, P)].rearrange("(k p) c -> p k c", p=P))\
                                .then_inc(w_landed[(s0 + u) % 2], 16)
                s0 = slab0[l, half, "down"]
                with sp.Fori(0, KT // 2) as i:
                    for u in range(2):
                        sp.wait_ge(w_lo, i * 2 + (s0 + u - 1))
                        for part in range(2):
                            k0, n = part * nf // 2, nf // 2
                            r = (f0 + k0) * P
                            sp.dma_start(raw(s0 + u)[:, k0 * P:(k0 + n) * P].rearrange("p (k c) -> p k c", c=P),
                                         a["ffn_w_down"][l][r:r + n * P, bass.ds(i * (2 * P) + u * P, P)]
                                         .rearrange("(k p) c -> p k c", p=P)).then_inc(w_landed[(s0 + u) % 2], 16)

        load_ffn(0)
        for i in range(MB0, OM0 + KT):
            load_slab(i)
        load_ffn(1)
        for t in range(2):
            sp.wait_ge(rows_act, t + 1)
            sp.wait_ge(rows_dve, t + 1)
            sp.dma_start(out[0, t * P:(t + 1) * P, :], rows_out[:, t, :]).then_inc(stored, 16)
        sp.wait_ge(stored, 32)

    @block.gpsimd
    def _(pool):
        step = Steps(pool, pool_step)
        pool.memset(ones[:, :], 1.0)
        step(pool.memset(ident[:, :], 0.0))
        pool.memset(eps[:, :], EPS)
        pool.memset(scc[:, :, 2:32], 0.0)
        pool.memset(maskf[:, :, :], 1.0)
        pool.memset(keep[:, :, :], 1.0)
        for d in range(2):
            pool.memset(attm[d][:, :, :], 0.0)
        step(pool.memset(vm[:, :, :, :, :], 0.0))
        step.wait()
        pool.affine_select(out=ident[:, :], in_=ident[:, :], compare_op=ALU.not_equal, fill=1.0, base=0,
                           pattern=[[-1, P]], channel_multiplier=1)
        step(pool.memset(keep[:, :, 0:1], 0.0))
        v = maskf[:, :, :].rearrange("p d (c j) -> p d c j", j=CH)
        step(pool.affine_select(out=v, in_=v, compare_op=ALU.is_ge, fill=0.0, base=0,
                                pattern=[[0, 2], [-CH, 4], [0, CH]], channel_multiplier=1))
        step.wait()
        step(pool.affine_select(out=v, in_=v, compare_op=ALU.is_ge, fill=0.0, base=CH - 1,
                                pattern=[[0, 2], [CH, 4], [0, CH]], channel_multiplier=-1))
        step.wait()
        step(pool.affine_select(out=maskf[:, 0, :], in_=maskf[:, 0, :], compare_op=ALU.is_ge, fill=0.0, base=0,
                                pattern=[[1, P]], channel_multiplier=-1))
        step(pool.affine_select(out=maskf[:, 1, :], in_=maskf[:, 1, :], compare_op=ALU.is_ge, fill=0.0, base=0,
                                pattern=[[-1, P]], channel_multiplier=1))
        step.wait()
        pool.tensor_copy(mask[:, :, :], maskf[:, :, :]).then_inc(consts, 1)

        def split_rest(l):
            def part(s, i, lo, hi):
                pool.wait_ge(w_hi_pool, i * 2 + (l * (2 * KT + FT) + s - slab0[l, 0, "up"] + 1))
                pool.tensor_tensor(wl[:, s % 2, lo:hi], wraw[:, s % 2, lo:hi], wh[:, s % 2, lo:hi].bitcast(F32),
                                   ALU.subtract).then_inc(w_lo_pool, 1)

            for half in range(2):
                for kind, n, lo, hi in (("up", FH[half], DVE_LO, 2048), ("down", KT, DVE_LO, FH[half] * P)):
                    s0 = slab0[l, half, kind]
                    with pool.Fori(0, n // 2) as i:
                        part(s0, i, lo, hi)
                        part(s0 + 1, i, lo, hi)

        split_rest(0)
        pool.wait_ge(x_new, KT + 1)
        step(pool.memset(tri[:, :, :], 1.0))
        step.wait()
        pool.affine_select(out=tri[:, 0, :], in_=tri[:, 0, :], compare_op=ALU.is_ge, fill=0.0, base=0,
                           pattern=[[1, P]], channel_multiplier=-1).then_inc(tri_ready, 1)
        pool.affine_select(out=tri[:, 1, :], in_=tri[:, 1, :], compare_op=ALU.is_ge, fill=0.0, base=0,
                           pattern=[[-1, P]], channel_multiplier=1).then_inc(tri_ready, 1)
        hd = lambda x, n: x.rearrange("p t (j c) -> p t j c", c=HD)
        pool.wait_ge(dt_dve, 5)
        for g in range(MB_GROUPS):
            plan.wait_emptied(pool, ("tx", g, 1))
            if g >= 1:
                plan.wait_ready(pool, ("dg", g - 1))
                pool.wait_ge(off_done, g)
            for d in range(2):
                r = slice(32 * d + 4 * g, 32 * d + 4 * g + 4)
                scale = lambda w, t0, n: w[:, t0:t0 + n, r].unsqueeze(3).to_broadcast([P, n, 4, HD])
                pool.tensor_tensor(hd(wx[d][:, 0:2, :], 2), hd(xtok[:, 2:4, :], 2), scale(wtk, 2, 2), ALU.mult)\
                    .then_inc(scaled_ready, 1)
                pool.tensor_tensor(hd(wx[d][:, 2:3, :], 1), hd(xtok[:, d:d + 1, :], 1), scale(wtk, d, 1), ALU.mult)\
                    .then_inc(scaled_ready, 1)
            for d in range(2):
                r = slice(32 * d + 4 * g, 32 * d + 4 * g + 4)
                pool.tensor_tensor(hd(dx[d][:, :, :], 2), hd(xtok[:, 0:2, :], 2),
                                   dtk[:, 0:2, r].unsqueeze(3).to_broadcast([P, 2, 4, HD]), ALU.mult).then_inc(scaled_ready, 1)
            pool.tensor_tensor(hd(skip[:, :, :], 2), hd(xtok[:, 0:2, :], 2),
                               bc[:, 64 + 4 * g:68 + 4 * g].unsqueeze(1).unsqueeze(3).to_broadcast([P, 2, 4, HD]), ALU.mult)\
                .then_inc(scaled_ready, 1)
        split_rest(1)

    @block.scalar
    def _(act):
        step = Steps(act, act_step)
        sqn = [0]

        def split_hi(i):
            n = slabs[i][1]
            act.wait_ge(w_landed[i % 2], 32 * (i // 2 + 1))
            if i >= 2:
                plan.wait_ready(act, slabs[i - 2][3])
            act.activation(wh[:, i % 2, 0:n], wraw[:, i % 2, 0:n], ACT.Copy).then_inc(w_hi, 1)

        def split_hi_next(s, i, ready, n=2048):
            act.wait_ge(w_landed[s % 2], i * 32 + 32 * (s // 2 + 1))
            act.wait_ge(psum_ready, ready)
            act.activation(wh[:, s % 2, DVE_LO:n], wraw[:, s % 2, DVE_LO:n], ACT.Copy).then_inc(w_hi_pool, 1)
            act.activation(wh[:, s % 2, 0:DVE_LO], wraw[:, s % 2, 0:DVE_LO], ACT.Copy).then_inc(w_hi, 1)

        def square(m, src, n):
            if m >= 2:
                act.wait_ge(sq_used, sqn[0] // KT * (KT - 1) + m - 1)
            act.activation(sq[:, m % 2, 0:n], src, ACT.Square).then_inc(sq_ready, 1)
            sqn[0] += 1

        def squares(n=T):
            for m in range(KT):
                xs[0] += 1
                act.wait_ge(x_new, xs[0])
                square(m, xT[:, m, 0:n], n)

        xs, hf = [0], [0]

        def rsqrt(key, n, dim, dst=None, signal=None):
            dst = rstd if dst is None else dst
            plan.wait_ready(act, key)
            ins = act.activation(dst[:, 0:n], bank[plan.bank(key)][:, 0:n], ACT.Ln, scale=1.0 / dim, bias=eps[:, 0:1])
            plan.empty(ins, "act", key)
            plan.wait_emptied(act, key)
            act.activation(dst[:, 0:n], dst[:, 0:n], ACT.Exp, scale=-0.5).then_inc(signal or rstd_ready, 1)

        def h_high(n=T):
            for m in range(KT):
                hf[0] += 1
                act.wait_ge(hf_ready, hf[0])
                act.activation(hh[:, m, 0:n], tmp[:, m % 2, 0:n], ACT.Copy).then_inc(hh_ready, 1)

        def ada_rows(n):
            key = ("am", n)
            plan.wait_ready(act, key)
            plan.empty(act.activation(asum[:, :], bank[plan.bank(key)][:, :], ACT.Copy), "act", key)

        def ada_slot(h, slot):
            if slot < ada_of[h]:
                ada_rows(ada_start[h] + slot)

        def exp_ln_tables():
            act.preload_act_table_set("natural_log_exp_and_others")

        def silu_table():
            act.preload_act_table_set("silu_and_others")

        exp_ln_tables()
        plan.wait_emptied(act, ("pv", 0))
        cc = pv[:, 0:16].rearrange("p (b k) -> p k b", b=2)
        act.activation(scc[:, :, 0:2], cc, ACT.Exp, scale=-1.0).then_inc(silu_c, 1)
        act.wait_ge(silu_c, 2)
        step(act.activation(scc[:, :, 0:2], scc[:, :, 0:2], ACT.Ln, bias=1.0))
        step.wait()
        act.activation(scc[:, :, 0:2], scc[:, :, 0:2], ACT.Exp, scale=-1.0).then_inc(silu_c, 1)
        act.wait_ge(lb_step, 1)
        act.activation(lbt[:, 0:2, :, :], lbt[:, 0:2, :, :], ACT.Exp).then_inc(lb_step, 1)
        for k in range(1, KT, 2):
            plan.wait_ready(act, ("xt", k))
            plan.empty(act.activation(xT[:, k, :], bank[plan.bank(("xt", k))][:, :], ACT.Copy), "act", ("xt", k))
        for n in range(ADA_FIRST):
            ada_rows(n)
        for k in range(KT):
            plan.wait_emptied(act, ("xt", k))
            square(k, xT[:, k, :], T)
        act.wait_ge(consts, 1)
        rsqrt(("ss", "pre", 0, 0), T, D)
        split_hi(0)
        h_high()

        def gate_exps(h, d):
            n = 2 * h + d
            A, B, C = gA[d], gB[d], gC[d]
            plan.wait_ready(act, ("f", h, d))
            if h >= 1:
                plan.wait_ready(act, ("ke", h - 1, d))
                act.wait_ge(qin_ready, n - 1)
            ins = act.activation(A[:, :], bank[plan.bank(("f", h, d))][:, :], ACT.Exp, scale=-1.0)
            plan.empty(ins, "act", ("f", h, d))
            act.wait_ge(e_clamped, n + 1)
            step(act.activation(A[:, :], A[:, :], ACT.Ln, bias=1.0))
            step.wait()
            act.activation(A[:, :], A[:, :], ACT.Exp, scale=-1.0).then_inc(sig_ready, 1)
            act.wait_ge(sig_ready, n + 1)
            act.activation(B[:, :], A[:, :], ACT.Ln, scale=omlb[:, 0, d, h:h + 1], bias=lb[:, d, h:h + 1])\
                .then_inc(logf_ready, 1)
            act.wait_ge(d_ready, n + 1)
            act.activation(C[:, :], B[:, :], ACT.Exp)
            act.activation(A[:, :], B[:, :], ACT.Exp, scale=-1.0)
            s = sm[:, h % 2, d, :, :]
            act.activation(s, s, ACT.Exp).then_inc(en_ready, 1)

        def value_columns(h):
            key = ("v", h)
            plan.wait_ready(act, key)
            if h >= 1:
                plan.wait_ready(act, ("vt", h - 1))
            plan.empty(act.activation(sq[:, 1, :], bank[plan.bank(key)][:, :], ACT.Copy), "act", key)

        def value_rows(h):
            key = ("vt", h)
            plan.wait_ready(act, key)
            src = bank[plan.bank(key)][:, :].rearrange("p (t v) -> p t v", t=4)
            if h >= 2:
                act.wait_ge(intra_done, 2 * (h - 2) + 2)
                plan.wait_ready(act, ("kv", h - 2, 1, 3))
            act.activation(vtok[:, h % 2, :, :], src, ACT.Copy)
            for c in range(4):
                r = slice(c * CH, (c + 1) * CH)
                ins = act.activation(vm[r, h % 2, :, c, :], src[r, :, :], ACT.Copy)
            plan.empty(ins, "act", key)

        def ke_rows(h, d):
            plan.wait_ready(act, ("ke", h, d))
            if h >= 1:
                plan.wait_ready(act, ("kv", h - 1, d, 3))
            src = bank[plan.bank(("ke", h, d))][:, :].rearrange("p (t k) -> p t k", t=4)
            plan.empty(act.activation(ket[d][:, :, :], src, ACT.Copy), "act", ("ke", h, d))

        for h in range(HEADS + 2):
            p = h - 1
            G, S = h < HEADS, 0 <= p < HEADS
            if G:
                split_hi(3 * h + 1)
                value_columns(h)
            if p >= 1:
                act.wait_ge(inter_done, 2 * (p - 1) + 2)
                if p >= 2:
                    act.wait_ge(oms_ready, p - 1)
                act.activation(sq[:, 0, :], bank[7][:, :], ACT.Square).then_inc(osq_ready, 1)
            if S:
                ke_rows(p, 0)
            if p >= 1:
                act.wait_ge(oms_ready, p)
                if p >= 2:
                    act.wait_ge(on_ready, p - 1)
                step(act.activation(osm[:, 1, :], osm[:, 0, :], ACT.Ln, scale=1.0 / P, bias=eps[:, 0:1]))
                step.wait()
                act.activation(osm[:, 1, :], osm[:, 1, :], ACT.Exp, scale=-0.5).then_inc(or_ready, 1)
            if G:
                plan.wait_ready(act, ("g", h))
                if h >= 3:
                    plan.wait_emptied(act, ("ot", h - 3))
                g = gs[:, h % 3, :]
                act.activation(g, bank[plan.bank(("g", h))][:, :], ACT.Exp, scale=-1.0).then_inc(eg_ready, 1)
                act.wait_ge(eg_clamped, h + 1)
                step(act.activation(g, g, ACT.Ln, bias=1.0))
                step.wait()
                act.activation(g, g, ACT.Exp, scale=-1.0).then_inc(sg_ready, 1)
                value_rows(h)
                split_hi(3 * h + 2)
                ada_slot(h, 0)
                plan.wait_ready(act, ("q", h))
                if h >= 1:
                    act.wait_ge(qin_ready, 2 * h)
                plan.empty(act.activation(qt, bank[plan.bank(("q", h))][:, :], ACT.Copy), "act", ("q", h))
                ada_slot(h, 1)
            if S:
                ke_rows(p, 1)
            if G:
                gate_exps(h, 0)
                split_hi(3 * h + 3)
                ada_slot(h, 2)
                gate_exps(h, 1)
        for k in range(KT):
            plan.wait_emptied(act, ("ot", k))
            act.activation(hh[:, k, :], yT[:, k, :], ACT.Copy).then_inc(hh_ready, 1)
        for m in range(KT):
            if m % 2 == 0 and m // 2 < 3:
                split_hi(3 * HEADS + m // 2 + 1)
            key = ("y", 0, m)
            plan.wait_ready(act, key)
            if m == KT - 2:
                split_hi_next(slab0[0, 0, "up"], 0, plan.index[("y", 0, 5)][0])
            plan.empty(act.activation(yT[:, m, :], bank[plan.bank(key)][:, :], ACT.Copy), "act", key)
            plan.wait_emptied(act, key)
            square(m, yT[:, m, :], T)

        def ffn_act(l, n, last_split):
            silu_table()
            for half in range(2):
                nf = FH[half]
                s0 = slab0[l, half, "up"]
                r0, reads = ffp[l, half, "up"]
                v0 = reads["dve"]
                t0 = l * FT + half * FH[0]
                cw, cb = PROWS["ff_cw"] + (9 * l + 4) * FT + half * FH[0], PROWS["ff_cb"] + l * FT + half * FH[0]

                def tile(i, c, first=False, last=False):
                    u, v = c % 2, 1 - c % 2
                    split_hi_next(s0 + c + 1, i, i * 4 + (r0 + 2 * c), nf * P if last else 2048)
                    if not first:
                        gate(i, c - 1)
                    act.wait_ge(psum_ready, i * 4 + (r0 + 2 * c + 1))
                    act.wait_ge(psum_freed_dve, i * 4 + (v0 + 2 * c - 2))
                    act.activation(conv[:, u, 0:n], bank[2 * u][:, 0:n], ACT.Identity,
                                   scale=pv[:, bass.ds(i * 2 + (cw + c), 1)],
                                   bias=pv[:, bass.ds(i * 2 + (cb + c), 1)]).then_inc(conv_start, 1)
                    if not first:
                        high(i, c - 1)

                def gate(i, c):
                    act.wait_ge(psum_freed_dve, i * 4 + (v0 + 2 * c + 1))
                    act.activation(gated[:, c % 2, 0:n], conv[:, c % 2, 0:n], ACT.Silu).then_inc(silu_done, 1)

                def high(i, c):
                    act.wait_ge(psum_freed_dve, i * 4 + (v0 + 2 * c + 2))
                    act.activation(fh[:, bass.ds(i * 2 + c, 1), 0:n], prod[:, c % 2, 0:n].unsqueeze(1), ACT.Copy).then_inc(fh_ready, 1)

                tile(0, 0, first=True)
                with act.Fori(0, nf // 2 - 1) as i:
                    tile(i, 1)
                    tile(i, 2)
                tile(0, nf - 1, last=True)
                gate(0, nf - 1)
                high(0, nf - 1)
                plan.passed()
                s0 = slab0[l, half, "down"]
                if half == 0:
                    r0, reads = ffp[l, half, "down"]

                    def down_tile(i, c, last=False):
                        split_hi_next(s0 + c + 1, i, i * 2 + (r0 + c), 2048 if last else nf * P)
                        act.wait_ge(psum_ready, i * 2 + (r0 + c + 1))
                        act.activation(yT[:, bass.ds(i * 2 + c, 1), 0:n], bank[4 + c % 2][:, 0:n].unsqueeze(1), ACT.Copy)\
                            .then_inc(plan.freed["act"], 1)

                    with act.Fori(0, KT // 2 - 1) as i:
                        down_tile(i, 0)
                        down_tile(i, 1)
                    down_tile(0, KT - 2)
                    down_tile(0, KT - 1, last=True)
                    plan.passed(by="act", reads=KT)
                else:
                    for m in range(KT):
                        if m < KT - 1:
                            split_hi_next(s0 + m + 1, 0, plan.index[("fy", l, m - 1)][0] if m else r0 + 2 * nf, nf * P)
                        elif last_split is not None:
                            plan.wait_ready(act, ("fy", l, m - 1))
                            last_split()
                        plan.wait_emptied(act, ("fy", l, m))
                        square(m, yT[:, m, 0:n], n)

        psum_freed_dve = plan.freed["dve"]
        rsqrt(("ss", 0, 0), T, D)
        squares()
        rsqrt(("ss2", 0, 0), T, D)
        h_high()
        ffn_act(0, T, lambda: split_hi(MB0))
        exp_ln_tables()
        rsqrt(("ss", 0, 1), T, D)
        split_hi(MB0 + 1)
        squares()
        rsqrt(("ss2", 0, 1), T, D)
        h_high()

        def centre(g, i, key, dst, n, tile):
            plan.wait_ready(act, key)
            act.activation(dst, bank[plan.bank(key)][:, 0:n], ACT.Identity, scale=prm("mb_cw", 32 + tile),
                           bias=prm("mb_cb", tile)).then_inc(centre_ready, 1)

        def decays(p, d, i):
            act.wait_ge(seg_ready, 4 * p + 2 * d + i + 1)
            act.activation(wd[d][i][:, :, :, :], wd[d][i][:, :, :, :], ACT.Exp).then_inc(decay_ready, 1)

        def dt_rates():
            act.wait_ge(mbs_landed, 64)
            act.wait_ge(dt_dve, 1)
            act.activation(dtw[:, 1, :], dtw[:, 1, :], ACT.Exp).then_inc(dt_act, 1)
            act.activation(acol[:, 0:1], mbs[:, 1:2], ACT.Exp).then_inc(dt_act, 1)
            act.wait_ge(dt_dve, 2)
            act.activation(dtw[:, 2, :], dtw[:, 2, :], ACT.Ln).then_inc(dt_act, 1)
            act.wait_ge(dt_dve, 3)
            for d in range(2):
                r = slice(32 * d, 32 * d + 32)
                act.activation(acol[r, 1:2], atf[r, P - 1 + d:P + d], ACT.Exp).then_inc(dt_act, 1)

        def dt_exps():
            plan.wait_emptied(act, ("tk", 1))
            act.activation(wtk[:, :, :], wtk[:, :, :], ACT.Exp).then_inc(dt_act, 1)
            act.activation(eik[:, :, :], atk[:, :, :], ACT.Exp).then_inc(dt_act, 1)

        dt_rates()
        for g in range(MB_GROUPS + 2):
            p, q = g - 1, g - 2
            G, S, Q = g < MB_GROUPS, 0 <= p < MB_GROUPS, q >= 0
            sl = MB0 + 2 + 3 * g
            exp_ln_tables()
            if g == 0:
                split_hi(sl)
            if G:
                split_hi(sl + 1)
            if S:
                for f in range(2):
                    key = ("tx", p, f)
                    plan.wait_ready(act, key)
                    if p >= 1:
                        act.wait_ge(scaled_ready, 7 * p)
                    plan.empty(act.activation(xtok[:, :, f * P:(f + 1) * P],
                                              bank[plan.bank(key)][:, :].rearrange("p (t c) -> p t c", c=P), ACT.Copy), "act", key)
                key = ("tb", p)
                plan.wait_ready(act, key)
                if p >= 1:
                    plan.wait_ready(act, ("st", p - 1, 1))
                plan.empty(act.activation(btok[:, :, :], bank[plan.bank(key)][:, :].rearrange("p (t c) -> p t c", c=P), ACT.Copy),
                           "act", key)
            if G:
                if S:
                    plan.wait_ready(act, ("tx", p, 0))
                centre(g, 0, ("xs", g, 0), xf[:, 0, :], T, 2 * g)
            if Q:
                act.wait_ge(yg_ready, q + 1)
                act.activation(sq[:, 0, :], yg[:, :], ACT.Square).then_inc(ygsq_ready, 1)
            if G:
                centre(g, 1, ("xs", g, 1), xf[:, 1, :], T, 2 * g + 1)
            if g == 0:
                dt_exps()
            if S:
                decays(p, 0, 0)
                decays(p, 0, 1)
            if Q:
                act.wait_ge(ygms_ready, q + 1)
                step(act.activation(msq[:, 1, :], msq[:, 0, :], ACT.Ln, scale=1.0 / 256, bias=eps[:, 0:1]))
                step.wait()
                act.activation(msq[:, 1, :], msq[:, 1, :], ACT.Exp, scale=-0.5).then_inc(ygr_ready, 1)
            if G:
                split_hi(sl + 2)
                centre(g, 2, ("b", g), bf[:, g % 2, :], T, 16 + g)
            if S:
                for d in range(2):
                    key = ("st", p, d)
                    plan.wait_ready(act, key)
                    if p >= 1:
                        plan.wait_ready(act, ("off", p - 1, 1))
                    act.activation(hs[:, d, :], bank[plan.bank(key)][:, 0:256], ACT.Copy).then_inc(hs_ready, 1)
                decays(p, 1, 0)
                decays(p, 1, 1)
            if Q:
                key = ("yt", q)
                plan.wait_ready(act, key)
                yk = yT[:, :, :].rearrange("p a b -> p (a b)")
                for f in range(2):
                    k = 2 * q + f
                    ins = act.activation(yk[:, k * 256:(k + 1) * 256], bank[plan.bank(key)][:, f * 256:(f + 1) * 256],
                                         ACT.Copy, scale=prm("mb_norm", k))
                plan.empty(ins, "act", key)
            if G:
                centre(g, 3, ("c", g), cf[:, g % 2, :], SEQ, 24 + g)
                silu_table()
                split_hi(sl + 3)
                for key, dst in ((("xs", g, 0), xf[:, 0, :]), (("xs", g, 1), xf[:, 1, :]), (("b", g), bf[:, g % 2, :]),
                                 (("c", g), cf[:, g % 2, :])):
                    plan.wait_emptied(act, key)
                    act.activation(dst, dst, ACT.Silu).then_inc(conv_silu, 1)
                key = ("z", g)
                plan.wait_ready(act, key)
                plan.empty(act.activation(sz[:, g % 2, :, :], bank[plan.bank(key)][:, :].rearrange("p (t c) -> p t c", c=256),
                                          ACT.Silu), "act", key)
        for k in range(KT):
            plan.wait_emptied(act, ("yt", k))
            act.activation(hh[:, k, :], yT[:, k, :], ACT.Copy).then_inc(hh_ready, 1)
        for m in range(KT):
            if m < KT - 1:
                split_hi(OM0 + m + 1)
            else:
                split_hi_next(slab0[1, 0, "up"], 0, plan.index[("y", 1, KT - 2)][0])
            key = ("y", 1, m)
            plan.wait_ready(act, key)
            plan.empty(act.activation(yT[:, m, 0:SEQ], bank[plan.bank(key)][:, 0:SEQ], ACT.Copy), "act", key)
            plan.wait_emptied(act, key)
            square(m, yT[:, m, 0:SEQ], SEQ)
        rsqrt(("ss", 1, 0), SEQ, D)
        squares(SEQ)
        rsqrt(("ss2", 1, 0), SEQ, D)
        h_high(SEQ)
        ffn_act(1, SEQ, None)
        exp_ln_tables()
        rsqrt(("ss", 1, 1), SEQ, D)
        for t in range(2):
            key = ("out", t, 0)
            plan.wait_ready(act, key)
            act.activation(rows_out[:, t, 0:512], bank[plan.bank(key)][:, :], ACT.Copy).then_inc(rows_act, 1)

    @block.vector
    def _(dve):
        step = Steps(dve, dve_step)
        V = dve

        def split_lo(i):
            n = slabs[i][1]
            dve.wait_ge(w_hi, i + 1)
            dve.tensor_tensor(wl[:, i % 2, 0:n], wraw[:, i % 2, 0:n], wh[:, i % 2, 0:n].bitcast(F32),
                              ALU.subtract).then_inc(w_lo, 1)

        def split_lo_part(l, s, i, lo, hi, last=True):
            if lo == 0:
                dve.wait_ge(w_hi, i * 2 + (s + 1))
            if last:
                if lo == 0:
                    lo = hi - 512
                    dve.tensor_tensor(wl[:, s % 2, 0:lo], wraw[:, s % 2, 0:lo], wh[:, s % 2, 0:lo].bitcast(F32), ALU.subtract)
                dve.wait_ge(w_lo_pool, i * 2 + (l * (2 * KT + FT) + s - slab0[l, 0, "up"] + 1))
            ins = dve.tensor_tensor(wl[:, s % 2, lo:hi], wraw[:, s % 2, lo:hi], wh[:, s % 2, lo:hi].bitcast(F32), ALU.subtract)
            if last:
                ins.then_inc(w_lo, 1)

        def ada_add(n):
            key = ("at", n)
            plan.wait_ready(dve, key)
            src = bank[plan.bank(key)][:, :].rearrange("p (c j b) -> p c j b", c=4, j=4)[:, :, :, 0:2]
            step.wait()
            plan.empty(V.tensor_reduce(ared[:, :, :], src.rearrange("p c j b -> p c b j"), mybir.AxisListType.X, ALU.add),
                       "dve", key)
            plan.wait_emptied(dve, key)
            dst = mod[:, :, :, :].rearrange("p l j b -> p (l j) b")[:, 4 * n:4 * n + 4, :]
            step(V.tensor_tensor(dst, ared[:, :, :], prm("ada_b", 4 * n, 4).unsqueeze(2).to_broadcast([P, 4, 2]), ALU.add))

        def ada_slot(h, slot):
            if 1 <= slot <= ada_of[h]:
                ada_add(ada_start[h] + slot - 1)

        def norm_scales(l, s):
            w = prm("pre", (2 * l + s) * KT, KT).unsqueeze(2).to_broadcast([P, KT, 2])
            sc = mod[:, l, (3 * s + 1) * KT:(3 * s + 2) * KT, :]
            step(V.tensor_scalar(nsc[:, l, s, :, :], sc, 1.0, None, ALU.add))
            step.wait()
            step(V.tensor_tensor(nsc[:, l, s, :, :], nsc[:, l, s, :, :], w, ALU.mult))

        def gate_scales(l, s):
            w = prm("post", (2 * l + s) * KT, KT).unsqueeze(2).to_broadcast([P, KT, 2])
            step(V.tensor_tensor(gsc[:, l, s, :, :], mod[:, l, (3 * s + 2) * KT:(3 * s + 3) * KT, :], w, ALU.mult))

        def residual(l, s, n=T):
            rn[0] += 1
            dve.wait_ge(rstd_ready, rn[0])
            x0 = xn[0]
            step.wait()
            turned = {}
            for m in range(KT + 1):
                if m < KT:
                    if m >= 2:
                        dve.wait_ge(x_new, x0 + m - 1)
                    turned[m] = step(V.tensor_tensor(tmp[:, m % 2, 0:n], yT[:, m, 0:n], rstd[:, 0:n], ALU.mult))
                if m >= 1:
                    k = m - 1
                    step.wait(turned[k])
                    for b in range(n // SEQ):
                        r = slice(b * SEQ, (b + 1) * SEQ)
                        ins = V.scalar_tensor_tensor(out=xT[:, k, r], in0=tmp[:, k % 2, r], scalar=gsc[:, l, s, k, b:b + 1],
                                                     in1=xT[:, k, r], op0=ALU.mult, op1=ALU.add)
                    ins.then_inc(x_new, 1)
            xn[0] += KT

        xn, rn = [0], [0]

        def modulated(l, s, n=T):
            rn[0] += 1
            dve.wait_ge(rstd_ready, rn[0])
            step.wait()
            base = hfn[0]
            for m in range(KT + 1):
                if m < KT:
                    if m >= 2:
                        dve.wait_ge(hl_ready, base + m - 1)
                    t = tmp[:, m % 2, :]
                    step(V.tensor_tensor(t[:, 0:n], xT[:, m, 0:n], rstd[:, 0:n], ALU.mult))
                    step.wait()
                    for b in range(n // SEQ):
                        r = slice(b * SEQ, (b + 1) * SEQ)
                        ins = V.tensor_scalar(t[:, r], t[:, r], nsc[:, l, s, m, b:b + 1],
                                              mod[:, l, 3 * s * KT + m, b:b + 1], ALU.mult, ALU.add)
                    ins.then_inc(hf_ready, 1)
                if m >= 1:
                    k = m - 1
                    dve.wait_ge(hh_ready, base + k + 1)
                    V.tensor_tensor(hl[:, k, 0:n], tmp[:, k % 2, 0:n], hh[:, k, 0:n].bitcast(F32),
                                    ALU.subtract).then_inc(hl_ready, 1)
            hfn[0] += KT

        hfn = [0]
        for s in range(PSLOTS):
            plan.wait_ready(dve, ("pv", s))
            n = min(P, NPROWS - s * P)
            plan.empty(V.tensor_copy(pv[:, s * P:s * P + n], bank[plan.bank(("pv", s))][:, 0:n]), "dve", ("pv", s))
            if s == 0:
                dve.wait_ge(silu_c, 1)
                V.tensor_scalar(scc[:, :, 0:2], scc[:, :, 0:2], CLAMP, None, ALU.min).then_inc(silu_c, 1)
                dve.wait_ge(silu_c, 3)
                cc = pv[:, 0:16].rearrange("p (b k) -> p k b", b=2)
                V.tensor_tensor(scc[:, :, 0:2], scc[:, :, 0:2], cc, ALU.mult).then_inc(silu_c, 1)
        plan.wait_emptied(dve, ("pv", PSLOTS - 1))
        lg = prm("lb", 0, 32).rearrange("p (d i k) -> p d i k", d=2, i=2)
        step(V.tensor_tensor(lbt[:, 2, :, :], lg[:, :, 0, :], lg[:, :, 1, :], ALU.max))
        step.wait()
        step(V.tensor_tensor(lbt[:, 0, :, :], lg[:, :, 0, :], lbt[:, 2, :, :], ALU.subtract))
        V.tensor_tensor(lbt[:, 1, :, :], lg[:, :, 1, :], lbt[:, 2, :, :], ALU.subtract).then_inc(lb_step, 1)
        for k in range(0, KT, 2):
            plan.wait_ready(dve, ("xt", k))
            plan.empty(V.tensor_copy(xT[:, k, :], bank[plan.bank(("xt", k))][:, :]), "dve", ("xt", k))
        dve.wait_ge(lb_step, 2)
        step(V.tensor_tensor(lbt[:, 1, :, :], lbt[:, 0, :, :], lbt[:, 1, :, :], ALU.add))
        step.wait()
        step(V.reciprocal(lbt[:, 1, :, :], lbt[:, 1, :, :]))
        step.wait()
        step(V.tensor_tensor(lb[:, :, :], lbt[:, 0, :, :], lbt[:, 1, :, :], ALU.mult))
        step.wait()
        step(V.tensor_scalar(omlb[:, 0, :, :], lb[:, :, :], -1.0, 1.0, ALU.mult, ALU.add))
        step(V.tensor_scalar(omlb[:, 1, :, :], lb[:, :, :], -1.0, None, ALU.add))
        for n in range(ADA_FIRST):
            ada_add(n)
        step.wait()
        norm_scales(0, 0)
        split_lo(0)
        plan.wait_emptied(dve, ("xt", KT - 1))
        modulated(0, 0)

        def states(h, d, ti):
            key = ("kv", h, d, ti)
            plan.wait_ready(dve, key)
            kv = bank[plan.bank(key)]
            if ti == 0 and h >= 1:
                dve.wait_ge(inter_done, 2 * (h - 1) + d + 1)
            for jj in range(4):
                j = 4 * ti + jj
                c = jj if d == 0 else 3 - jj
                if j == NCH - 1:
                    break
                src = kv[:, c * P:(c + 1) * P]
                if j == 0:
                    ins = V.tensor_copy(st[d][:, 0, :], src)
                else:
                    dec = sm[:, h % 2, d, 2, 4 * TILES[d][ti] + c:4 * TILES[d][ti] + c + 1]
                    step.wait() if jj else plan.wait_emptied(dve, ("kv", h, d, ti - 1))
                    ins = V.scalar_tensor_tensor(out=st[d][:, j, :], in0=st[d][:, j - 1, :], scalar=dec, in1=src,
                                                 op0=ALU.mult, op1=ALU.add)
                if jj < 3 and j < NCH - 2:
                    step(ins)
                else:
                    plan.empty(ins, "dve", key)


        def mask_att(h, d):
            key = ("att", h, d)
            plan.wait_ready(dve, key)
            if h >= 1:
                dve.wait_ge(intra_done, 2 * (h - 1) + d + 1)
            ins = V.copy_predicated(attm[d][:, :, :], mask[:, d, :].unsqueeze(1).to_broadcast([P, 4, P]),
                              bank[plan.bank(key)][:, :].rearrange("p (t s) -> p t s", t=4))
            plan.empty(ins, "dve", key)

        def gate_products(h, d):
            n = 2 * h + d
            A, B, C, Dd = gA[d], gB[d], gC[d], gD[d][h % 2]
            ch = lambda x: x[:, :].rearrange("p (c j) -> p c j", j=CH)
            plan.wait_emptied(dve, ("f", h, d))
            V.tensor_scalar(A[:, :], A[:, :], CLAMP, None, ALU.min).then_inc(e_clamped, 1)
            dve.wait_ge(sig_ready, n + 1)
            if h >= 2:
                dve.wait_ge(inter_done, 2 * (h - 2) + d + 1)
            flat_keep = keep[:, :, :].rearrange("p c j -> p (c j)")
            kk = step(V.tensor_scalar(Dd[:, :], A[:, :], omlb[:, 1, d, h:h + 1], omlb[:, 0, d, h:h + 1], ALU.mult, ALU.add))
            dve.wait_ge(logf_ready, n + 1)
            if d == 0:
                step(V.tensor_tensor_scan(C[:, :], flat_keep[:, 0:T], B[:, :], 0.0, ALU.mult, ALU.add))
            else:
                step(V.tensor_tensor_scan(C[:, ::-1], flat_keep[:, T:0:-1], B[:, ::-1],
                                          0.0, ALU.mult, ALU.add))
            mid, last = (CH // 2 - 1, CH - 1) if d == 0 else (CH // 2, 0)
            s = sm[:, h % 2, d, :, :]
            step.wait()
            V.tensor_copy(s[:, 0, :].unsqueeze(2), ch(C)[:, :, mid:mid + 1])
            V.tensor_copy(s[:, 2, :].unsqueeze(2), ch(C)[:, :, last:last + 1])
            V.tensor_tensor(s[:, 1, :].unsqueeze(2), ch(C)[:, :, last:last + 1], ch(C)[:, :, mid:mid + 1], ALU.subtract)
            V.tensor_tensor(ch(B), ch(C), ch(C)[:, :, mid:mid + 1].to_broadcast([P, NCH, CH]), ALU.subtract).then_inc(d_ready, 1)
            dve.wait_ge(en_ready, n + 1)
            plan.wait_emptied(dve, ("q", h))
            V.tensor_tensor(C[:, :], qt, C[:, :], ALU.mult)
            step(V.tensor_tensor(A[:, :], Dd[:, :], A[:, :], ALU.mult))
            step.wait()
            V.tensor_tensor(ch(B), ch(A), s[:, 1, :].unsqueeze(2).to_broadcast([P, NCH, CH]), ALU.mult).then_inc(qk_ready, 1)
            V.tensor_tensor(ch(Dd), ch(C), s[:, 0, :].unsqueeze(2).to_broadcast([P, NCH, CH]), ALU.mult).then_inc(qin_ready, 1)

        for h in range(HEADS + 2):
            p = h - 1
            G, S = h < HEADS, 0 <= p < HEADS
            if G:
                split_lo(3 * h + 1)
            if S:
                mask_att(p, 0)
            if p >= 1:
                dve.wait_ge(osq_ready, p)
                V.tensor_reduce(osm[:, 0, :], sq[:, 0, :].rearrange("p (t v) -> p t v", t=4), mybir.AxisListType.X,
                                ALU.add).then_inc(oms_ready, 1)
            if G:
                g = gs[:, h % 3, :]
                dve.wait_ge(eg_ready, h + 1)
                V.tensor_scalar(g, g, CLAMP, None, ALU.min).then_inc(eg_clamped, 1)
                dve.wait_ge(sg_ready, h + 1)
                plan.empty(V.tensor_tensor(g, bank[plan.bank(("g", h))][:, :], g, ALU.mult), "dve", ("g", h))
                split_lo(3 * h + 2)
            if p >= 1:
                dve.wait_ge(or_ready, p)
                V.tensor_tensor(tmp[:, 0, :].rearrange("p (t v) -> p t v", t=4),
                                bank[7][:, :].rearrange("p (t v) -> p t v", t=4),
                                osm[:, 1, :].unsqueeze(2).to_broadcast([P, 4, P]), ALU.mult).then_inc(on_ready, 1)
            if S:
                states(p, 0, 0)
                states(p, 0, 1)
            if G:
                ada_slot(h, 1)
            if p >= 1:
                r = p - 1
                key = ("ot", r)
                plan.wait_ready(dve, key)
                ins = V.scalar_tensor_tensor(out=yT[:, r, :], in0=bank[plan.bank(key)][:, :], scalar=prm("hg_norm", r),
                                             in1=gs[:, r % 3, :], op0=ALU.mult, op1=ALU.mult)
                plan.empty(ins, "dve", key)
            if S:
                states(p, 0, 2)
                states(p, 0, 3)
                mask_att(p, 1)
            if G:
                ada_slot(h, 2)
                gate_products(h, 0)
            if S:
                states(p, 1, 0)
                states(p, 1, 1)
            if G:
                split_lo(3 * h + 3)
                ada_slot(h, 3)
                gate_products(h, 1)
            if S:
                states(p, 1, 2)
                states(p, 1, 3)
        for k in range(KT):
            dve.wait_ge(hh_ready, KT + k + 1)
            V.tensor_tensor(hl[:, k, :], yT[:, k, :], hh[:, k, :].bitcast(F32), ALU.subtract).then_inc(hl_ready, 1)
        hfn[0] += KT
        for i in range(1, 4):
            split_lo(3 * HEADS + i)
        split_lo_part(0, slab0[0, 0, "up"], 0, 0, DVE_LO)
        gate_scales(0, 0)
        norm_scales(0, 1)
        gate_scales(0, 1)
        residual(0, 0)
        modulated(0, 1)

        def taps(l, n):
            out = []
            for dr in (-1, 0, 1):
                for dc in (-1, 0, 1):
                    if dr or dc:
                        ro = slice(max(0, -dr), 4 - max(0, dr))
                        co = slice(max(0, -dc), 64 - max(0, dc))
                        ri = slice(ro.start + dr, ro.stop + dr)
                        ci = slice(co.start + dc, co.stop + dc)
                        grid = lambda x, r, c: x[:, 0:SEQ].rearrange("p (r c) -> p r c", c=64)[:, r, c]
                        out.append(((dr + 1) * 3 + dc + 1, lambda x, r=ro, c=co: grid(x, r, c), lambda x, r=ri, c=ci: grid(x, r, c)))
            if n > SEQ:
                out.insert(1, (3, lambda x: x[:, SEQ + 1:T], lambda x: x[:, SEQ:T - 1]))
                out.insert(3, (5, lambda x: x[:, SEQ:T - 1], lambda x: x[:, SEQ + 1:T]))
            return out

        ntap = [0]

        def ffn_dve(l, n, last_split):
            tp = taps(l, n)
            for half in range(2):
                nf = FH[half]
                s0 = slab0[l, half, "up"]
                r0, reads = ffp[l, half, "up"]
                v0 = reads["dve"]
                t0 = l * FT + half * FH[0]
                cw = PROWS["ff_cw"] + 9 * l * FT + half * FH[0]
                c0, per = ntap[0], len(tp) - 1

                def tile(i, c, first=False, last=False):
                    u = c % 2
                    split_lo_part(l, s0 + c + 1, i, 0, 512, last=False)
                    if not first:
                        product(i, c - 1)
                    dve.wait_ge(conv_start, i * 2 + (t0 + c + 1))
                    for t, (row, o, src) in enumerate(tp):
                        if t:
                            dve.wait_ge(tap_done, i * (2 * per) + (c0 + c * per + t))
                        ins = V.scalar_tensor_tensor(out=o(conv[:, u, :]), in0=src(bank[2 * u]),
                                                     scalar=pv[:, bass.ds(i * 2 + (cw + row * FT + c), 1)],
                                                     in1=o(conv[:, u, :]), op0=ALU.mult, op1=ALU.add)
                        ins.then_inc(tap_done if t < per else psum_freed_dve, 1)
                        if t == 1:
                            split_lo_part(l, s0 + c + 1, i, 512, 1024)
                        if t == 3 and not first:
                            low(i, c - 1)

                def product(i, c):
                    dve.wait_ge(silu_done, i * 2 + (t0 + c + 1))
                    dve.wait_ge(psum_ready, i * 4 + (r0 + 2 * c + 2))
                    if t0 + c >= 2:
                        dve.wait_ge(fl_ready, i * 2 + (t0 + c - 1))
                    V.tensor_tensor(prod[:, c % 2, 0:n], bank[2 * (c % 2) + 1][:, 0:n], gated[:, c % 2, 0:n], ALU.mult)\
                        .then_inc(psum_freed_dve, 1)

                def low(i, c):
                    dve.wait_ge(fh_ready, i * 2 + (t0 + c + 1))
                    V.tensor_tensor(fl[:, bass.ds(i * 2 + c, 1), 0:n], prod[:, c % 2, 0:n].unsqueeze(1),
                                    fh[:, bass.ds(i * 2 + c, 1), 0:n].bitcast(F32), ALU.subtract).then_inc(fl_ready, 1)

                tile(0, 0, first=True)
                with dve.Fori(0, nf // 2 - 1) as i:
                    tile(i, 1)
                    tile(i, 2)
                tile(0, nf - 1, last=True)
                product(0, nf - 1)
                low(0, nf - 1)
                ntap[0] += per * nf
                plan.passed(by="dve", reads=2 * nf)
                s0 = slab0[l, half, "down"]
                if half == 0:
                    with dve.Fori(0, KT // 2 - 1) as i:
                        split_lo_part(l, s0 + 1, i, 0, DVE_LO)
                        split_lo_part(l, s0 + 2, i, 0, DVE_LO)
                    split_lo_part(l, s0 + KT - 1, 0, 0, DVE_LO)
                    split_lo_part(l, s0 + KT, 0, 0, DVE_LO)
                else:
                    for m in range(KT):
                        if m < KT - 1:
                            split_lo_part(l, s0 + m + 1, 0, 0, DVE_LO)
                        elif last_split is not None:
                            last_split()
                        key = ("fy", l, m)
                        plan.wait_ready(dve, key)
                        if m == 0:
                            dve.wait_ge(plan.freed["act"], ffp[l, 0, "down"][1]["act"] + KT)
                        plan.empty(V.tensor_tensor(yT[:, m, 0:n], bank[plan.bank(key)][:, 0:n], yT[:, m, 0:n], ALU.add),
                                   "dve", key)

        psum_freed_dve = plan.freed["dve"]
        ffn_dve(0, T, lambda: split_lo(MB0))
        norm_scales(1, 0)
        gate_scales(1, 0)
        norm_scales(1, 1)
        gate_scales(1, 1)
        residual(0, 1)
        split_lo(MB0 + 1)
        modulated(1, 0)

        def dt_rates():
            key = ("dt",)
            plan.wait_ready(dve, key)
            dve.wait_ge(mbs_landed, 64)
            u, e, w = dtw[:, 0, :], dtw[:, 1, :], dtw[:, 2, :]
            plan.empty(V.tensor_scalar(u, bank[plan.bank(key)][0:64, :], mbs[:, 0:1], None, ALU.add), "dve", key)
            plan.wait_emptied(dve, key)
            V.scalar_tensor_tensor(out=e, in0=u, scalar=-1.0, in1=u, op0=ALU.mult, op1=ALU.min).then_inc(dt_dve, 1)
            dve.wait_ge(dt_act, 1)
            step(V.tensor_scalar(w, e, 1.0, None, ALU.add))
            step.wait()
            V.scalar_tensor_tensor(out=e, in0=w, scalar=1.0, in1=e, op0=ALU.subtract, op1=ALU.subtract).then_inc(dt_dve, 1)
            dve.wait_ge(dt_act, 3)
            step(V.tensor_tensor(w, w, e, ALU.subtract))
            step.wait()
            step(V.scalar_tensor_tensor(out=dtf[:, :], in0=u, scalar=0.0, in1=w, op0=ALU.max, op1=ALU.add))
            step.wait()
            step(V.tensor_scalar(e, dtf[:, :], acol[:, 0:1], -1.0, ALU.mult, ALU.mult))
            step.wait()
            ends = []
            for d in range(2):
                r = slice(32 * d, 32 * d + 32)
                for lo, hi in ((0, P), (P, SEQ), (SEQ, T)):
                    c = slice(lo, hi) if d == 0 else slice(hi - 1, lo - 1 if lo else None, -1)
                    ins = V.tensor_tensor_scan(atf[r, c], ones[r, 0:1].to_broadcast([32, hi - lo]), dtw[r, 1, c], 0.0,
                                               ALU.mult, ALU.add)
                    if (d, lo) != (1, SEQ):
                        step(ins)
                    ends.append((r, slice(lo, hi), hi - 1 if d == 0 else lo))
            ins.then_inc(dt_dve, 1)
            dve.wait_ge(dt_dve, 3)
            for r, c, last in ends:
                step(V.tensor_scalar(elf[r, c], atf[r, c], -1.0, atf[r, last:last + 1], ALU.mult, ALU.add))
            dve.wait_ge(dt_act, 5)
            step(V.tensor_scalar(dg[:, 0:64], ident[0:64, 0:64], acol[:, 1:2], None, ALU.mult))
            V.tensor_scalar(dg[:, 64:96], ident[0:64, 0:32], mbs[:, 2:3], None, ALU.mult).then_inc(dt_dve, 1)

        def dt_by_token():
            key = ("tk", 0)
            plan.wait_ready(dve, key)
            b = bank[plan.bank(key)][:, :].rearrange("p (i t r) -> p i t r", i=2, r=64)
            V.tensor_copy(dtk[:, :, :], b[:, 0, :, :])
            plan.empty(V.tensor_copy(wtk[:, :, :], b[:, 1, :, :]), "dve", key)
            key = ("tk", 1)
            plan.wait_ready(dve, key)
            plan.empty(V.tensor_copy(atk[:, :, :], bank[plan.bank(key)][:, 0:P].rearrange("p (t r) -> p t r", r=64)), "dve", key)
            key = ("cd",)
            plan.wait_ready(dve, key)
            plan.wait_emptied(dve, ("tk", 1))
            ins = V.tensor_copy(bc[:, :], bank[plan.bank(key)][:, 0:96])
            plan.empty(ins, "dve", key)
            dve.wait_ge(dt_act, 6)
            V.tensor_tensor(wtk[:, :, :], wtk[:, :, :], dtk[:, :, :], ALU.mult).then_inc(dt_dve, 1)

        def conv_taps(g, i, key, dst, n, tile):
            dve.wait_ge(centre_ready, 4 * g + i + 1)
            b, t = n // SEQ, bank[plan.bank(key)][:, 0:n].rearrange("p (b t) -> p b t", t=SEQ)
            o = dst.rearrange("p (b t) -> p b t", t=SEQ)
            step(V.scalar_tensor_tensor(out=o[:, :, 1:SEQ], in0=t[:, :, 0:SEQ - 1], scalar=prm("mb_cw", tile),
                                        in1=o[:, :, 1:SEQ], op0=ALU.mult, op1=ALU.add))
            step.wait()
            plan.empty(V.scalar_tensor_tensor(out=o[:, :, 0:SEQ - 1], in0=t[:, :, 1:SEQ], scalar=prm("mb_cw", 64 + tile),
                                              in1=o[:, :, 0:SEQ - 1], op0=ALU.mult, op1=ALU.add), "dve", key)

        def segments(p, d, i):
            key = ("row", p, d, i)
            plan.wait_ready(dve, key)
            if p >= 1:
                plan.wait_ready(dve, ("dg", p - 1))
            r = 32 * d + 4 * p + 2 * i
            plan.empty(V.tensor_tensor(wd[d][i][:, :, :, :], bank[plan.bank(key)][:, :].rearrange("p (j t l) -> p j t l", j=2, t=2),
                                       atk[:, :, r:r + 2].rearrange("p t j -> p j t").unsqueeze(3).to_broadcast([P, 2, 2, P]),
                                       ALU.subtract), "dve", key)
            plan.wait_emptied(dve, key)
            V.tensor_scalar(wd[d][i][:, :, :, :], wd[d][i][:, :, :, :], 0.0, None, ALU.min).then_inc(seg_ready, 1)

        def weights(p, d, i):
            dve.wait_ge(decay_ready, 4 * p + 2 * d + i + 1)
            V.tensor_tensor(wd[d][i][:, :, :, :], wd[d][i][:, :, :, :],
                            cbm[:, d, :, :].unsqueeze(1).to_broadcast([P, 2, 2, P]), ALU.mult)\
                .then_inc(w_ready, 1)

        heads = lambda x: x.rearrange("p (t j c) -> p t j c", t=2, c=HD)
        dt_rates()
        for g in range(MB_GROUPS + 2):
            p, q = g - 1, g - 2
            G, S, Q = g < MB_GROUPS, 0 <= p < MB_GROUPS, q >= 0
            sl = MB0 + 2 + 3 * g
            if g == 0:
                split_lo(sl)
            if G:
                split_lo(sl + 1)
            if Q:
                key = ("dg", q)
                plan.wait_ready(dve, key)
                dve.wait_ge(off_done, q + 1)
                if q >= 1:
                    plan.wait_ready(dve, ("yt", q - 1))
                plan.empty(V.tensor_tensor(yg[:, :], bank[7][:, :], ysum[:, 0, :], ALU.add), "dve", key)
                plan.wait_emptied(dve, key)
                plan.wait_emptied(dve, ("z", q))
                V.tensor_tensor(yg[:, :], yg[:, :], sz[:, q % 2, :, :].rearrange("p t c -> p (t c)"), ALU.mult)\
                    .then_inc(yg_ready, 1)
            if G:
                conv_taps(g, 0, ("xs", g, 0), xf[:, 0, :], T, 2 * g)
            if S:
                key = ("cb", p)
                plan.wait_ready(dve, key)
                if p == 0:
                    dve.wait_ge(tri_ready, 2)
                else:
                    dve.wait_ge(w_ready, 4 * p)
                for d in range(2):
                    ins = V.tensor_tensor(cbm[:, d, :, :], bank[plan.bank(key)][:, 0:256].rearrange("p (t l) -> p t l", t=2),
                                          tri[:, d, :].unsqueeze(1).to_broadcast([P, 2, P]), ALU.mult)
                plan.empty(ins, "dve", key)
            if G:
                conv_taps(g, 1, ("xs", g, 1), xf[:, 1, :], T, 2 * g + 1)
            if g == 0:
                dt_by_token()
            if S:
                segments(p, 0, 0)
                segments(p, 0, 1)
            if Q:
                dve.wait_ge(ygsq_ready, q + 1)
                V.tensor_reduce(msq[:, 0, :], sq[:, 0, :].rearrange("p (t c) -> p t c", t=2), mybir.AxisListType.X, ALU.add)\
                    .then_inc(ygms_ready, 1)
            if S:
                weights(p, 0, 0)
                weights(p, 0, 1)
            if G:
                split_lo(sl + 2)
            if Q:
                dve.wait_ge(ygr_ready, q + 1)
                V.tensor_tensor(yg[:, :].rearrange("p (t c) -> p t c", t=2), yg[:, :].rearrange("p (t c) -> p t c", t=2),
                                msq[:, 1, :].unsqueeze(2).to_broadcast([P, 2, 256]), ALU.mult).then_inc(yn_ready, 1)
            if G:
                conv_taps(g, 2, ("b", g), bf[:, g % 2, :], T, 16 + g)
            if S:
                for d in range(2):
                    key = ("st", p, d)
                    dve.wait_ge(hs_ready, 2 * p + d + 1)
                    r = slice(32 * d + 4 * p, 32 * d + 4 * p + 4)
                    step(V.tensor_tensor(h1[:, d, :].rearrange("p (j c) -> p j c", c=HD), hs[:, d, :].rearrange("p (j c) -> p j c", c=HD),
                                         bc[:, r].unsqueeze(2).to_broadcast([P, 4, HD]), ALU.mult))
                    step.wait()
                    plan.empty(V.tensor_tensor(h1[:, d, :], bank[plan.bank(key)][:, 256:512], h1[:, d, :], ALU.add), "dve", key)
                segments(p, 1, 0)
                segments(p, 1, 1)
                weights(p, 1, 0)
                weights(p, 1, 1)
            if G:
                conv_taps(g, 3, ("c", g), cf[:, g % 2, :], SEQ, 24 + g)
                split_lo(sl + 3)
            if S:
                for d in range(2):
                    key = ("off", p, d)
                    plan.wait_ready(dve, key)
                    if p == 0 and d == 0:
                        dve.wait_ge(dt_act, 7)
                    r = slice(32 * d + 4 * p, 32 * d + 4 * p + 4)
                    plan.empty(V.tensor_tensor(heads(ysum[:, d, :]), heads(bank[plan.bank(key)][:, :]),
                                               eik[:, :, r].unsqueeze(3).to_broadcast([P, 2, 4, HD]), ALU.mult), "dve", key)
                plan.wait_emptied(dve, ("off", p, 1))
                step(V.tensor_tensor(ysum[:, 0, :], ysum[:, 0, :], ysum[:, 1, :], ALU.add))
                dve.wait_ge(scaled_ready, 7 * p + 7)
                step.wait()
                V.tensor_tensor(ysum[:, 0, :], ysum[:, 0, :], skip[:, :, :].rearrange("p t c -> p (t c)"), ALU.add)\
                    .then_inc(off_done, 1)
        for k in range(KT):
            dve.wait_ge(hh_ready, hfn[0] + k + 1)
            V.tensor_tensor(hl[:, k, :], yT[:, k, :], hh[:, k, :].bitcast(F32), ALU.subtract).then_inc(hl_ready, 1)
        hfn[0] += KT
        for m in range(KT - 1):
            split_lo(OM0 + m + 1)
        split_lo_part(1, slab0[1, 0, "up"], 0, 0, DVE_LO)
        residual(1, 0, SEQ)
        modulated(1, 1, SEQ)
        ffn_dve(1, SEQ, None)
        residual(1, 1, SEQ)
        for t in range(2):
            key = ("out", t, 1)
            plan.wait_ready(dve, key)
            V.tensor_copy(rows_out[:, t, 512:1024], bank[plan.bank(key)][:, :]).then_inc(rows_dve, 1)

    @block.tensor
    def _(pe):
        def gemm(dst, w, hi, lo, nk):
            for k in range(nk):
                W, L = w(wh, k), w(wl, k)
                pe.matmul(dst, W, hi(k), start=(k == 0), stop=False)
                pe.matmul(dst, W, lo(k), start=False, stop=False)
                ins = pe.matmul(dst, L, hi(k), start=False, stop=(k == nk - 1))
            return ins

        def act_tiles(n=T):
            return (lambda k: hh[:, k, 0:n]), (lambda k: hl[:, k, 0:n])

        def need_slab(i):
            pe.wait_ge(w_lo, i + 1)

        def wide_w(i, half):
            s = i % 2
            return lambda w, k: w[:, s, k * 256 + half * P:k * 256 + half * P + P]

        def project(key, i, half, n=T, nk=KT):
            plan.wait_free(pe, key)
            hi, lo = act_tiles(n)
            plan.done(gemm(bank[plan.bank(key)][:, 0:n], wide_w(i, half), hi, lo, nk), key)

        def square_sum(key, n=T):
            plan.wait_free(pe, key)
            for m in range(KT):
                sqm[0] += 1
                pe.wait_ge(sq_ready, sqm[0])
                ins = pe.matmul(bank[7][:, 0:n], ones[:, :], sq[:, m % 2, 0:n], start=(m == 0), stop=(m == KT - 1))
                if m < KT - 1:
                    ins.then_inc(sq_used, 1)
            plan.done(ins, key)

        sqm = [0]
        pe.wait_ge(consts, 1)
        pe.wait_ge(p_landed, 16 * len(pdma))
        for s in range(PSLOTS):
            key = ("pv", s)
            plan.wait_free(pe, key)
            n = min(P, NPROWS - s * P)
            plan.done(pe.transpose(bank[plan.bank(key)][:, 0:n], prow[0:n, s, :], ident[0:n, 0:n]), key)
        pe.wait_ge(x_landed, 32)
        for k in range(KT):
            key = ("xt", k)
            plan.wait_free(pe, key)
            for t in range(4):
                ins = pe.transpose(bank[plan.bank(key)][:, t * P:(t + 1) * P], xrow[:, t, k * P:(k + 1) * P], ident[:, :])
            plan.done(ins, key)

        def ada_block(n):
            key = ("am", n)
            plan.wait_free(pe, key)
            for half in range(2):
                pe.wait_ge(a_landed[half], 16 * (n + 1))
                for j in range(4):
                    ins = pe.matmul(bank[plan.bank(key)][32 * j:32 * j + 32, :], scc[:, 4 * half + j, :], araw[:, half, j, :],
                                    start=(half == 0), stop=(half == 1))
                if half == 0:
                    ins.then_inc(a_used, 1)
            plan.done(ins, key)

        def ada_turn(n):
            key = ("at", n)
            plan.wait_free(pe, key)
            for c in range(4):
                ins = pe.transpose(bank[plan.bank(key)][:, c * P:(c + 1) * P], asum[:, c * P:(c + 1) * P], ident[:, :])
            plan.done(ins, key)

        def ada_slot(h, slot):
            if 1 <= slot <= ada_of[h]:
                ada_turn(ada_start[h] + slot - 1)
            if slot < ada_of[h]:
                ada_block(ada_start[h] + slot)

        pe.wait_ge(silu_c, 4)
        for n in range(ADA_FIRST):
            ada_block(n)
            ada_turn(n)
        square_sum(("ss", "pre", 0, 0))

        def head_v(h):
            key = ("v", h)
            need_slab(3 * h)
            plan.wait_free(pe, key)
            s = (3 * h) % 2
            if h == 0:
                pe.wait_ge(hl_ready, KT)
            hi, lo = act_tiles()
            plan.done(gemm(bank[plan.bank(key)][:, :], lambda w, k: w[:, s, k * P:(k + 1) * P], hi, lo, KT), key)

        def v_turn(h):
            key = ("vt", h)
            plan.wait_emptied(pe, ("v", h))
            plan.wait_free(pe, key)
            for t in range(4):
                r = slice(t * P, (t + 1) * P)
                ins = pe.transpose(bank[plan.bank(key)][:, r], sq[:, 1, r], ident[:, :])
            plan.done(ins, key)

        def att(h, d):
            key = ("att", h, d)
            pe.wait_ge(qk_ready, 2 * h + d + 1)
            plan.wait_free(pe, key)
            for t in range(4):
                r = slice(t * P, (t + 1) * P)
                ins = pe.matmul(bank[plan.bank(key)][:, r], gA[d][:, r], gC[d][:, r], start=True, stop=True)
            plan.done(ins, key)

        def ke(h, d):
            key = ("ke", h, d)
            plan.wait_free(pe, key)
            for t in range(4):
                r = slice(t * P, (t + 1) * P)
                ins = pe.transpose(bank[plan.bank(key)][:, r], gB[d][:, r], ident[:, :])
            plan.done(ins, key)

        def kv(h, d, ti):
            key = ("kv", h, d, ti)
            t = TILES[d][ti]
            plan.wait_emptied(pe, ("ke", h, d))
            plan.wait_free(pe, key)
            plan.done(pe.matmul(bank[plan.bank(key)][:, :], ket[d][:, t, :],
                                vm[:, h % 2, t, :, :].rearrange("p c v -> p (c v)"), start=True, stop=True), key)

        def intra(h, d):
            plan.wait_emptied(pe, ("att", h, d))
            if d == 0 and h >= 1:
                pe.wait_ge(on_ready, h)
            for t in range(4):
                r = slice(t * P, (t + 1) * P)
                ins = pe.matmul(bank[7][:, r], attm[d][:, t, :], vtok[:, h % 2, t, :], start=(d == 0 and t == 0), stop=False,
                                skip_group_check=True)
            ins.then_inc(intra_done, 1)

        def inter(h, d):
            pe.wait_ge(qin_ready, 2 * h + d + 1)
            plan.wait_emptied(pe, ("kv", h, d, 3))
            for j in range(1, NCH):
                t = TILES[d][j // 4]
                c = 4 * t + (j % 4 if d == 0 else 3 - j % 4)
                q = (c % 4) * CH
                ins = pe.matmul(bank[7][q:q + CH, t * P:(t + 1) * P], gD[d][h % 2][:, c * CH:(c + 1) * CH], st[d][:, j - 1, :],
                                start=False, stop=(d == 1 and j == NCH - 1), skip_group_check=True)
            ins.then_inc(inter_done, 1)

        def o_turn(h):
            key = ("ot", h)
            pe.wait_ge(on_ready, h + 1)
            plan.wait_free(pe, key)
            for t in range(4):
                r = slice(t * P, (t + 1) * P)
                ins = pe.transpose(bank[plan.bank(key)][:, r], tmp[:, 0, r], ident[:, :])
            plan.done(ins, key)

        for h in range(HEADS + 2):
            p = h - 1
            G, S = h < HEADS, 0 <= p < HEADS
            if G:
                head_v(h)
            if p >= 1:
                inter(p - 1, 1)
            if S:
                att(p, 0)
                ke(p, 0)
            if G:
                need_slab(3 * h + 1)
                project(("g", h), 3 * h + 1, 0)
                v_turn(h)
                ada_slot(h, 0)
            if S:
                kv(p, 0, 0)
                kv(p, 0, 1)
            if G:
                project(("q", h), 3 * h + 1, 1)
                ada_slot(h, 1)
            if p >= 1:
                o_turn(p - 1)
            if S:
                kv(p, 0, 2)
                kv(p, 0, 3)
                att(p, 1)
                ke(p, 1)
                intra(p, 0)
            if G:
                need_slab(3 * h + 2)
                project(("f", h, 0), 3 * h + 2, 0)
                ada_slot(h, 2)
            if S:
                kv(p, 1, 0)
                kv(p, 1, 1)
                intra(p, 1)
            if G:
                project(("f", h, 1), 3 * h + 2, 1)
                ada_slot(h, 3)
            if S:
                kv(p, 1, 2)
                kv(p, 1, 3)
                inter(p, 0)
        pe.wait_ge(hl_ready, 2 * KT)
        def add_squares(m, key, n):
            if m == 0:
                plan.wait_free(pe, key)
            sqm[0] += 1
            pe.wait_ge(sq_ready, sqm[0])
            ins = pe.matmul(bank[7][:, 0:n], ones[:, :], sq[:, m % 2, 0:n], start=(m == 0), stop=(m == KT - 1),
                            skip_group_check=True)
            if m < KT - 1:
                ins.then_inc(sq_used, 1)
            else:
                plan.done(ins, key)

        for m in range(KT):
            i = 3 * HEADS + m // 2
            need_slab(i)
            project(("y", 0, m), i, m % 2)
            if m:
                add_squares(m - 1, ("ss", 0, 0), T)
        add_squares(KT - 1, ("ss", 0, 0), T)
        square_sum(("ss2", 0, 0))

        def ffn_pe(l, n, hl_count):
            psum_freed_dve = plan.freed["dve"]
            hi, lo = act_tiles(n)
            fhi, flo = (lambda k: fh[:, k, 0:n]), (lambda k: fl[:, k, 0:n])
            pe.wait_ge(hl_ready, hl_count)
            for half in range(2):
                nf = FH[half]
                s0 = slab0[l, half, "up"]
                r0, reads = ffp[l, half, "up"]
                v0 = reads["dve"]
                with pe.Fori(0, nf // 2) as i:
                    for u in range(2):
                        s = s0 + u
                        pe.wait_ge(w_lo, i * 2 + (s + 1))
                        for part in range(2):
                            pe.wait_ge(psum_freed_dve, i * 4 + (v0 + 2 * u - 3 + part))
                            w = lambda w, k, s=s, part=part: w[:, s % 2, k * 256 + part * P:k * 256 + part * P + P]
                            gemm(bank[2 * u + part][:, 0:n], w, hi, lo, KT).then_inc(psum_ready, 1)
                plan.passed(fills=2 * nf)
                s0 = slab0[l, half, "down"]
                r0, reads = ffp[l, 0, "down"]
                pe.wait_ge(fl_ready, l * FT + half * FH[0] + nf)
                if half == 0:
                    with pe.Fori(0, KT // 2) as i:
                        for u in range(2):
                            s = s0 + u
                            pe.wait_ge(w_lo, i * 2 + (s + 1))
                            pe.wait_ge(plan.freed["act"], i * 2 + (reads["act"] + u - 1))
                            w = lambda w, k, s=s: w[:, s % 2, k * P:(k + 1) * P]
                            gemm(bank[4 + u][:, 0:n], w, fhi, flo, nf).then_inc(psum_ready, 1)
                    plan.passed(fills=KT)
                else:
                    for m in range(KT):
                        s = s0 + m
                        pe.wait_ge(w_lo, s + 1)
                        key = ("fy", l, m)
                        if m < 2:
                            pe.wait_ge(plan.freed["act"], reads["act"] + KT)
                        plan.wait_free(pe, key)
                        w = lambda w, k, s=s: w[:, s % 2, k * P:(k + 1) * P]
                        plan.done(gemm(bank[plan.bank(key)][:, 0:n], w, fhi, flo, nf), key)
                        if m:
                            add_squares(m - 1, ("ss", l, 1), n)
                    add_squares(KT - 1, ("ss", l, 1), n)

        ffn_pe(0, T, 3 * KT)
        square_sum(("ss2", 0, 1))

        pe.wait_ge(hl_ready, 4 * KT)
        hi, lo = act_tiles()
        key = ("dt",)
        plan.wait_free(pe, key)
        for half in range(2):
            i = MB0 + half
            need_slab(i)
            for kk in range(4):
                k = 4 * half + kk
                W, L = wh[:, i % 2, kk * 64:(kk + 1) * 64], wl[:, i % 2, kk * 64:(kk + 1) * 64]
                dst = bank[plan.bank(key)][0:64, :]
                pe.matmul(dst, W, hi(k), start=(k == 0), stop=False)
                pe.matmul(dst, W, lo(k), start=False, stop=False)
                ins = pe.matmul(dst, L, hi(k), start=False, stop=(k == KT - 1))
        plan.done(ins, key)

        def dt_turns():
            pe.wait_ge(dt_dve, 4)
            key = ("tk", 0)
            plan.wait_free(pe, key)
            for i, src in enumerate((dtf, elf)):
                for t in range(4):
                    c = (4 * i + t) * 64
                    ins = pe.transpose(bank[plan.bank(key)][:, c:c + 64], src[:, t * P:(t + 1) * P], ident[0:64, 0:64])
            plan.done(ins, key)
            key = ("tk", 1)
            plan.wait_free(pe, key)
            for t in range(2):
                ins = pe.transpose(bank[plan.bank(key)][:, t * 64:(t + 1) * 64], atf[:, t * P:(t + 1) * P], ident[0:64, 0:64])
            plan.done(ins, key)
            key = ("cd",)
            plan.wait_free(pe, key)
            plan.done(pe.matmul(bank[plan.bank(key)][:, 0:96], ones[0:64, :], dg[:, :], start=True, stop=True), key)

        def turns(key, src):
            plan.wait_free(pe, key)
            for t in range(4):
                r = slice(t * P, (t + 1) * P)
                ins = pe.transpose(bank[plan.bank(key)][:, r], src[:, r], ident[:, :])
            plan.done(ins, key)

        def at_rows(p, d, i):
            key = ("row", p, d, i)
            plan.wait_free(pe, key)
            for jj in range(2):
                r = 32 * d + 4 * p + 2 * i + jj
                ins = pe.matmul(bank[plan.bank(key)][:, jj * SEQ:(jj + 1) * SEQ], ident[0:64, r:r + 1].to_broadcast([64, P]),
                                atf[:, 0:SEQ], start=True, stop=True)
            plan.done(ins, key)

        for g in range(MB_GROUPS + 2):
            p, q = g - 1, g - 2
            G, S, Q = g < MB_GROUPS, 0 <= p < MB_GROUPS, q >= 0
            sl = MB0 + 2 + 3 * g
            if G:
                need_slab(sl)
                project(("xs", g, 0), sl, 0)
            if S:
                for f in range(2):
                    pe.wait_ge(conv_silu, 4 * p + f + 1)
                    turns(("tx", p, f), xf[:, f, :])
                pe.wait_ge(conv_silu, 4 * p + 4)
                turns(("tb", p), bf[:, p % 2, :])
                key = ("cb", p)
                plan.wait_free(pe, key)
                for t in range(2):
                    r = slice(t * P, (t + 1) * P)
                    ins = pe.matmul(bank[plan.bank(key)][:, r], bf[:, p % 2, r], cf[:, p % 2, r], start=True, stop=True)
                plan.done(ins, key)
            if G:
                project(("xs", g, 1), sl, 1)
            if g == 0:
                dt_turns()
            if S:
                at_rows(p, 0, 0)
                at_rows(p, 0, 1)
            if G:
                need_slab(sl + 1)
                project(("b", g), sl + 1, 0)
            if S:
                plan.wait_emptied(pe, ("tb", p))
                for d in range(2):
                    pe.wait_ge(scaled_ready, 7 * p + 2 * d + 2)
                    key = ("st", p, d)
                    plan.wait_free(pe, key)
                    b = bank[plan.bank(key)]
                    pe.matmul(b[:, 0:256], btok[:, 2, :], wx[d][:, 0, :], start=True, stop=False)
                    pe.matmul(b[:, 0:256], btok[:, 3, :], wx[d][:, 1, :], start=False, stop=True)
                    plan.done(pe.matmul(b[:, 256:512], btok[:, d, :], wx[d][:, 2, :], start=True, stop=True), key)
                at_rows(p, 1, 0)
                at_rows(p, 1, 1)
            if Q:
                key = ("yt", q)
                pe.wait_ge(yn_ready, q + 1)
                plan.wait_free(pe, key)
                for f in range(2):
                    for t in range(2):
                        ins = pe.transpose(bank[plan.bank(key)][:, f * 256 + t * P:f * 256 + (t + 1) * P],
                                           yg[:, t * 256 + f * P:t * 256 + (f + 1) * P], ident[:, :])
                plan.done(ins, key)
            if G:
                project(("c", g), sl + 1, 1, SEQ)
            if S:
                for d in range(2):
                    key = ("off", p, d)
                    plan.wait_emptied(pe, ("st", p, d))
                    plan.wait_free(pe, key)
                    for t in range(2):
                        h = hs if t == d else h1
                        ins = pe.matmul(bank[plan.bank(key)][:, t * 256:(t + 1) * 256], cf[:, p % 2, t * P:(t + 1) * P],
                                        h[:, d, :], start=True, stop=True)
                    plan.done(ins, key)
            if G:
                key = ("z", g)
                need_slab(sl + 2)
                plan.wait_free(pe, key)
                s = (sl + 2) % 2
                for t in range(2):
                    dst, r = bank[plan.bank(key)][:, t * 256:(t + 1) * 256], slice(t * P, (t + 1) * P)
                    for k in range(KT):
                        c = slice(k * 256, (k + 1) * 256)
                        pe.matmul(dst, hh[:, k, r], wh[:, s, c], start=(k == 0), stop=False)
                        pe.matmul(dst, hl[:, k, r], wh[:, s, c], start=False, stop=False)
                        ins = pe.matmul(dst, hh[:, k, r], wl[:, s, c], start=False, stop=(k == KT - 1))
                plan.done(ins, key)
            if S:
                key = ("dg", p)
                plan.wait_free(pe, key)
                pe.wait_ge(scaled_ready, 7 * p + 6)
                for d in range(2):
                    for j in range(4):
                        if j % 2 == 0:
                            pe.wait_ge(w_ready, 4 * p + 2 * d + j // 2 + 1)
                        for t in range(2):
                            ins = pe.matmul(bank[7][:, t * 256 + j * HD:t * 256 + (j + 1) * HD], wd[d][j // 2][:, j % 2, t, :],
                                            dx[d][:, t, j * HD:(j + 1) * HD], start=(d == 0 and j == 0 and t == 0),
                                            stop=(d == 1 and j == 3 and t == 1), skip_group_check=True)
                plan.done(ins, key)
        pe.wait_ge(hl_ready, 5 * KT)
        flat = lambda x: x[:, :, :].rearrange("p a b -> p (a b)")
        for m in range(KT):
            i = OM0 + m
            need_slab(i)
            key = ("y", 1, m)
            plan.wait_free(pe, key)
            plan.done(gemm(bank[plan.bank(key)][:, 0:SEQ], lambda w, k: w[:, i % 2, k * P:(k + 1) * P],
                           lambda k: flat(hh)[:, k * SEQ:(k + 1) * SEQ], lambda k: flat(hl)[:, k * SEQ:(k + 1) * SEQ], 2 * KT), key)
            if m:
                add_squares(m - 1, ("ss", 1, 0), SEQ)
        add_squares(KT - 1, ("ss", 1, 0), SEQ)
        square_sum(("ss2", 1, 0), SEQ)
        ffn_pe(1, SEQ, 6 * KT)
        pe.wait_ge(x_new, 4 * KT)
        for t in range(2):
            for half in range(2):
                key = ("out", t, half)
                plan.wait_free(pe, key)
                for c in range(4):
                    ins = pe.transpose(bank[plan.bank(key)][:, c * P:(c + 1) * P], xT[:, 4 * half + c, t * P:(t + 1) * P],
                                       ident[:, :])
                plan.done(ins, key)

    ctx.close()


INPUTS = ["x", "c", "ctx", "c_ctx", "ada_w", "ada_b", "pre_norm", "post_norm", "hg_w_in", "hg_w_out", "hg_norm",
          "hg_lb_logits", "mb_w_in", "mb_conv_w", "mb_conv_b", "mb_dt_bias", "mb_a_log", "mb_d", "mb_norm", "mb_w_out",
          "ffn_w_up", "ffn_conv_w", "ffn_conv_b", "ffn_w_down"]


def kernel(**inputs):
    import numpy as _np
    import concourse.bacc as _bacc
    from concourse import mybir as _mybir
    from concourse.bass_utils import run_bass_kernel_spmd as _run

    nc = _bacc.Bacc("TRN2", target_bir_lowering=False, num_devices=1, dynamic_dma_scratch_size=1024)
    arrays, aps = {}, {}
    for name in INPUTS:
        arr = _np.ascontiguousarray(inputs[name])
        arrays[f"in_{name}"] = arr
        aps[name] = nc.dram_tensor(f"in_{name}", arr.shape, _mybir.dt.from_np(arr.dtype), kind="ExternalInput").ap()
    out = nc.dram_tensor("out_x", (1, SEQ, D), _mybir.dt.float32, kind="ExternalOutput").ap()
    program(nc, aps, out)
    r = _run(nc, [arrays], core_ids=[0])
    return r.results[0]["out_x"]
```

```python
from contextlib import ExitStack

import concourse.bass as bass
from concourse import mybir

F32 = mybir.dt.float32
F32R = mybir.dt.float32r
U32 = mybir.dt.uint32
ALU = mybir.AluOpType
ACT = mybir.ActivationFunctionType

P = 128
D = 1024
SEQ = 256
T = 2 * SEQ
KT = D // P
EPS = 1e-6
DVE_LO = 1024
HEADS = 8
CH = 32
NCH = T // CH
MB_INNER = 2048
MB_GROUPS = 8
HD = 64
FF = 2816
FT = FF // P
FH = (12, 10)
CLAMP = 2.0 ** 62


class Steps:

    def __init__(self, eng, sem):
        self.eng, self.sem, self.n = eng, sem, 0

    def __call__(self, ins):
        self.n += 1
        ins.then_inc(self.sem, 1)
        return self.n

    def wait(self, n=None):
        self.eng.wait_ge(self.sem, self.n if n is None else n)


class PsumPlan:

    def __init__(self, ready, freed):
        self.ready, self.freed = ready, freed
        self.index, self.prev, self.by, self.last = {}, {}, {}, {}
        self.total, self.count = 0, {e: 0 for e in freed}
        self.filled, self.read = 0, {e: 0 for e in freed}

    def add(self, key, bank, by):
        self.prev[key] = self.last.get(bank)
        self.total += 1
        self.index[key] = (self.total, bank)
        self.count[by] += 1
        self.by[key] = (by, self.count[by])
        self.last[bank] = key

    def loop(self, fills, reads):
        before = (self.total, dict(self.count))
        self.total += fills
        for by, n in reads.items():
            self.count[by] += n
        return before

    def passed(self, fills=0, by=None, reads=0):
        self.filled += fills
        if by:
            self.read[by] += reads

    def done(self, ins, key):
        self.filled += 1
        assert self.index[key][0] == self.filled, key
        ins.then_inc(self.ready, 1)

    def empty(self, ins, by, key):
        self.read[by] += 1
        assert self.by[key] == (by, self.read[by]), key
        ins.then_inc(self.freed[by], 1)

    def wait_emptied(self, eng, key):
        by, n = self.by[key]
        eng.wait_ge(self.freed[by], n)

    def bank(self, key):
        return self.index[key][1]

    def wait_free(self, pe, key):
        if self.prev[key] is not None:
            by, n = self.by[self.prev[key]]
            pe.wait_ge(self.freed[by], n)

    def wait_ready(self, eng, key):
        eng.wait_ge(self.ready, self.index[key][0])


def rows(*groups):
    at, out = 0, {}
    for name, n in groups:
        out[name] = at
        at += n
    return out, at


PROWS, NPROWS = rows(("c", 8), ("c_ctx", 8), ("ada_b", 96), ("pre", 32), ("post", 32), ("hg_norm", 8),
                     ("lb", 32), ("mb_cw", 96), ("mb_cb", 32), ("mb_norm", 16), ("ff_cb", 44), ("ff_cw", 396))
PSLOTS = -(-NPROWS // P)


def program(nc, a, out):
    ctx = ExitStack()
    sems = {}

    def sem(name):
        if name not in sems:
            sems[name] = ctx.enter_context(nc.semaphore(name))
        return sems[name]

    def sb(stack, name, shape, dt=F32):
        return stack.enter_context(nc.sbuf_tensor(name, shape, dt))

    xT = sb(ctx, "xT", [P, KT, T])
    yT = sb(ctx, "yT", [P, KT, T])
    hh = sb(ctx, "hh", [P, KT, T], F32R)
    hl = sb(ctx, "hl", [P, KT, T], F32R)
    wraw = sb(ctx, "wraw", [P, 2, 2048])
    wh = sb(ctx, "wh", [P, 2, 2048], F32R)
    wl = sb(ctx, "wl", [P, 2, 2048], F32R)
    pv = sb(ctx, "pv", [P, NPROWS])
    mod = sb(ctx, "mod", [P, 2, 48, 2])
    nsc = sb(ctx, "nsc", [P, 2, 2, KT, 2])
    gsc = sb(ctx, "gsc", [P, 2, 2, KT, 2])
    ident = sb(ctx, "ident", [P, P])
    ones = sb(ctx, "ones", [P, P])
    eps = sb(ctx, "eps", [P, 1])
    sq = sb(ctx, "sq", [P, 2, T])
    tmp = sb(ctx, "tmp", [P, 2, T])
    rstd = sb(ctx, "rstd", [P, T])
    mbs = sb(ctx, "mbs", [64, 3])
    bank = [ctx.enter_context(nc.psum_tensor(f"bank{i}", [P, 512], F32)) for i in range(8)]
    xrow = yT[:, :, :].rearrange("p a b -> p (a b)").rearrange("p (t c) -> p t c", t=4)

    ff = ExitStack()
    fh = sb(ff, "fh", [P, FH[0], T], F32R)
    fl = sb(ff, "fl", [P, FH[0], T], F32R)
    conv = sb(ff, "conv", [P, 2, T])
    gated = sb(ff, "gated", [P, 2, T])
    prod = sb(ff, "prod", [P, 2, T])
    rows_out = sb(ff, "rows_out", [P, 2, D])
    ff.close()

    hg = ExitStack()
    araw = sb(hg, "araw", [P, 2, 4, 512])
    scc = sb(hg, "scc", [P, KT, 32])
    asum = sb(hg, "asum", [P, 512])
    ared = sb(hg, "ared", [P, 4, 2])
    osm = sb(hg, "osm", [P, 2, 4])
    gA = [sb(hg, f"gA{d}", [P, T]) for d in range(2)]
    gB = [sb(hg, f"gB{d}", [P, T]) for d in range(2)]
    gC = [sb(hg, f"gC{d}", [P, T]) for d in range(2)]
    gD = [[sb(hg, f"gD{d}{i}", [P, T]) for i in range(2)] for d in range(2)]
    sm = sb(hg, "sm", [P, 2, 2, 3, NCH])
    gs = sb(hg, "gs", [P, 3, T])
    vtok = sb(hg, "vtok", [P, 2, 4, P])
    vm = sb(hg, "vm", [P, 2, 4, 4, P])
    st = [sb(hg, f"st{d}", [P, NCH - 1, P]) for d in range(2)]
    ket = [sb(hg, f"ket{d}", [P, 4, P]) for d in range(2)]
    attm = [sb(hg, f"attm{d}", [P, 4, P]) for d in range(2)]
    mask = sb(hg, "mask", [P, 2, P], U32)
    lb = sb(hg, "lb", [P, 2, KT])
    omlb = sb(hg, "omlb", [P, 2, 2, KT])
    lbt = sb(hg, "lbt", [P, 3, 2, KT])
    keep = sb(hg, "keep", [P, NCH + 1, CH])
    hg.close()

    mb = ExitStack()
    dtw = sb(mb, "dtw", [64, 3, T])
    dtf = sb(mb, "dtf", [64, T])
    atf = sb(mb, "atf", [64, T])
    elf = sb(mb, "elf", [64, T])
    acol = sb(mb, "acol", [64, 2])
    identr = sb(mb, "identr", [64, 64], F32R)
    ath = sb(mb, "ath", [64, SEQ], F32R)
    atl = sb(mb, "atl", [64, SEQ], F32R)
    dg = sb(mb, "dg", [64, 96])
    bc = sb(mb, "bc", [P, 96])
    dtk = sb(mb, "dtk", [P, 4, 64])
    wtk = sb(mb, "wtk", [P, 4, 64])
    atk = sb(mb, "atk", [P, 2, 64])
    eik = sb(mb, "eik", [P, 2, 64])
    tri = sb(mb, "tri", [P, 2, P])
    xf = sb(mb, "xf", [P, 2, T])
    bf = sb(mb, "bf", [P, 2, T])
    cf = sb(mb, "cf", [P, 2, SEQ])
    xtok = sb(mb, "xtok", [P, 4, 256])
    btok = sb(mb, "btok", [P, 4, P])
    wx = [sb(mb, f"wx{d}", [P, 3, 256]) for d in range(2)]
    dx = [sb(mb, f"dx{d}", [P, 2, 256]) for d in range(2)]
    skip = sb(mb, "skip", [P, 2, 256])
    sz = sb(mb, "sz", [P, 2, 2, 256])
    hs = sb(mb, "hs", [P, 2, 256])
    h1 = sb(mb, "h1", [P, 2, 256])
    cbm = sb(mb, "cbm", [P, 2, 2, P])
    wd = [[sb(mb, f"wd{d}{i}", [P, 2, 2, P]) for i in range(2)] for d in range(2)]
    ysum = sb(mb, "ysum", [P, 2, T])
    yg = sb(mb, "yg", [P, T])
    msq = sb(mb, "msq", [P, 2, 2])
    mb.close()
    qt = tmp[:, 1, :]
    maskf = sq[:, 1, 0:2 * P].rearrange("p (d s) -> p d s", d=2)
    prow = st[0][:, :, :].rearrange("p a b -> p (a b)")[:, 0:PSLOTS * P].rearrange("p (s c) -> p s c", s=PSLOTS)

    psum_ready = sem("psum_ready")
    plan = PsumPlan(psum_ready, {"act": sem("psum_freed_by_act"), "dve": sem("psum_freed_by_dve")})

    ADA_FIRST = 4
    SUM_AT = 1
    ada_of = [3, 3, 3, 3, 2, 2, 2, 2]
    ada_start = [ADA_FIRST + sum(ada_of[:h]) for h in range(HEADS + 1)]
    for s in range(PSLOTS):
        plan.add(("pv", s), s % 3, "dve")
    for k in range(KT):
        plan.add(("xt", k), (PSLOTS + k) % 3, "act" if k % 2 else "dve")
    for n in range(ADA_FIRST):
        if n == SUM_AT:
            plan.add(("ss", "pre", 0, 0), 7, "act")
        plan.add(("am", n), 3, "act")
        plan.add(("at", n), 3, "dve")
    ring = {"g": 0, "s": 0}

    def gkey(key, by):
        plan.add(key, ring["g"] % 3, by)
        ring["g"] += 1

    def skey(key, by):
        plan.add(key, 4 + ring["s"] % 3, by)
        ring["s"] += 1

    TILES = ([2, 3, 0, 1], [3, 2, 1, 0])
    def ada_key(h, slot):
        if h < HEADS:
            if 1 <= slot <= ada_of[h]:
                skey(("at", ada_start[h] + slot - 1), "dve")
            if slot < ada_of[h]:
                plan.add(("am", ada_start[h] + slot), 3, "act")

    for h in range(HEADS + 2):
        p = h - 1
        G, S = h < HEADS, 0 <= p < HEADS
        if G:
            gkey(("v", h), "act")
        if S:
            skey(("att", p, 0), "dve")
            skey(("ke", p, 0), "act")
        if G:
            gkey(("g", h), "dve")
            skey(("vt", h), "act")
        ada_key(h, 0)
        if S:
            skey(("kv", p, 0, 0), "dve")
            skey(("kv", p, 0, 1), "dve")
        if G:
            gkey(("q", h), "act")
        ada_key(h, 1)
        if p >= 1:
            skey(("ot", p - 1), "dve")
        if S:
            skey(("kv", p, 0, 2), "dve")
            skey(("kv", p, 0, 3), "dve")
            skey(("att", p, 1), "dve")
            skey(("ke", p, 1), "act")
        if G:
            gkey(("f", h, 0), "act")
        ada_key(h, 2)
        if S:
            skey(("kv", p, 1, 0), "dve")
            skey(("kv", p, 1, 1), "dve")
        if G:
            gkey(("f", h, 1), "act")
        ada_key(h, 3)
        if S:
            skey(("kv", p, 1, 2), "dve")
            skey(("kv", p, 1, 3), "dve")
    for m in range(KT):
        plan.add(("y", 0, m), m % 3, "act")

    plan.add(("ss", 0, 0), 7, "act")
    plan.add(("ss2", 0, 0), 7, "act")
    ffp = {}

    def plan_ffn(l):
        for half in range(2):
            ffp[l, half, "up"] = plan.loop(2 * FH[half], {"dve": 2 * FH[half]})
            if half == 0:
                ffp[l, half, "down"] = plan.loop(KT, {"act": KT})
            else:
                for m in range(KT):
                    plan.add(("fy", l, m), 4 + m % 2, "dve")
        plan.add(("ss", l, 1), 7, "act")

    plan_ffn(0)
    plan.add(("ss2", 0, 1), 7, "act")
    plan.add(("dt",), 3, "dve")
    ring = {"g": 0, "s": 0}

    def mkey(key, by):
        plan.add(key, 3 + ring["s"] % 4, by)
        ring["s"] += 1

    for g in range(MB_GROUPS + 2):
        p, q = g - 1, g - 2
        G, S, Q = g < MB_GROUPS, 0 <= p < MB_GROUPS, q >= 0
        if G:
            gkey(("xs", g, 0), "dve")
        if S:
            mkey(("tx", p, 0), "act")
            mkey(("tx", p, 1), "act")
            mkey(("tb", p), "act")
            mkey(("cb", p), "dve")
        if G:
            gkey(("xs", g, 1), "dve")
        if S:
            mkey(("row", p, 0, 0), "dve")
            mkey(("row", p, 0, 1), "dve")
        if G:
            gkey(("b", g), "dve")
        if g == 0:
            mkey(("tk", 0), "dve")
            mkey(("tk", 1), "dve")
            mkey(("cd",), "dve")
        if S:
            mkey(("st", p, 0), "dve")
            mkey(("st", p, 1), "dve")
            mkey(("row", p, 1, 0), "dve")
            mkey(("row", p, 1, 1), "dve")
        if G:
            gkey(("c", g), "dve")
        if Q:
            mkey(("yt", q), "act")
        if S:
            mkey(("off", p, 0), "dve")
            mkey(("off", p, 1), "dve")
        if G:
            gkey(("z", g), "act")
        if S:
            plan.add(("dg", p), 7, "dve")
    for m in range(KT):
        plan.add(("y", 1, m), m % 3, "act")
    plan.add(("ss", 1, 0), 7, "act")
    plan.add(("ss2", 1, 0), 7, "act")
    plan_ffn(1)
    for half in range(2):
        for t in range(2):
            plan.add(("out", t, half), 2 * t + half, ("act", "dve")[half])

    slabs = []

    def slab(key, n, parts, last):
        slabs.append((key, n, parts, last))

    def cols(w, kts, c0, n):
        return w[kts[0] * P:kts[1] * P, c0:c0 + n].rearrange("(k p) c -> p k c", p=P)

    def pair(key, w, c0, c1, last):
        slab(key, 2048, [(lambda r: r.rearrange("p (k c) -> p k c", c=256)[:, :, 0:128], cols(w, (0, KT), c0, 128)),
                         (lambda r: r.rearrange("p (k c) -> p k c", c=256)[:, :, 128:256], cols(w, (0, KT), c1, 128))], last)

    def wide(key, w, c0, last, k0=0):
        slab(key, 2048, [(lambda r: r.rearrange("p (k c) -> p k c", c=256)[:, 0:4, :], cols(w, (k0, k0 + 4), c0, 256)),
                         (lambda r: r.rearrange("p (k c) -> p k c", c=256)[:, 4:8, :], cols(w, (k0 + 4, k0 + 8), c0, 256))], last)

    w_in = a["hg_w_in"][0]
    for h in range(HEADS):
        c = h * P
        slab(("V", h), 1024, [(lambda r: r[:, 0:1024].rearrange("p (k c) -> p k c", c=128)[:, 0:4, :], cols(w_in, (0, 4), D + c, P)),
                              (lambda r: r[:, 0:1024].rearrange("p (k c) -> p k c", c=128)[:, 4:8, :], cols(w_in, (4, 8), D + c, P))], ("v", h))
        pair(("GQ", h), w_in, 4 * D + c, c, ("q", h))
        pair(("F", h), w_in, 2 * D + c, 3 * D + c, ("f", h, 1))
    for i in range(4):
        wide(("O", i), a["hg_w_out"][0], 256 * i, ("y", 0, 2 * i + 1))
    slab0 = {}

    def plan_ffn_slabs(l):
        for half in range(2):
            slab0[l, half, "up"] = len(slabs)
            slabs.extend([None] * FH[half])
            slab0[l, half, "down"] = len(slabs)
            slabs.extend([(None, FH[half] * P, None, ("fy", l, m) if half else None) for m in range(KT)])

    plan_ffn_slabs(0)
    m_in = a["mb_w_in"][0]
    MB0 = len(slabs)
    XS0, B0 = MB_INNER, 2 * MB_INNER
    C0, DT0 = B0 + MB_GROUPS * P, B0 + 2 * MB_GROUPS * P
    v = lambda r, k0: r[:, 0:512].rearrange("p (k c) -> p k c", c=64)[:, k0:k0 + 4, :]
    slab(("DT",), 512, [(lambda r, v=v: v(r, 0), cols(m_in, (0, 4), DT0, 64)), (lambda r, v=v: v(r, 4), cols(m_in, (4, 8), DT0, 64))],
         ("dt",))
    for g in range(MB_GROUPS):
        wide(("XS", g), m_in, XS0 + 256 * g, ("xs", g, 1))
        pair(("BC", g), m_in, B0 + P * g, C0 + P * g, ("c", g))
        wide(("Z", g), m_in, 256 * g, ("z", g))
    for m in range(KT):
        v = lambda r, k0: r.rearrange("p (k c) -> p k c", c=P)[:, k0:k0 + 8, :]
        slab(("M", m), 2048, [(lambda r, v=v: v(r, 0), cols(a["mb_w_out"][0], (0, 8), P * m, P)),
                              (lambda r, v=v: v(r, 8), cols(a["mb_w_out"][0], (8, 16), P * m, P))], ("y", 1, m))
    OM0 = len(slabs) - KT
    plan_ffn_slabs(1)

    w_landed = [sem("w_landed0"), sem("w_landed1")]
    w_hi, w_lo, w_lo_pool = sem("w_hi"), sem("w_lo"), sem("w_lo_pool")
    w_hi_pool = sem("w_hi_pool")
    a_landed = [sem("a_landed0"), sem("a_landed1")]
    a_used = sem("a_used")
    mbs_landed = sem("mbs_landed")
    x_landed, p_landed, stored = sem("x_landed"), sem("p_landed"), sem("stored")
    consts = sem("consts")
    silu_c, lb_step = sem("silu_c"), sem("lb_step")
    sq_ready, sq_used, sq_added = sem("sq_ready"), sem("sq_used"), sem("sq_added")
    rstd_ready = sem("rstd_ready")
    x_new = sem("x_new")
    hf_ready, hh_ready, hl_ready = sem("hf_ready"), sem("hh_ready"), sem("hl_ready")
    yl_ready, odd_ready = sem("yl_ready"), sem("odd_ready")
    eg_ready, eg_clamped, sg_ready = sem("eg_ready"), sem("eg_clamped"), sem("sg_ready")
    e_clamped, sig_ready, logf_ready = sem("e_clamped"), sem("sig_ready"), sem("logf_ready")
    d_ready, en_ready = sem("d_ready"), sem("en_ready")
    qk_ready, qin_ready = sem("qk_ready"), sem("qin_ready")
    intra_done, inter_done = sem("intra_done"), sem("inter_done")
    osq_ready, oms_ready, or_ready = sem("osq_ready"), sem("oms_ready"), sem("or_ready")
    on_ready = sem("on_ready")
    conv_start, silu_done = sem("conv_start"), sem("silu_done")
    fh_ready, fl_ready, tap_done = sem("fh_ready"), sem("fl_ready"), sem("tap_done")
    centre_ready, conv_silu = sem("centre_ready"), sem("conv_silu")
    dt_act, dt_dve = sem("dt_act"), sem("dt_dve")
    tri_ready, scaled_ready = sem("tri_ready"), sem("scaled_ready")
    decay_ready, w_ready, hs_ready = sem("decay_ready"), sem("w_ready"), sem("hs_ready")
    off_done, seg_ready = sem("off_done"), sem("seg_ready")
    yg_ready, ygsq_ready, ygms_ready, ygr_ready, yn_ready = sem("yg_ready"), sem("ygsq_ready"), sem("ygms_ready"), sem("ygr_ready"), sem("yn_ready")
    rows_act, rows_dve = sem("rows_act"), sem("rows_dve")
    act_step, dve_step, pool_step = sem("act_step"), sem("dve_step"), sem("pool_step")

    pgroups = [("c", a["c"].rearrange("b (n q) -> (b n) q", q=P)),
               ("c_ctx", a["c_ctx"].rearrange("(n q) -> n q", q=P)),
               ("ada_b", a["ada_b"].rearrange("l (n q) -> (l n) q", q=P)),
               ("pre", a["pre_norm"].rearrange("l s (n q) -> (l s n) q", q=P)),
               ("post", a["post_norm"].rearrange("l s (n q) -> (l s n) q", q=P)),
               ("hg_norm", a["hg_norm"].rearrange("l (n q) -> (l n) q", q=P)),
               ("lb", a["hg_lb_logits"].rearrange("d i (n q) -> (d i n) q", q=P)),
               ("mb_cw", a["mb_conv_w"].rearrange("l t (n q) -> (l t n) q", q=P)),
               ("mb_cb", a["mb_conv_b"].rearrange("l (n q) -> (l n) q", q=P)),
               ("mb_norm", a["mb_norm"].rearrange("l (n q) -> (l n) q", q=P)),
               ("ff_cb", a["ffn_conv_b"].rearrange("l (n q) -> (l n) q", q=P)),
               ("ff_cw", a["ffn_conv_w"].rearrange("l i j (n q) -> (l i j n) q", q=P))]
    pdma = []
    for name, src in pgroups:
        r, n, done = PROWS[name], src.shape[0], 0
        while done < n:
            k = min(n - done, P - (r + done) % P)
            pdma.append(((r + done) // P, (r + done) % P, k, src[done:done + k, :]))
            done += k

    def prm(name, i, n=1):
        r = PROWS[name] + i
        return pv[:, r:r + n]

    block = ctx.enter_context(nc.Block())

    @block.sync
    def _(sp):
        def load_params():
            for slot, r, k, src in pdma:
                sp.dma_start(prow[r:r + k, slot, :], src).then_inc(p_landed, 16)
            for i, name in enumerate(("mb_dt_bias", "mb_a_log")):
                sp.dma_start(mbs[:, i:i + 1], a[name].rearrange("l d (h o) -> (l d h) o", o=1)).then_inc(mbs_landed, 16)
            for d in range(2):
                sp.dma_start(mbs[32 * d:32 * d + 32, 2:3], a["mb_d"].rearrange("l (h o) -> (l h) o", o=1)).then_inc(mbs_landed, 16)

        def load_slab(i):
            key, n, parts, last = slabs[i]
            if i >= 2:
                sp.wait_ge(w_lo, i - 1)
            for view, src in parts:
                sp.dma_start(view(wraw[:, i % 2, :]), src).then_inc(w_landed[i % 2], 16)

        def load_ada(n):
            l, c = n // 12, 512 * (n % 12)
            for half in range(2):
                if n >= 1:
                    if half == 0:
                        sp.wait_ge(a_used, n)
                    else:
                        plan.wait_ready(sp, ("am", n - 1))
                sp.dma_start(araw[:, half, :, :],
                             a["ada_w"][l][half * 512:half * 512 + 512, c:c + 512].rearrange("(k p) c -> p k c", p=P))\
                    .then_inc(a_landed[half], 16)

        load_params()
        for n in range(ADA_FIRST):
            load_ada(n)
        load_slab(0)
        load_slab(1)
        for h in range(HEADS):
            for n in range(3):
                load_slab(3 * h + n + 2)
                if n < ada_of[h]:
                    load_ada(ada_start[h] + n)
        for i in range(3 * HEADS + 2, 3 * HEADS + 4):
            load_slab(i)

        def raw(i):
            return wraw[:, i % 2, :]

        def load_ffn(l):
            for half in range(2):
                nf, f0 = FH[half], half * FH[0]
                s0 = slab0[l, half, "up"]
                with sp.Fori(0, nf // 2) as i:
                    for u in range(2):
                        sp.wait_ge(w_lo, i * 2 + (s0 + u - 1))
                        for part in range(2):
                            c = i * (2 * P) + ((f0 + u) * P + part * FF)
                            sp.dma_start(raw(s0 + u).rearrange("p (k c) -> p k c", c=256)[:, :, part * P:(part + 1) * P],
                                         a["ffn_w_up"][l][:, bass.ds(c, P)].rearrange("(k p) c -> p k c", p=P))\
                                .then_inc(w_landed[(s0 + u) % 2], 16)
                s0 = slab0[l, half, "down"]
                with sp.Fori(0, KT // 2) as i:
                    for u in range(2):
                        sp.wait_ge(w_lo, i * 2 + (s0 + u - 1))
                        for part in range(2):
                            k0, n = part * nf // 2, nf // 2
                            r = (f0 + k0) * P
                            sp.dma_start(raw(s0 + u)[:, k0 * P:(k0 + n) * P].rearrange("p (k c) -> p k c", c=P),
                                         a["ffn_w_down"][l][r:r + n * P, bass.ds(i * (2 * P) + u * P, P)]
                                         .rearrange("(k p) c -> p k c", p=P)).then_inc(w_landed[(s0 + u) % 2], 16)

        load_ffn(0)
        for i in range(MB0, OM0 + KT):
            load_slab(i)
        load_ffn(1)
        for t in range(2):
            sp.wait_ge(rows_act, t + 1)
            sp.wait_ge(rows_dve, t + 1)
            sp.dma_start(out[0, t * P:(t + 1) * P, :], rows_out[:, t, :]).then_inc(stored, 16)
        sp.wait_ge(stored, 32)

    @block.gpsimd
    def _(pool):
        step = Steps(pool, pool_step)
        pool.memset(ones[:, :], 1.0)
        step(pool.memset(ident[:, :], 0.0))
        pool.memset(eps[:, :], EPS)
        pool.memset(scc[:, :, 2:32], 0.0)
        pool.memset(maskf[:, :, :], 1.0)
        pool.memset(keep[:, :, :], 1.0)
        for d in range(2):
            pool.memset(attm[d][:, :, :], 0.0)
        step(pool.memset(vm[:, :, :, :, :], 0.0))
        step.wait()
        pool.affine_select(out=ident[:, :], in_=ident[:, :], compare_op=ALU.not_equal, fill=1.0, base=0,
                           pattern=[[-1, P]], channel_multiplier=1)
        step(pool.memset(keep[:, :, 0:1], 0.0))
        v = maskf[:, :, :].rearrange("p d (c j) -> p d c j", j=CH)
        step(pool.affine_select(out=v, in_=v, compare_op=ALU.is_ge, fill=0.0, base=0,
                                pattern=[[0, 2], [-CH, 4], [0, CH]], channel_multiplier=1))
        step.wait()
        step(pool.affine_select(out=v, in_=v, compare_op=ALU.is_ge, fill=0.0, base=CH - 1,
                                pattern=[[0, 2], [CH, 4], [0, CH]], channel_multiplier=-1))
        step.wait()
        step(pool.affine_select(out=maskf[:, 0, :], in_=maskf[:, 0, :], compare_op=ALU.is_ge, fill=0.0, base=0,
                                pattern=[[1, P]], channel_multiplier=-1))
        step(pool.affine_select(out=maskf[:, 1, :], in_=maskf[:, 1, :], compare_op=ALU.is_ge, fill=0.0, base=0,
                                pattern=[[-1, P]], channel_multiplier=1))
        step.wait()
        pool.tensor_copy(mask[:, :, :], maskf[:, :, :]).then_inc(consts, 1)

        def part(l, s, i, lo, hi):
            pool.wait_ge(w_hi_pool, i * 2 + (l * (2 * KT + FT) + s - slab0[l, 0, "up"] + 1))
            pool.tensor_tensor(wl[:, s % 2, lo:hi], wraw[:, s % 2, lo:hi], wh[:, s % 2, lo:hi].bitcast(F32),
                               ALU.subtract).then_inc(w_lo_pool, 1)

        def split_rest(l, w):
            for half in range(2):
                nf, t0 = FH[half], l * FT + half * FH[0]
                s0, hi = slab0[l, half, "up"], FH[half] * P

                def tile(i, c, first=False, last=False, slab=None):
                    slab = c + 1 if slab is None else slab
                    if slab:
                        part(l, s0 + slab, i, DVE_LO, hi if last else 2048)
                    if not first:
                        low(i, c - 1)

                def low(i, c):
                    pool.wait_ge(fh_ready, i * 2 + (t0 + c + 1))
                    pool.tensor_tensor(fl[:, bass.ds(i * 2 + c, 1), 0:w], prod[:, c % 2, 0:w].unsqueeze(1),
                                       fh[:, bass.ds(i * 2 + c, 1), 0:w].bitcast(F32), ALU.subtract).then_inc(fl_ready, 1)

                if half == 0:
                    part(l, s0 + 1, 0, DVE_LO, 2048)
                    tile(0, 0, first=True, slab=2)
                    tile(0, 1, slab=0)
                    tile(0, 2)
                    with pool.Fori(0, nf // 2 - 2) as i:
                        tile(i, 3)
                        tile(i, 4)
                else:
                    tile(0, 0, first=True)
                    with pool.Fori(0, nf // 2 - 1) as i:
                        tile(i, 1)
                        tile(i, 2)
                tile(0, nf - 1, last=True)
                low(0, nf - 1)
                s0 = slab0[l, half, "down"]
                if half == 0:
                    with pool.Fori(0, KT // 2 - 1) as i:
                        part(l, s0 + 1, i, DVE_LO, hi)
                        part(l, s0 + 2, i, DVE_LO, hi)
                    part(l, s0 + KT - 1, 0, DVE_LO, hi)
                    part(l, s0 + KT, 0, DVE_LO, 2048)
                else:
                    for m in range(KT):
                        if m < KT - 1:
                            part(l, s0 + m + 1, 0, DVE_LO, hi)
                        add_square(2 * l + 1, m, w)

        def y_low(n):
            for k in range(KT):
                pool.wait_ge(hh_ready, (2 * n + 1) * KT + n * KT + k + 1)
                pool.tensor_tensor(hl[:, k, :], yT[:, k, :], hh[:, k, :].bitcast(F32), ALU.subtract).then_inc(yl_ready, 1)

        def add_square(n, m, w):
            if 1 <= m < KT - 1:
                pool.wait_ge(sq_ready, KT * (2 * n + 1) + m + 1)
                if m > 1:
                    pool.wait_ge(sq_added, (KT - 2) * n + m - 1)
                pool.tensor_tensor(sq[:, m % 2, 0:w], sq[:, m % 2, 0:w], sq[:, 1 - m % 2, 0:w], ALU.add).then_inc(sq_added, 1)

        def scale_odd(n, w):
            pool.wait_ge(rstd_ready, 2 * n + 2)
            for m in range(1, KT, 2):
                if m >= 2:
                    pool.wait_ge(x_new, KT * n + m - 1)
                pool.tensor_tensor(tmp[:, 1, 0:w], yT[:, m, 0:w], rstd[:, 0:w], ALU.mult).then_inc(odd_ready, 1)

        for i in range(2):
            n = slabs[i][1]
            pool.wait_ge(w_hi, i + 1)
            pool.tensor_tensor(wl[:, i, 0:n], wraw[:, i, 0:n], wh[:, i, 0:n].bitcast(F32), ALU.subtract).then_inc(w_lo, 1)
        y_low(0)
        for m in range(KT):
            add_square(0, m, T)
        part(0, slab0[0, 0, "up"], 0, DVE_LO, 2048)
        scale_odd(0, T)
        split_rest(0, T)
        scale_odd(1, T)
        pool.wait_ge(x_new, KT + 1)
        step(pool.memset(tri[:, :, :], 1.0))
        step.wait()
        pool.affine_select(out=tri[:, 0, :], in_=tri[:, 0, :], compare_op=ALU.is_ge, fill=0.0, base=0,
                           pattern=[[1, P]], channel_multiplier=-1).then_inc(tri_ready, 1)
        pool.affine_select(out=tri[:, 1, :], in_=tri[:, 1, :], compare_op=ALU.is_ge, fill=0.0, base=0,
                           pattern=[[-1, P]], channel_multiplier=1).then_inc(tri_ready, 1)
        hd = lambda x, n: x.rearrange("p t (j c) -> p t j c", c=HD)
        pool.wait_ge(dt_dve, 5)
        for g in range(MB_GROUPS):
            plan.wait_emptied(pool, ("tx", g, 1))
            if g >= 1:
                plan.wait_ready(pool, ("dg", g - 1))
                pool.wait_ge(off_done, g)
            for d in range(2):
                r = slice(32 * d + 4 * g, 32 * d + 4 * g + 4)
                scale = lambda w, t0, n: w[:, t0:t0 + n, r].unsqueeze(3).to_broadcast([P, n, 4, HD])
                pool.tensor_tensor(hd(wx[d][:, 0:2, :], 2), hd(xtok[:, 2:4, :], 2), scale(wtk, 2, 2), ALU.mult)\
                    .then_inc(scaled_ready, 1)
                pool.tensor_tensor(hd(wx[d][:, 2:3, :], 1), hd(xtok[:, d:d + 1, :], 1), scale(wtk, d, 1), ALU.mult)\
                    .then_inc(scaled_ready, 1)
            for d in range(2):
                r = slice(32 * d + 4 * g, 32 * d + 4 * g + 4)
                pool.tensor_tensor(hd(dx[d][:, :, :], 2), hd(xtok[:, 0:2, :], 2),
                                   dtk[:, 0:2, r].unsqueeze(3).to_broadcast([P, 2, 4, HD]), ALU.mult).then_inc(scaled_ready, 1)
            pool.tensor_tensor(hd(skip[:, :, :], 2), hd(xtok[:, 0:2, :], 2),
                               bc[:, 64 + 4 * g:68 + 4 * g].unsqueeze(1).unsqueeze(3).to_broadcast([P, 2, 4, HD]), ALU.mult)\
                .then_inc(scaled_ready, 1)
        y_low(1)
        for m in range(KT):
            add_square(2, m, SEQ)
        part(1, slab0[1, 0, "up"], 0, DVE_LO, 2048)
        scale_odd(2, SEQ)
        split_rest(1, SEQ)
        scale_odd(3, SEQ)

    @block.scalar
    def _(act):
        step = Steps(act, act_step)
        sqx, sqy = [0], [0]

        def split_hi(i):
            n = slabs[i][1]
            act.wait_ge(w_landed[i % 2], 32 * (i // 2 + 1))
            if i >= 2:
                plan.wait_ready(act, slabs[i - 2][3])
            act.activation(wh[:, i % 2, 0:n], wraw[:, i % 2, 0:n], ACT.Copy).then_inc(w_hi, 1)

        def split_hi_next(s, i, ready, n=2048):
            act.wait_ge(w_landed[s % 2], i * 32 + 32 * (s // 2 + 1))
            act.wait_ge(psum_ready, ready)
            act.activation(wh[:, s % 2, DVE_LO:n], wraw[:, s % 2, DVE_LO:n], ACT.Copy).then_inc(w_hi_pool, 1)
            act.activation(wh[:, s % 2, 0:DVE_LO], wraw[:, s % 2, 0:DVE_LO], ACT.Copy).then_inc(w_hi, 1)

        def square(m, src, n, y=False):
            if m >= 2:
                user, norms = (sq_added, sqy) if y else (sq_used, sqx)
                act.wait_ge(user, norms[0] * (KT - 2 if y else KT - 1) + m - 1)
            act.activation(sq[:, m % 2, 0:n], src, ACT.Square).then_inc(sq_ready, 1)
            if m == KT - 1:
                (sqy if y else sqx)[0] += 1

        def squares(n=T):
            for m in range(KT):
                xs[0] += 1
                act.wait_ge(x_new, xs[0])
                square(m, xT[:, m, 0:n], n)

        xs, hf = [0], [0]

        def rsqrt(key, n, dim, dst=None, signal=None):
            dst = rstd if dst is None else dst
            plan.wait_ready(act, key)
            ins = act.activation(dst[:, 0:n], bank[plan.bank(key)][:, 0:n], ACT.Ln, scale=1.0 / dim, bias=eps[:, 0:1])
            plan.empty(ins, "act", key)
            plan.wait_emptied(act, key)
            act.activation(dst[:, 0:n], dst[:, 0:n], ACT.Exp, scale=-0.5).then_inc(signal or rstd_ready, 1)

        def h_high(n=T):
            for m in range(KT):
                hf[0] += 1
                act.wait_ge(hf_ready, hf[0])
                act.activation(hh[:, m, 0:n], tmp[:, m % 2, 0:n], ACT.Copy).then_inc(hh_ready, 1)

        def ada_rows(n):
            key = ("am", n)
            plan.wait_ready(act, key)
            plan.empty(act.activation(asum[:, :], bank[plan.bank(key)][:, :], ACT.Copy), "act", key)

        def ada_slot(h, slot):
            if slot < ada_of[h]:
                ada_rows(ada_start[h] + slot)

        def exp_ln_tables():
            act.preload_act_table_set("natural_log_exp_and_others")

        def silu_table():
            act.preload_act_table_set("silu_and_others")

        act.dma_start(xrow[:, 0:2, :], a["x"][0].rearrange("(t p) c -> p t c", p=P)).then_inc(x_landed, 16)
        act.dma_start(xrow[:, 2:4, :], a["ctx"][0].rearrange("(t p) c -> p t c", p=P)).then_inc(x_landed, 16)
        exp_ln_tables()
        plan.wait_emptied(act, ("pv", 0))
        cc = pv[:, 0:16].rearrange("p (b k) -> p k b", b=2)
        act.activation(scc[:, :, 0:2], cc, ACT.Exp, scale=-1.0).then_inc(silu_c, 1)
        act.wait_ge(silu_c, 2)
        step(act.activation(scc[:, :, 0:2], scc[:, :, 0:2], ACT.Ln, bias=1.0))
        step.wait()
        act.activation(scc[:, :, 0:2], scc[:, :, 0:2], ACT.Exp, scale=-1.0).then_inc(silu_c, 1)
        act.wait_ge(lb_step, 1)
        act.activation(lbt[:, 0:2, :, :], lbt[:, 0:2, :, :], ACT.Exp).then_inc(lb_step, 1)
        for k in range(1, KT, 2):
            plan.wait_ready(act, ("xt", k))
            plan.empty(act.activation(xT[:, k, :], bank[plan.bank(("xt", k))][:, :], ACT.Copy), "act", ("xt", k))
        for n in range(ADA_FIRST):
            if n == SUM_AT:
                for k in range(KT):
                    plan.wait_emptied(act, ("xt", k))
                    square(k, xT[:, k, :], T)
                act.wait_ge(consts, 1)
                rsqrt(("ss", "pre", 0, 0), T, D)
            ada_rows(n)
        split_hi(0)
        split_hi(1)
        h_high()

        def gate_exps(h, d):
            n = 2 * h + d
            A, B, C = gA[d], gB[d], gC[d]
            plan.wait_ready(act, ("f", h, d))
            if h >= 1:
                plan.wait_ready(act, ("ke", h - 1, d))
                act.wait_ge(qin_ready, n - 1)
            ins = act.activation(A[:, :], bank[plan.bank(("f", h, d))][:, :], ACT.Exp, scale=-1.0)
            plan.empty(ins, "act", ("f", h, d))
            act.wait_ge(e_clamped, n + 1)
            step(act.activation(A[:, :], A[:, :], ACT.Ln, bias=1.0))
            step.wait()
            act.activation(A[:, :], A[:, :], ACT.Exp, scale=-1.0).then_inc(sig_ready, 1)
            act.wait_ge(sig_ready, n + 1)
            act.activation(B[:, :], A[:, :], ACT.Ln, scale=omlb[:, 0, d, h:h + 1], bias=lb[:, d, h:h + 1])\
                .then_inc(logf_ready, 1)
            if d == 1:
                split_hi(3 * h + 4)
            act.wait_ge(d_ready, n + 1)
            act.activation(C[:, :], B[:, :], ACT.Exp)
            act.activation(A[:, :], B[:, :], ACT.Exp, scale=-1.0)
            s = sm[:, h % 2, d, :, :]
            act.activation(s, s, ACT.Exp).then_inc(en_ready, 1)

        def value_columns(h):
            key = ("v", h)
            plan.wait_ready(act, key)
            if h >= 1:
                plan.wait_ready(act, ("vt", h - 1))
            plan.empty(act.activation(sq[:, 1, :], bank[plan.bank(key)][:, :], ACT.Copy), "act", key)

        def value_rows(h):
            key = ("vt", h)
            plan.wait_ready(act, key)
            src = bank[plan.bank(key)][:, :].rearrange("p (t v) -> p t v", t=4)
            if h >= 2:
                act.wait_ge(intra_done, 2 * (h - 2) + 2)
                plan.wait_ready(act, ("kv", h - 2, 1, 3))
            act.activation(vtok[:, h % 2, :, :], src, ACT.Copy)
            for c in range(4):
                r = slice(c * CH, (c + 1) * CH)
                ins = act.activation(vm[r, h % 2, :, c, :], src[r, :, :], ACT.Copy)
            plan.empty(ins, "act", key)

        def ke_rows(h, d):
            plan.wait_ready(act, ("ke", h, d))
            if h >= 1:
                plan.wait_ready(act, ("kv", h - 1, d, 3))
            src = bank[plan.bank(("ke", h, d))][:, :].rearrange("p (t k) -> p t k", t=4)
            plan.empty(act.activation(ket[d][:, :, :], src, ACT.Copy), "act", ("ke", h, d))

        def y_high(ks, key):
            for k in ks:
                plan.wait_emptied(act, (key, k))
                act.activation(hh[:, k, :], yT[:, k, :], ACT.Copy).then_inc(hh_ready, 1)

        for h in range(HEADS + 2):
            p = h - 1
            G, S = h < HEADS, 0 <= p < HEADS
            if h == HEADS + 1:
                y_high((KT - 2,), "ot")
            if G:
                value_columns(h)
            if p >= 1:
                act.wait_ge(inter_done, 2 * (p - 1) + 2)
                if p >= 2:
                    act.wait_ge(oms_ready, p - 1)
                act.activation(sq[:, 0, :], bank[7][:, :], ACT.Square).then_inc(osq_ready, 1)
            if S:
                ke_rows(p, 0)
            if h == HEADS:
                y_high(range(KT - 2), "ot")
            if p >= 1:
                act.wait_ge(oms_ready, p)
                if p >= 2:
                    act.wait_ge(on_ready, p - 1)
                step(act.activation(osm[:, 1, :], osm[:, 0, :], ACT.Ln, scale=1.0 / P, bias=eps[:, 0:1]))
                step.wait()
                act.activation(osm[:, 1, :], osm[:, 1, :], ACT.Exp, scale=-0.5).then_inc(or_ready, 1)
            if G:
                plan.wait_ready(act, ("g", h))
                if h >= 3:
                    plan.wait_emptied(act, ("ot", h - 3))
                g = gs[:, h % 3, :]
                act.activation(g, bank[plan.bank(("g", h))][:, :], ACT.Exp, scale=-1.0).then_inc(eg_ready, 1)
                act.wait_ge(eg_clamped, h + 1)
                step(act.activation(g, g, ACT.Ln, bias=1.0))
                step.wait()
                act.activation(g, g, ACT.Exp, scale=-1.0).then_inc(sg_ready, 1)
                value_rows(h)
                split_hi(3 * h + 2)
                ada_slot(h, 0)
                plan.wait_ready(act, ("q", h))
                if h >= 1:
                    act.wait_ge(qin_ready, 2 * h)
                plan.empty(act.activation(qt, bank[plan.bank(("q", h))][:, :], ACT.Copy), "act", ("q", h))
                ada_slot(h, 1)
            if S:
                ke_rows(p, 1)
            if G:
                gate_exps(h, 0)
                split_hi(3 * h + 3)
                ada_slot(h, 2)
                gate_exps(h, 1)
        y_high((KT - 1,), "ot")
        for m in range(KT):
            if m in (2, 4):
                split_hi(3 * HEADS + m // 2 + 1)
            key = ("y", 0, m)
            plan.wait_ready(act, key)
            if m == KT - 2:
                split_hi_next(slab0[0, 0, "up"], 0, plan.index[("y", 0, 5)][0])
            plan.empty(act.activation(yT[:, m, :], bank[plan.bank(key)][:, :], ACT.Copy), "act", key)
            plan.wait_emptied(act, key)
            square(m, yT[:, m, :], T, y=True)

        def ffn_act(l, n, last_split):
            silu_table()
            for half in range(2):
                nf = FH[half]
                s0 = slab0[l, half, "up"]
                r0, reads = ffp[l, half, "up"]
                v0 = reads["dve"]
                t0 = l * FT + half * FH[0]
                cw, cb = PROWS["ff_cw"] + (9 * l + 4) * FT + half * FH[0], PROWS["ff_cb"] + l * FT + half * FH[0]

                def tile(i, c, first=False, last=False, slab=None):
                    u = c % 2
                    slab = c + 1 if slab is None else slab
                    if slab:
                        split_hi_next(s0 + slab, i, i * 4 + (r0 + 2 * slab - 2), nf * P if last else 2048)
                    if not first:
                        gate(i, c - 1)
                    act.wait_ge(psum_ready, i * 4 + (r0 + 2 * c + 1))
                    act.wait_ge(psum_freed_dve, i * 4 + (v0 + 2 * c - 2))
                    act.activation(conv[:, u, 0:n], bank[2 * u][:, 0:n], ACT.Identity,
                                   scale=pv[:, bass.ds(i * 2 + (cw + c), 1)],
                                   bias=pv[:, bass.ds(i * 2 + (cb + c), 1)]).then_inc(conv_start, 1)
                    if not first:
                        high(i, c - 1)

                def gate(i, c):
                    act.wait_ge(psum_freed_dve, i * 4 + (v0 + 2 * c + 1))
                    act.activation(gated[:, c % 2, 0:n], conv[:, c % 2, 0:n], ACT.Silu).then_inc(silu_done, 1)

                def high(i, c):
                    act.wait_ge(psum_freed_dve, i * 4 + (v0 + 2 * c + 2))
                    act.activation(fh[:, bass.ds(i * 2 + c, 1), 0:n], prod[:, c % 2, 0:n].unsqueeze(1), ACT.Copy).then_inc(fh_ready, 1)

                if half == 0:
                    tile(0, 0, first=True, slab=2)
                    tile(0, 1, slab=0)
                    tile(0, 2)
                    with act.Fori(0, nf // 2 - 2) as i:
                        tile(i, 3)
                        tile(i, 4)
                else:
                    tile(0, 0, first=True)
                    with act.Fori(0, nf // 2 - 1) as i:
                        tile(i, 1)
                        tile(i, 2)
                tile(0, nf - 1, last=True)
                gate(0, nf - 1)
                high(0, nf - 1)
                plan.passed()
                s0 = slab0[l, half, "down"]
                if half == 0:
                    r0, reads = ffp[l, half, "down"]

                    def down_tile(i, c, last=False):
                        split_hi_next(s0 + c + 1, i, i * 2 + (r0 + c), 2048 if last else nf * P)
                        act.wait_ge(psum_ready, i * 2 + (r0 + c + 1))
                        act.activation(yT[:, bass.ds(i * 2 + c, 1), 0:n], bank[4 + c % 2][:, 0:n].unsqueeze(1), ACT.Copy)\
                            .then_inc(plan.freed["act"], 1)

                    with act.Fori(0, KT // 2 - 1) as i:
                        down_tile(i, 0)
                        down_tile(i, 1)
                    down_tile(0, KT - 2)
                    down_tile(0, KT - 1, last=True)
                    plan.passed(by="act", reads=KT)
                else:
                    for m in range(KT):
                        if m < KT - 1:
                            split_hi_next(s0 + m + 1, 0, plan.index[("fy", l, m - 1)][0] if m else r0 + 2 * nf, nf * P)
                        elif last_split is not None:
                            plan.wait_ready(act, ("fy", l, m - 1))
                            last_split()
                        plan.wait_emptied(act, ("fy", l, m))
                        square(m, yT[:, m, 0:n], n, y=True)

        psum_freed_dve = plan.freed["dve"]
        rsqrt(("ss", 0, 0), T, D)
        squares()
        split_hi_next(slab0[0, 0, "up"] + 1, 0, plan.index[("y", 0, KT - 1)][0])
        rsqrt(("ss2", 0, 0), T, D)
        h_high()
        ffn_act(0, T, lambda: split_hi(MB0))
        exp_ln_tables()
        rsqrt(("ss", 0, 1), T, D)
        split_hi(MB0 + 1)
        squares()
        rsqrt(("ss2", 0, 1), T, D)
        h_high()

        def centre(g, i, key, dst, n, tile):
            plan.wait_ready(act, key)
            act.activation(dst, bank[plan.bank(key)][:, 0:n], ACT.Identity, scale=prm("mb_cw", 32 + tile),
                           bias=prm("mb_cb", tile)).then_inc(centre_ready, 1)

        def decays(p, d, i):
            act.wait_ge(seg_ready, 4 * p + 2 * d + i + 1)
            act.activation(wd[d][i][:, :, :, :], wd[d][i][:, :, :, :], ACT.Exp).then_inc(decay_ready, 1)

        def dt_rates():
            act.wait_ge(mbs_landed, 64)
            act.wait_ge(dt_dve, 1)
            act.activation(dtw[:, 1, :], dtw[:, 1, :], ACT.Exp).then_inc(dt_act, 1)
            act.activation(acol[:, 0:1], mbs[:, 1:2], ACT.Exp).then_inc(dt_act, 1)
            act.wait_ge(dt_dve, 2)
            act.activation(dtw[:, 2, :], dtw[:, 2, :], ACT.Ln).then_inc(dt_act, 1)
            act.wait_ge(dt_dve, 3)
            for d in range(2):
                r = slice(32 * d, 32 * d + 32)
                act.activation(acol[r, 1:2], atf[r, P - 1 + d:P + d], ACT.Exp).then_inc(dt_act, 1)

        def dt_exps():
            plan.wait_emptied(act, ("tk", 1))
            act.activation(wtk[:, :, :], wtk[:, :, :], ACT.Exp).then_inc(dt_act, 1)
            act.activation(eik[:, :, :], atk[:, :, :], ACT.Exp).then_inc(dt_act, 1)

        for g in range(MB_GROUPS + 2):
            p, q = g - 1, g - 2
            G, S, Q = g < MB_GROUPS, 0 <= p < MB_GROUPS, q >= 0
            sl = MB0 + 1 + 3 * g
            exp_ln_tables()
            if G:
                split_hi(sl + 1)
            if g == 0:
                dt_rates()
            if S:
                for f in range(2):
                    key = ("tx", p, f)
                    plan.wait_ready(act, key)
                    if p >= 1:
                        act.wait_ge(scaled_ready, 7 * p)
                    plan.empty(act.activation(xtok[:, :, f * P:(f + 1) * P],
                                              bank[plan.bank(key)][:, :].rearrange("p (t c) -> p t c", c=P), ACT.Copy), "act", key)
                key = ("tb", p)
                plan.wait_ready(act, key)
                if p >= 1:
                    plan.wait_ready(act, ("st", p - 1, 1))
                plan.empty(act.activation(btok[:, :, :], bank[plan.bank(key)][:, :].rearrange("p (t c) -> p t c", c=P), ACT.Copy),
                           "act", key)
            if g == MB_GROUPS:
                plan.wait_ready(act, ("z", g - 1))
                y_high(range(1), "yt")
            if g == MB_GROUPS + 1:
                y_high((KT - 2,), "yt")
            if G:
                if S:
                    plan.wait_ready(act, ("tx", p, 0))
                centre(g, 0, ("xs", g, 0), xf[:, 0, :], T, 2 * g)
            if Q:
                act.wait_ge(yg_ready, q + 1)
                act.activation(sq[:, 0, :], yg[:, :], ACT.Square).then_inc(ygsq_ready, 1)
            if G:
                centre(g, 1, ("xs", g, 1), xf[:, 1, :], T, 2 * g + 1)
            if S:
                decays(p, 0, 0)
                decays(p, 0, 1)
            if g == MB_GROUPS:
                split_hi(OM0 + 1)
                y_high(range(1, KT - 2), "yt")
            if Q:
                act.wait_ge(ygms_ready, q + 1)
                step(act.activation(msq[:, 1, :], msq[:, 0, :], ACT.Ln, scale=1.0 / 256, bias=eps[:, 0:1]))
                step.wait()
                act.activation(msq[:, 1, :], msq[:, 1, :], ACT.Exp, scale=-0.5).then_inc(ygr_ready, 1)
            if G:
                split_hi(sl + 2)
                centre(g, 2, ("b", g), bf[:, g % 2, :], T, 16 + g)
            if g == 0:
                dt_exps()
            if S:
                for d in range(2):
                    key = ("st", p, d)
                    plan.wait_ready(act, key)
                    if p >= 1:
                        plan.wait_ready(act, ("off", p - 1, 1))
                    act.activation(hs[:, d, :], bank[plan.bank(key)][:, 0:256], ACT.Copy).then_inc(hs_ready, 1)
                decays(p, 1, 0)
                decays(p, 1, 1)
            if G:
                centre(g, 3, ("c", g), cf[:, g % 2, :], SEQ, 24 + g)
            if Q:
                key = ("yt", q)
                plan.wait_ready(act, key)
                yk = yT[:, :, :].rearrange("p a b -> p (a b)")
                for f in range(2):
                    k = 2 * q + f
                    ins = act.activation(yk[:, k * 256:(k + 1) * 256], bank[plan.bank(key)][:, f * 256:(f + 1) * 256],
                                         ACT.Copy, scale=prm("mb_norm", k))
                plan.empty(ins, "act", key)
            if G:
                silu_table()
                split_hi(sl + 3)
                for key, dst in ((("xs", g, 0), xf[:, 0, :]), (("xs", g, 1), xf[:, 1, :]), (("b", g), bf[:, g % 2, :]),
                                 (("c", g), cf[:, g % 2, :])):
                    plan.wait_emptied(act, key)
                    act.activation(dst, dst, ACT.Silu).then_inc(conv_silu, 1)
                key = ("z", g)
                plan.wait_ready(act, key)
                plan.empty(act.activation(sz[:, g % 2, :, :], bank[plan.bank(key)][:, :].rearrange("p (t c) -> p t c", c=256),
                                          ACT.Silu), "act", key)
        y_high((KT - 1,), "yt")
        for m in range(KT):
            if 1 <= m < KT - 1:
                split_hi(OM0 + m + 1)
            elif m:
                split_hi_next(slab0[1, 0, "up"], 0, plan.index[("y", 1, KT - 2)][0])
            key = ("y", 1, m)
            plan.wait_ready(act, key)
            plan.empty(act.activation(yT[:, m, 0:SEQ], bank[plan.bank(key)][:, 0:SEQ], ACT.Copy), "act", key)
            plan.wait_emptied(act, key)
            square(m, yT[:, m, 0:SEQ], SEQ, y=True)
        rsqrt(("ss", 1, 0), SEQ, D)
        squares(SEQ)
        split_hi_next(slab0[1, 0, "up"] + 1, 0, plan.index[("y", 1, KT - 1)][0])
        rsqrt(("ss2", 1, 0), SEQ, D)
        h_high(SEQ)
        ffn_act(1, SEQ, None)
        exp_ln_tables()
        rsqrt(("ss", 1, 1), SEQ, D)
        for t in range(2):
            key = ("out", t, 0)
            plan.wait_ready(act, key)
            act.activation(rows_out[:, t, 0:512], bank[plan.bank(key)][:, :], ACT.Copy).then_inc(rows_act, 1)

    @block.vector
    def _(dve):
        step = Steps(dve, dve_step)
        V = dve

        def split_lo(i):
            n = slabs[i][1]
            if i == 2:
                dve.wait_ge(w_lo, 2)
            dve.wait_ge(w_hi, i + 1)
            dve.tensor_tensor(wl[:, i % 2, 0:n], wraw[:, i % 2, 0:n], wh[:, i % 2, 0:n].bitcast(F32),
                              ALU.subtract).then_inc(w_lo, 1)

        def split_lo_part(l, s, i, lo, hi, last=True):
            if lo == 0:
                dve.wait_ge(w_hi, i * 2 + (s + 1))
            if last:
                if lo == 0:
                    lo = hi - 512
                    dve.tensor_tensor(wl[:, s % 2, 0:lo], wraw[:, s % 2, 0:lo], wh[:, s % 2, 0:lo].bitcast(F32), ALU.subtract)
                dve.wait_ge(w_lo_pool, i * 2 + (l * (2 * KT + FT) + s - slab0[l, 0, "up"] + 1))
            ins = dve.tensor_tensor(wl[:, s % 2, lo:hi], wraw[:, s % 2, lo:hi], wh[:, s % 2, lo:hi].bitcast(F32), ALU.subtract)
            if last:
                ins.then_inc(w_lo, 1)

        def ada_add(n):
            key = ("at", n)
            plan.wait_ready(dve, key)
            src = bank[plan.bank(key)][:, :].rearrange("p (c j b) -> p c j b", c=4, j=4)[:, :, :, 0:2]
            step.wait()
            plan.empty(V.tensor_reduce(ared[:, :, :], src.rearrange("p c j b -> p c b j"), mybir.AxisListType.X, ALU.add),
                       "dve", key)
            plan.wait_emptied(dve, key)
            dst = mod[:, :, :, :].rearrange("p l j b -> p (l j) b")[:, 4 * n:4 * n + 4, :]
            step(V.tensor_tensor(dst, ared[:, :, :], prm("ada_b", 4 * n, 4).unsqueeze(2).to_broadcast([P, 4, 2]), ALU.add))

        def ada_slot(h, slot):
            if 1 <= slot <= ada_of[h]:
                ada_add(ada_start[h] + slot - 1)

        def norm_scales(l, s):
            w = prm("pre", (2 * l + s) * KT, KT).unsqueeze(2).to_broadcast([P, KT, 2])
            sc = mod[:, l, (3 * s + 1) * KT:(3 * s + 2) * KT, :]
            step(V.tensor_scalar(nsc[:, l, s, :, :], sc, 1.0, None, ALU.add))
            step.wait()
            step(V.tensor_tensor(nsc[:, l, s, :, :], nsc[:, l, s, :, :], w, ALU.mult))

        def gate_scales(l, s):
            w = prm("post", (2 * l + s) * KT, KT).unsqueeze(2).to_broadcast([P, KT, 2])
            step(V.tensor_tensor(gsc[:, l, s, :, :], mod[:, l, (3 * s + 2) * KT:(3 * s + 3) * KT, :], w, ALU.mult))

        def residual(l, s, n=T):
            rn[0] += 1
            dve.wait_ge(rstd_ready, rn[0])
            x0 = xn[0]
            step.wait()
            turned = {}
            for m in range(KT + 1):
                if m < KT and m % 2 == 0:
                    if m >= 2:
                        dve.wait_ge(x_new, x0 + m - 1)
                    turned[m] = step(V.tensor_tensor(tmp[:, m % 2, 0:n], yT[:, m, 0:n], rstd[:, 0:n], ALU.mult))
                if m >= 1:
                    k = m - 1
                    if k % 2:
                        odd[0] += 1
                        dve.wait_ge(odd_ready, odd[0])
                    else:
                        step.wait(turned[k])
                    for b in range(n // SEQ):
                        r = slice(b * SEQ, (b + 1) * SEQ)
                        ins = V.scalar_tensor_tensor(out=xT[:, k, r], in0=tmp[:, k % 2, r], scalar=gsc[:, l, s, k, b:b + 1],
                                                     in1=xT[:, k, r], op0=ALU.mult, op1=ALU.add)
                    ins.then_inc(x_new, 1)
            xn[0] += KT

        xn, rn, odd = [0], [0], [0]

        def modulated(l, s, n=T):
            rn[0] += 1
            dve.wait_ge(rstd_ready, rn[0])
            step.wait()
            base = hfn[0]
            for m in range(KT + 1):
                if m < KT:
                    if m >= 2:
                        dve.wait_ge(hl_ready, base + m - 1)
                    t = tmp[:, m % 2, :]
                    step(V.tensor_tensor(t[:, 0:n], xT[:, m, 0:n], rstd[:, 0:n], ALU.mult))
                    step.wait()
                    for b in range(n // SEQ):
                        r = slice(b * SEQ, (b + 1) * SEQ)
                        ins = V.tensor_scalar(t[:, r], t[:, r], nsc[:, l, s, m, b:b + 1],
                                              mod[:, l, 3 * s * KT + m, b:b + 1], ALU.mult, ALU.add)
                    ins.then_inc(hf_ready, 1)
                if m >= 1:
                    k = m - 1
                    dve.wait_ge(hh_ready, hhn[0] + k + 1)
                    V.tensor_tensor(hl[:, k, 0:n], tmp[:, k % 2, 0:n], hh[:, k, 0:n].bitcast(F32),
                                    ALU.subtract).then_inc(hl_ready, 1)
            hfn[0] += KT
            hhn[0] += KT

        hfn, hhn = [0], [0]
        for s in range(PSLOTS):
            plan.wait_ready(dve, ("pv", s))
            n = min(P, NPROWS - s * P)
            plan.empty(V.tensor_copy(pv[:, s * P:s * P + n], bank[plan.bank(("pv", s))][:, 0:n]), "dve", ("pv", s))
            if s == 0:
                dve.wait_ge(silu_c, 1)
                V.tensor_scalar(scc[:, :, 0:2], scc[:, :, 0:2], CLAMP, None, ALU.min).then_inc(silu_c, 1)
                dve.wait_ge(silu_c, 3)
                cc = pv[:, 0:16].rearrange("p (b k) -> p k b", b=2)
                V.tensor_tensor(scc[:, :, 0:2], scc[:, :, 0:2], cc, ALU.mult).then_inc(silu_c, 1)
        plan.wait_emptied(dve, ("pv", PSLOTS - 1))
        lg = prm("lb", 0, 32).rearrange("p (d i k) -> p d i k", d=2, i=2)
        step(V.tensor_tensor(lbt[:, 2, :, :], lg[:, :, 0, :], lg[:, :, 1, :], ALU.max))
        step.wait()
        step(V.tensor_tensor(lbt[:, 0, :, :], lg[:, :, 0, :], lbt[:, 2, :, :], ALU.subtract))
        V.tensor_tensor(lbt[:, 1, :, :], lg[:, :, 1, :], lbt[:, 2, :, :], ALU.subtract).then_inc(lb_step, 1)
        for k in range(0, KT, 2):
            plan.wait_ready(dve, ("xt", k))
            plan.empty(V.tensor_copy(xT[:, k, :], bank[plan.bank(("xt", k))][:, :]), "dve", ("xt", k))
        dve.wait_ge(lb_step, 2)
        step(V.tensor_tensor(lbt[:, 1, :, :], lbt[:, 0, :, :], lbt[:, 1, :, :], ALU.add))
        step.wait()
        step(V.reciprocal(lbt[:, 1, :, :], lbt[:, 1, :, :]))
        step.wait()
        step(V.tensor_tensor(lb[:, :, :], lbt[:, 0, :, :], lbt[:, 1, :, :], ALU.mult))
        step.wait()
        step(V.tensor_scalar(omlb[:, 0, :, :], lb[:, :, :], -1.0, 1.0, ALU.mult, ALU.add))
        step(V.tensor_scalar(omlb[:, 1, :, :], lb[:, :, :], -1.0, None, ALU.add))
        for n in range(ADA_FIRST):
            ada_add(n)
        step.wait()
        norm_scales(0, 0)
        plan.wait_emptied(dve, ("xt", KT - 1))
        modulated(0, 0)

        def states(h, d, ti):
            key = ("kv", h, d, ti)
            plan.wait_ready(dve, key)
            kv = bank[plan.bank(key)]
            if ti == 0 and h >= 1:
                dve.wait_ge(inter_done, 2 * (h - 1) + d + 1)
            for jj in range(4):
                j = 4 * ti + jj
                c = jj if d == 0 else 3 - jj
                if j == NCH - 1:
                    break
                src = kv[:, c * P:(c + 1) * P]
                if j == 0:
                    ins = V.tensor_copy(st[d][:, 0, :], src)
                else:
                    dec = sm[:, h % 2, d, 2, 4 * TILES[d][ti] + c:4 * TILES[d][ti] + c + 1]
                    step.wait() if jj else plan.wait_emptied(dve, ("kv", h, d, ti - 1))
                    ins = V.scalar_tensor_tensor(out=st[d][:, j, :], in0=st[d][:, j - 1, :], scalar=dec, in1=src,
                                                 op0=ALU.mult, op1=ALU.add)
                if jj < 3 and j < NCH - 2:
                    step(ins)
                else:
                    plan.empty(ins, "dve", key)


        def mask_att(h, d):
            key = ("att", h, d)
            plan.wait_ready(dve, key)
            if h >= 1:
                dve.wait_ge(intra_done, 2 * (h - 1) + d + 1)
            ins = V.copy_predicated(attm[d][:, :, :], mask[:, d, :].unsqueeze(1).to_broadcast([P, 4, P]),
                              bank[plan.bank(key)][:, :].rearrange("p (t s) -> p t s", t=4))
            plan.empty(ins, "dve", key)

        def gate_products(h, d):
            n = 2 * h + d
            A, B, C, Dd = gA[d], gB[d], gC[d], gD[d][h % 2]
            ch = lambda x: x[:, :].rearrange("p (c j) -> p c j", j=CH)
            plan.wait_emptied(dve, ("f", h, d))
            V.tensor_scalar(A[:, :], A[:, :], CLAMP, None, ALU.min).then_inc(e_clamped, 1)
            dve.wait_ge(sig_ready, n + 1)
            if h >= 2:
                dve.wait_ge(inter_done, 2 * (h - 2) + d + 1)
            flat_keep = keep[:, :, :].rearrange("p c j -> p (c j)")
            kk = step(V.tensor_scalar(Dd[:, :], A[:, :], omlb[:, 1, d, h:h + 1], omlb[:, 0, d, h:h + 1], ALU.mult, ALU.add))
            dve.wait_ge(logf_ready, n + 1)
            if d == 0:
                step(V.tensor_tensor_scan(C[:, :], flat_keep[:, 0:T], B[:, :], 0.0, ALU.mult, ALU.add))
            else:
                step(V.tensor_tensor_scan(C[:, ::-1], flat_keep[:, T:0:-1], B[:, ::-1],
                                          0.0, ALU.mult, ALU.add))
            mid, last = (CH // 2 - 1, CH - 1) if d == 0 else (CH // 2, 0)
            s = sm[:, h % 2, d, :, :]
            step.wait()
            V.tensor_copy(s[:, 0, :].unsqueeze(2), ch(C)[:, :, mid:mid + 1])
            V.tensor_copy(s[:, 2, :].unsqueeze(2), ch(C)[:, :, last:last + 1])
            V.tensor_tensor(s[:, 1, :].unsqueeze(2), ch(C)[:, :, last:last + 1], ch(C)[:, :, mid:mid + 1], ALU.subtract)
            V.tensor_tensor(ch(B), ch(C), ch(C)[:, :, mid:mid + 1].to_broadcast([P, NCH, CH]), ALU.subtract).then_inc(d_ready, 1)
            if d == 1:
                split_lo(3 * h + 4)
            dve.wait_ge(en_ready, n + 1)
            plan.wait_emptied(dve, ("q", h))
            V.tensor_tensor(C[:, :], qt, C[:, :], ALU.mult)
            step(V.tensor_tensor(A[:, :], Dd[:, :], A[:, :], ALU.mult))
            step.wait()
            V.tensor_tensor(ch(B), ch(A), s[:, 1, :].unsqueeze(2).to_broadcast([P, NCH, CH]), ALU.mult).then_inc(qk_ready, 1)
            V.tensor_tensor(ch(Dd), ch(C), s[:, 0, :].unsqueeze(2).to_broadcast([P, NCH, CH]), ALU.mult).then_inc(qin_ready, 1)

        for h in range(HEADS + 2):
            p = h - 1
            G, S = h < HEADS, 0 <= p < HEADS
            if S:
                mask_att(p, 0)
            if p >= 1:
                dve.wait_ge(osq_ready, p)
                V.tensor_reduce(osm[:, 0, :], sq[:, 0, :].rearrange("p (t v) -> p t v", t=4), mybir.AxisListType.X,
                                ALU.add).then_inc(oms_ready, 1)
            if G:
                g = gs[:, h % 3, :]
                dve.wait_ge(eg_ready, h + 1)
                V.tensor_scalar(g, g, CLAMP, None, ALU.min).then_inc(eg_clamped, 1)
                dve.wait_ge(sg_ready, h + 1)
                plan.empty(V.tensor_tensor(g, bank[plan.bank(("g", h))][:, :], g, ALU.mult), "dve", ("g", h))
                split_lo(3 * h + 2)
            if p >= 1:
                dve.wait_ge(or_ready, p)
                V.tensor_tensor(tmp[:, 0, :].rearrange("p (t v) -> p t v", t=4),
                                bank[7][:, :].rearrange("p (t v) -> p t v", t=4),
                                osm[:, 1, :].unsqueeze(2).to_broadcast([P, 4, P]), ALU.mult).then_inc(on_ready, 1)
            if S:
                states(p, 0, 0)
                states(p, 0, 1)
            if G:
                ada_slot(h, 1)
            if p >= 1:
                r = p - 1
                key = ("ot", r)
                plan.wait_ready(dve, key)
                ins = V.scalar_tensor_tensor(out=yT[:, r, :], in0=bank[plan.bank(key)][:, :], scalar=prm("hg_norm", r),
                                             in1=gs[:, r % 3, :], op0=ALU.mult, op1=ALU.mult)
                plan.empty(ins, "dve", key)
            if S:
                states(p, 0, 2)
                states(p, 0, 3)
                mask_att(p, 1)
            if G:
                ada_slot(h, 2)
                gate_products(h, 0)
            if S:
                states(p, 1, 0)
                states(p, 1, 1)
            if G:
                split_lo(3 * h + 3)
                ada_slot(h, 3)
            if S:
                states(p, 1, 2)
                states(p, 1, 3)
            if G:
                gate_products(h, 1)
        hhn[0] += KT
        for i in range(2, 4):
            split_lo(3 * HEADS + i)
        split_lo_part(0, slab0[0, 0, "up"], 0, 0, DVE_LO)
        gate_scales(0, 0)
        norm_scales(0, 1)
        gate_scales(0, 1)
        residual(0, 0)
        split_lo_part(0, slab0[0, 0, "up"] + 1, 0, 0, DVE_LO)
        modulated(0, 1)

        def taps(l, n):
            out = []
            for dr in (-1, 0, 1):
                for dc in (-1, 0, 1):
                    if dr or dc:
                        ro = slice(max(0, -dr), 4 - max(0, dr))
                        co = slice(max(0, -dc), 64 - max(0, dc))
                        ri = slice(ro.start + dr, ro.stop + dr)
                        ci = slice(co.start + dc, co.stop + dc)
                        grid = lambda x, r, c: x[:, 0:SEQ].rearrange("p (r c) -> p r c", c=64)[:, r, c]
                        out.append(((dr + 1) * 3 + dc + 1, lambda x, r=ro, c=co: grid(x, r, c), lambda x, r=ri, c=ci: grid(x, r, c)))
            if n > SEQ:
                out.insert(1, (3, lambda x: x[:, SEQ + 1:T], lambda x: x[:, SEQ:T - 1]))
                out.insert(3, (5, lambda x: x[:, SEQ:T - 1], lambda x: x[:, SEQ + 1:T]))
            return out

        ntap = [0]

        def ffn_dve(l, n, last_split):
            tp = taps(l, n)
            for half in range(2):
                nf = FH[half]
                s0 = slab0[l, half, "up"]
                r0, reads = ffp[l, half, "up"]
                v0 = reads["dve"]
                t0 = l * FT + half * FH[0]
                cw = PROWS["ff_cw"] + 9 * l * FT + half * FH[0]
                c0, per = ntap[0], len(tp) - 1

                def tile(i, c, first=False, last=False, slab=None):
                    u = c % 2
                    slab = c + 1 if slab is None else slab
                    if slab:
                        split_lo_part(l, s0 + slab, i, 0, 512, last=False)
                    if not first:
                        product(i, c - 1)
                    dve.wait_ge(conv_start, i * 2 + (t0 + c + 1))
                    for t, (row, o, src) in enumerate(tp):
                        if t:
                            dve.wait_ge(tap_done, i * (2 * per) + (c0 + c * per + t))
                        ins = V.scalar_tensor_tensor(out=o(conv[:, u, :]), in0=src(bank[2 * u]),
                                                     scalar=pv[:, bass.ds(i * 2 + (cw + row * FT + c), 1)],
                                                     in1=o(conv[:, u, :]), op0=ALU.mult, op1=ALU.add)
                        ins.then_inc(tap_done if t < per else psum_freed_dve, 1)
                        if t == 1 and slab:
                            split_lo_part(l, s0 + slab, i, 512, 1024)

                def product(i, c):
                    dve.wait_ge(silu_done, i * 2 + (t0 + c + 1))
                    dve.wait_ge(psum_ready, i * 4 + (r0 + 2 * c + 2))
                    if t0 + c >= 2:
                        dve.wait_ge(fl_ready, i * 2 + (t0 + c - 1))
                    V.tensor_tensor(prod[:, c % 2, 0:n], bank[2 * (c % 2) + 1][:, 0:n], gated[:, c % 2, 0:n], ALU.mult)\
                        .then_inc(psum_freed_dve, 1)

                if half == 0:
                    tile(0, 0, first=True, slab=2)
                    tile(0, 1, slab=0)
                    tile(0, 2)
                    with dve.Fori(0, nf // 2 - 2) as i:
                        tile(i, 3)
                        tile(i, 4)
                else:
                    tile(0, 0, first=True)
                    with dve.Fori(0, nf // 2 - 1) as i:
                        tile(i, 1)
                        tile(i, 2)
                tile(0, nf - 1, last=True)
                product(0, nf - 1)
                ntap[0] += per * nf
                plan.passed(by="dve", reads=2 * nf)
                s0 = slab0[l, half, "down"]
                if half == 0:
                    with dve.Fori(0, KT // 2 - 1) as i:
                        split_lo_part(l, s0 + 1, i, 0, DVE_LO)
                        split_lo_part(l, s0 + 2, i, 0, DVE_LO)
                    split_lo_part(l, s0 + KT - 1, 0, 0, DVE_LO)
                    split_lo_part(l, s0 + KT, 0, 0, DVE_LO)
                else:
                    for m in range(KT):
                        if m < KT - 1:
                            split_lo_part(l, s0 + m + 1, 0, 0, DVE_LO)
                        elif last_split is not None:
                            last_split()
                        key = ("fy", l, m)
                        plan.wait_ready(dve, key)
                        if m == 0:
                            dve.wait_ge(plan.freed["act"], ffp[l, 0, "down"][1]["act"] + KT)
                        plan.empty(V.tensor_tensor(yT[:, m, 0:n], bank[plan.bank(key)][:, 0:n], yT[:, m, 0:n], ALU.add),
                                   "dve", key)

        psum_freed_dve = plan.freed["dve"]
        ffn_dve(0, T, lambda: split_lo(MB0))
        norm_scales(1, 0)
        gate_scales(1, 0)
        norm_scales(1, 1)
        gate_scales(1, 1)
        residual(0, 1)
        split_lo(MB0 + 1)
        modulated(1, 0)

        def dt_rates():
            key = ("dt",)
            plan.wait_ready(dve, key)
            dve.wait_ge(mbs_landed, 64)
            u, e, w = dtw[:, 0, :], dtw[:, 1, :], dtw[:, 2, :]
            plan.empty(V.tensor_scalar(u, bank[plan.bank(key)][0:64, :], mbs[:, 0:1], None, ALU.add), "dve", key)
            plan.wait_emptied(dve, key)
            V.scalar_tensor_tensor(out=e, in0=u, scalar=-1.0, in1=u, op0=ALU.mult, op1=ALU.min).then_inc(dt_dve, 1)
            dve.wait_ge(dt_act, 1)
            step(V.tensor_scalar(w, e, 1.0, None, ALU.add))
            step.wait()
            V.scalar_tensor_tensor(out=e, in0=w, scalar=1.0, in1=e, op0=ALU.subtract, op1=ALU.subtract).then_inc(dt_dve, 1)
            dve.wait_ge(dt_act, 3)
            step(V.tensor_tensor(w, w, e, ALU.subtract))
            step.wait()
            step(V.scalar_tensor_tensor(out=dtf[:, :], in0=u, scalar=0.0, in1=w, op0=ALU.max, op1=ALU.add))
            step.wait()
            step(V.tensor_scalar(e, dtf[:, :], acol[:, 0:1], -1.0, ALU.mult, ALU.mult))
            step.wait()
            ends = []
            for d in range(2):
                r = slice(32 * d, 32 * d + 32)
                for lo, hi in ((0, P), (P, SEQ), (SEQ, T)):
                    c = slice(lo, hi) if d == 0 else slice(hi - 1, lo - 1 if lo else None, -1)
                    ins = V.tensor_tensor_scan(atf[r, c], ones[r, 0:1].to_broadcast([32, hi - lo]), dtw[r, 1, c], 0.0,
                                               ALU.mult, ALU.add)
                    if (d, lo) != (1, SEQ):
                        step(ins)
                    ends.append((r, slice(lo, hi), hi - 1 if d == 0 else lo))
            ins.then_inc(dt_dve, 1)
            dve.wait_ge(dt_dve, 3)
            for r, c, last in ends:
                step(V.tensor_scalar(elf[r, c], atf[r, c], -1.0, atf[r, last:last + 1], ALU.mult, ALU.add))
            V.tensor_copy(identr[:, :], ident[0:64, 0:64])
            step(V.tensor_copy(ath[:, :], atf[:, 0:SEQ]))
            step.wait()
            step(V.tensor_tensor(atl[:, :], atf[:, 0:SEQ], ath[:, :].bitcast(F32), ALU.subtract))
            dve.wait_ge(dt_act, 5)
            step(V.tensor_scalar(dg[:, 0:64], ident[0:64, 0:64], acol[:, 1:2], None, ALU.mult))
            V.tensor_scalar(dg[:, 64:96], ident[0:64, 0:32], mbs[:, 2:3], None, ALU.mult).then_inc(dt_dve, 1)

        def dt_by_token():
            key = ("tk", 0)
            plan.wait_ready(dve, key)
            b = bank[plan.bank(key)][:, :].rearrange("p (i t r) -> p i t r", i=2, r=64)
            V.tensor_copy(dtk[:, :, :], b[:, 0, :, :])
            plan.empty(V.tensor_copy(wtk[:, :, :], b[:, 1, :, :]), "dve", key)
            key = ("tk", 1)
            plan.wait_ready(dve, key)
            plan.empty(V.tensor_copy(atk[:, :, :], bank[plan.bank(key)][:, 0:P].rearrange("p (t r) -> p t r", r=64)), "dve", key)
            key = ("cd",)
            plan.wait_ready(dve, key)
            plan.wait_emptied(dve, ("tk", 1))
            ins = V.tensor_copy(bc[:, :], bank[plan.bank(key)][:, 0:96])
            plan.empty(ins, "dve", key)
            dve.wait_ge(dt_act, 6)
            V.tensor_tensor(wtk[:, :, :], wtk[:, :, :], dtk[:, :, :], ALU.mult).then_inc(dt_dve, 1)

        def conv_taps(g, i, key, dst, n, tile):
            dve.wait_ge(centre_ready, 4 * g + i + 1)
            b, t = n // SEQ, bank[plan.bank(key)][:, 0:n].rearrange("p (b t) -> p b t", t=SEQ)
            o = dst.rearrange("p (b t) -> p b t", t=SEQ)
            step(V.scalar_tensor_tensor(out=o[:, :, 1:SEQ], in0=t[:, :, 0:SEQ - 1], scalar=prm("mb_cw", tile),
                                        in1=o[:, :, 1:SEQ], op0=ALU.mult, op1=ALU.add))
            step.wait()
            plan.empty(V.scalar_tensor_tensor(out=o[:, :, 0:SEQ - 1], in0=t[:, :, 1:SEQ], scalar=prm("mb_cw", 64 + tile),
                                              in1=o[:, :, 0:SEQ - 1], op0=ALU.mult, op1=ALU.add), "dve", key)

        def segments(p, d, i):
            key = ("row", p, d, i)
            plan.wait_ready(dve, key)
            if p >= 1:
                plan.wait_ready(dve, ("dg", p - 1))
            r = 32 * d + 4 * p + 2 * i
            plan.empty(V.tensor_tensor(wd[d][i][:, :, :, :], bank[plan.bank(key)][:, :].rearrange("p (j t l) -> p j t l", j=2, t=2),
                                       atk[:, :, r:r + 2].rearrange("p t j -> p j t").unsqueeze(3).to_broadcast([P, 2, 2, P]),
                                       ALU.subtract), "dve", key)
            plan.wait_emptied(dve, key)
            V.tensor_scalar(wd[d][i][:, :, :, :], wd[d][i][:, :, :, :], 0.0, None, ALU.min).then_inc(seg_ready, 1)

        def weights(p, d, i):
            dve.wait_ge(decay_ready, 4 * p + 2 * d + i + 1)
            V.tensor_tensor(wd[d][i][:, :, :, :], wd[d][i][:, :, :, :],
                            cbm[:, d, :, :].unsqueeze(1).to_broadcast([P, 2, 2, P]), ALU.mult)\
                .then_inc(w_ready, 1)

        heads = lambda x: x.rearrange("p (t j c) -> p t j c", t=2, c=HD)
        for g in range(MB_GROUPS + 2):
            p, q = g - 1, g - 2
            G, S, Q = g < MB_GROUPS, 0 <= p < MB_GROUPS, q >= 0
            sl = MB0 + 1 + 3 * g
            if G:
                split_lo(sl + 1)
            if g == 0:
                dt_rates()
            if Q:
                key = ("dg", q)
                plan.wait_ready(dve, key)
                dve.wait_ge(off_done, q + 1)
                if q >= 1:
                    plan.wait_ready(dve, ("yt", q - 1))
                plan.empty(V.tensor_tensor(yg[:, :], bank[7][:, :], ysum[:, 0, :], ALU.add), "dve", key)
                plan.wait_emptied(dve, key)
                plan.wait_emptied(dve, ("z", q))
                V.tensor_tensor(yg[:, :], yg[:, :], sz[:, q % 2, :, :].rearrange("p t c -> p (t c)"), ALU.mult)\
                    .then_inc(yg_ready, 1)
            if G:
                conv_taps(g, 0, ("xs", g, 0), xf[:, 0, :], T, 2 * g)
            if S:
                key = ("cb", p)
                plan.wait_ready(dve, key)
                if p == 0:
                    dve.wait_ge(tri_ready, 2)
                else:
                    dve.wait_ge(w_ready, 4 * p)
                for d in range(2):
                    ins = V.tensor_tensor(cbm[:, d, :, :], bank[plan.bank(key)][:, 0:256].rearrange("p (t l) -> p t l", t=2),
                                          tri[:, d, :].unsqueeze(1).to_broadcast([P, 2, P]), ALU.mult)
                plan.empty(ins, "dve", key)
            if G:
                conv_taps(g, 1, ("xs", g, 1), xf[:, 1, :], T, 2 * g + 1)
            if S:
                segments(p, 0, 0)
                segments(p, 0, 1)
            if Q:
                dve.wait_ge(ygsq_ready, q + 1)
                V.tensor_reduce(msq[:, 0, :], sq[:, 0, :].rearrange("p (t c) -> p t c", t=2), mybir.AxisListType.X, ALU.add)\
                    .then_inc(ygms_ready, 1)
            if S:
                weights(p, 0, 0)
                weights(p, 0, 1)
            if g == MB_GROUPS:
                split_lo(OM0 + 1)
            if G:
                split_lo(sl + 2)
            if Q:
                dve.wait_ge(ygr_ready, q + 1)
                V.tensor_tensor(yg[:, :].rearrange("p (t c) -> p t c", t=2), yg[:, :].rearrange("p (t c) -> p t c", t=2),
                                msq[:, 1, :].unsqueeze(2).to_broadcast([P, 2, 256]), ALU.mult).then_inc(yn_ready, 1)
            if G:
                conv_taps(g, 2, ("b", g), bf[:, g % 2, :], T, 16 + g)
            if g == 0:
                dt_by_token()
            if S:
                for d in range(2):
                    key = ("st", p, d)
                    dve.wait_ge(hs_ready, 2 * p + d + 1)
                    r = slice(32 * d + 4 * p, 32 * d + 4 * p + 4)
                    step(V.tensor_tensor(h1[:, d, :].rearrange("p (j c) -> p j c", c=HD), hs[:, d, :].rearrange("p (j c) -> p j c", c=HD),
                                         bc[:, r].unsqueeze(2).to_broadcast([P, 4, HD]), ALU.mult))
                    step.wait()
                    plan.empty(V.tensor_tensor(h1[:, d, :], bank[plan.bank(key)][:, 256:512], h1[:, d, :], ALU.add), "dve", key)
                segments(p, 1, 0)
                segments(p, 1, 1)
                weights(p, 1, 0)
                weights(p, 1, 1)
            if G:
                conv_taps(g, 3, ("c", g), cf[:, g % 2, :], SEQ, 24 + g)
                split_lo(sl + 3)
            if S:
                for d in range(2):
                    key = ("off", p, d)
                    plan.wait_ready(dve, key)
                    if p == 0 and d == 0:
                        dve.wait_ge(dt_act, 7)
                    r = slice(32 * d + 4 * p, 32 * d + 4 * p + 4)
                    plan.empty(V.tensor_tensor(heads(ysum[:, d, :]), heads(bank[plan.bank(key)][:, :]),
                                               eik[:, :, r].unsqueeze(3).to_broadcast([P, 2, 4, HD]), ALU.mult), "dve", key)
                plan.wait_emptied(dve, ("off", p, 1))
                step(V.tensor_tensor(ysum[:, 0, :], ysum[:, 0, :], ysum[:, 1, :], ALU.add))
                dve.wait_ge(scaled_ready, 7 * p + 7)
                step.wait()
                V.tensor_tensor(ysum[:, 0, :], ysum[:, 0, :], skip[:, :, :].rearrange("p t c -> p (t c)"), ALU.add)\
                    .then_inc(off_done, 1)
        hhn[0] += KT
        for m in range(1, KT - 1):
            split_lo(OM0 + m + 1)
        split_lo_part(1, slab0[1, 0, "up"], 0, 0, DVE_LO)
        residual(1, 0, SEQ)
        split_lo_part(1, slab0[1, 0, "up"] + 1, 0, 0, DVE_LO)
        modulated(1, 1, SEQ)
        ffn_dve(1, SEQ, None)
        residual(1, 1, SEQ)
        for t in range(2):
            key = ("out", t, 1)
            plan.wait_ready(dve, key)
            V.tensor_copy(rows_out[:, t, 512:1024], bank[plan.bank(key)][:, :]).then_inc(rows_dve, 1)

    @block.tensor
    def _(pe):
        def gemm(dst, w, hi, lo, nk, k0=0, need=None):
            skip = dict(skip_group_check=True) if k0 else {}
            for k in range(k0, nk):
                if need is not None:
                    need(k)
                W, L = w(wh, k), w(wl, k)
                pe.matmul(dst, W, hi(k), start=(k == 0), stop=False, **skip)
                pe.matmul(dst, W, lo(k), start=False, stop=False, **skip)
                ins = pe.matmul(dst, L, hi(k), start=False, stop=(k == nk - 1), **skip)
            return ins

        def by_tile(count, products, n=T):
            hi, lo = act_tiles(n)
            for k in range(KT):
                pe.wait_ge(hl_ready, count + k + 1)
                for dst, w, nk, finish in products:
                    if k >= nk:
                        continue
                    W, L = w(wh, k), w(wl, k)
                    pe.matmul(dst, W, hi(k), start=(k == 0), stop=False, skip_group_check=True)
                    pe.matmul(dst, W, lo(k), start=False, stop=False, skip_group_check=True)
                    ins = pe.matmul(dst, L, hi(k), start=False, stop=(k == KT - 1), skip_group_check=True)
                    if k == KT - 1:
                        finish(ins)

        def act_tiles(n=T):
            return (lambda k: hh[:, k, 0:n]), (lambda k: hl[:, k, 0:n])

        def need_slab(i):
            pe.wait_ge(w_lo, i + 1)

        def wide_w(i, half):
            s = i % 2
            return lambda w, k: w[:, s, k * 256 + half * P:k * 256 + half * P + P]

        def project(key, i, half, n=T, k0=0):
            plan.wait_free(pe, key)
            hi, lo = act_tiles(n)
            plan.done(gemm(bank[plan.bank(key)][:, 0:n], wide_w(i, half), hi, lo, KT, k0), key)

        def square_sum(key, n=T):
            plan.wait_free(pe, key)
            for m in range(KT):
                sqm[0] += 1
                pe.wait_ge(sq_ready, sqm[0])
                ins = pe.matmul(bank[7][:, 0:n], ones[:, :], sq[:, m % 2, 0:n], start=(m == 0), stop=(m == KT - 1))
                if m < KT - 1:
                    ins.then_inc(sq_used, 1)
            plan.done(ins, key)

        sqm = [0]
        pe.wait_ge(consts, 1)
        pe.wait_ge(p_landed, 16 * len(pdma))
        for s in range(PSLOTS):
            key = ("pv", s)
            plan.wait_free(pe, key)
            n = min(P, NPROWS - s * P)
            plan.done(pe.transpose(bank[plan.bank(key)][:, 0:n], prow[0:n, s, :], ident[0:n, 0:n]), key)
        pe.wait_ge(x_landed, 32)
        for k in range(KT):
            key = ("xt", k)
            plan.wait_free(pe, key)
            for t in range(4):
                ins = pe.transpose(bank[plan.bank(key)][:, t * P:(t + 1) * P], xrow[:, t, k * P:(k + 1) * P], ident[:, :])
            plan.done(ins, key)

        def ada_block(n):
            key = ("am", n)
            plan.wait_free(pe, key)
            for half in range(2):
                pe.wait_ge(a_landed[half], 16 * (n + 1))
                for j in range(4):
                    ins = pe.matmul(bank[plan.bank(key)][32 * j:32 * j + 32, :], scc[:, 4 * half + j, :], araw[:, half, j, :],
                                    start=(half == 0), stop=(half == 1))
                if half == 0:
                    ins.then_inc(a_used, 1)
            plan.done(ins, key)

        def ada_turn(n):
            key = ("at", n)
            plan.wait_emptied(pe, ("am", n))
            plan.wait_free(pe, key)
            for c in range(4):
                ins = pe.transpose(bank[plan.bank(key)][:, c * P:(c + 1) * P], asum[:, c * P:(c + 1) * P], ident[:, :])
            plan.done(ins, key)

        def ada_slot(h, slot):
            if 1 <= slot <= ada_of[h]:
                ada_turn(ada_start[h] + slot - 1)
            if slot < ada_of[h]:
                ada_block(ada_start[h] + slot)

        pe.wait_ge(silu_c, 4)
        for n in range(ADA_FIRST):
            if n == SUM_AT:
                square_sum(("ss", "pre", 0, 0))
            ada_block(n)
            ada_turn(n)

        def head_v(h):
            key = ("v", h)
            need_slab(3 * h)
            plan.wait_free(pe, key)
            s = (3 * h) % 2
            hi, lo = act_tiles()
            plan.done(gemm(bank[plan.bank(key)][:, :], lambda w, k: w[:, s, k * P:(k + 1) * P], hi, lo, KT), key)

        def v_turn(h):
            key = ("vt", h)
            plan.wait_emptied(pe, ("v", h))
            plan.wait_free(pe, key)
            for t in range(4):
                r = slice(t * P, (t + 1) * P)
                ins = pe.transpose(bank[plan.bank(key)][:, r], sq[:, 1, r], ident[:, :])
            plan.done(ins, key)

        def att(h, d):
            key = ("att", h, d)
            pe.wait_ge(qk_ready, 2 * h + d + 1)
            plan.wait_free(pe, key)
            for t in range(4):
                r = slice(t * P, (t + 1) * P)
                ins = pe.matmul(bank[plan.bank(key)][:, r], gA[d][:, r], gC[d][:, r], start=True, stop=True)
            plan.done(ins, key)

        def ke(h, d):
            key = ("ke", h, d)
            plan.wait_free(pe, key)
            for t in range(4):
                r = slice(t * P, (t + 1) * P)
                ins = pe.transpose(bank[plan.bank(key)][:, r], gB[d][:, r], ident[:, :])
            plan.done(ins, key)

        def kv(h, d, ti):
            key = ("kv", h, d, ti)
            t = TILES[d][ti]
            plan.wait_emptied(pe, ("ke", h, d))
            plan.wait_free(pe, key)
            plan.done(pe.matmul(bank[plan.bank(key)][:, :], ket[d][:, t, :],
                                vm[:, h % 2, t, :, :].rearrange("p c v -> p (c v)"), start=True, stop=True), key)

        def intra(h, d):
            plan.wait_emptied(pe, ("att", h, d))
            if d == 0 and h >= 1:
                pe.wait_ge(on_ready, h)
            for t in range(4):
                r = slice(t * P, (t + 1) * P)
                ins = pe.matmul(bank[7][:, r], attm[d][:, t, :], vtok[:, h % 2, t, :], start=(d == 0 and t == 0), stop=False,
                                skip_group_check=True)
            ins.then_inc(intra_done, 1)

        def inter(h, d):
            pe.wait_ge(qin_ready, 2 * h + d + 1)
            plan.wait_emptied(pe, ("kv", h, d, 3))
            for j in range(1, NCH):
                t = TILES[d][j // 4]
                c = 4 * t + (j % 4 if d == 0 else 3 - j % 4)
                q = (c % 4) * CH
                ins = pe.matmul(bank[7][q:q + CH, t * P:(t + 1) * P], gD[d][h % 2][:, c * CH:(c + 1) * CH], st[d][:, j - 1, :],
                                start=False, stop=(d == 1 and j == NCH - 1), skip_group_check=True)
            ins.then_inc(inter_done, 1)

        def o_turn(h):
            key = ("ot", h)
            pe.wait_ge(on_ready, h + 1)
            plan.wait_free(pe, key)
            for t in range(4):
                r = slice(t * P, (t + 1) * P)
                ins = pe.transpose(bank[plan.bank(key)][:, r], tmp[:, 0, r], ident[:, :])
            plan.done(ins, key)

        need_slab(0)
        need_slab(1)
        for key in (("v", 0), ("g", 0), ("q", 0)):
            plan.wait_free(pe, key)
        dst = lambda key: bank[plan.bank(key)][:, :]
        by_tile(0, [(dst(("v", 0)), lambda w, k: w[:, 0, k * P:(k + 1) * P], KT, lambda ins: plan.done(ins, ("v", 0))),
                    (dst(("g", 0)), wide_w(1, 0), KT, lambda ins: plan.done(ins, ("g", 0))),
                    (dst(("q", 0)), wide_w(1, 1), KT - 1, None)])

        def early(n, products, ks, hi, lo, tile):
            for k in ks:
                pe.wait_ge(yl_ready, n * KT + k // tile + 1)
                for key, w in products:
                    if k == 0:
                        plan.wait_free(pe, key)
                    d = bank[plan.bank(key)][:, 0:hi(k).shape[-1]]
                    pe.matmul(d, w(wh, k), hi(k), start=(k == 0), stop=False, skip_group_check=True)
                    pe.matmul(d, w(wh, k), lo(k), start=False, stop=False, skip_group_check=True)
                    pe.matmul(d, w(wl, k), hi(k), start=False, stop=False, skip_group_check=True)

        O0 = 3 * HEADS

        def hg_early(*ks):
            need_slab(O0 + 1)
            early(0, [(("y", 0, m), wide_w(O0 + m // 2, m % 2)) for m in range(3)], ks, *act_tiles(), 1)

        for h in range(HEADS + 2):
            p = h - 1
            G, S = h < HEADS, 0 <= p < HEADS
            end = h == HEADS
            if h == HEADS + 1:
                hg_early(5)
            if G and h:
                head_v(h)
            if p >= 1:
                inter(p - 1, 1)
            if S:
                att(p, 0)
                ke(p, 0)
            if end:
                hg_early(0, 1)
            if G:
                if h:
                    need_slab(3 * h + 1)
                    project(("g", h), 3 * h + 1, 0)
                v_turn(h)
                ada_slot(h, 0)
            if S:
                kv(p, 0, 0)
                kv(p, 0, 1)
            if G:
                project(("q", h), 3 * h + 1, 1, k0=0 if h else KT - 1)
                ada_slot(h, 1)
            if p >= 1:
                o_turn(p - 1)
            if S:
                kv(p, 0, 2)
                kv(p, 0, 3)
                att(p, 1)
                ke(p, 1)
                intra(p, 0)
            if end:
                hg_early(2, 3)
            if G:
                need_slab(3 * h + 2)
                project(("f", h, 0), 3 * h + 2, 0)
                ada_slot(h, 2)
            if S:
                kv(p, 1, 0)
                kv(p, 1, 1)
                intra(p, 1)
            if G:
                project(("f", h, 1), 3 * h + 2, 1)
                ada_slot(h, 3)
            if end:
                hg_early(4)
            if S:
                kv(p, 1, 2)
                kv(p, 1, 3)
                inter(p, 0)
        hg_early(6)
        pe.wait_ge(yl_ready, KT)

        def y_square_sum(key, n):
            sqm[0] += KT
            ysums[0] += 1
            plan.wait_free(pe, key)
            pe.wait_ge(sq_added, (KT - 2) * ysums[0])
            pe.matmul(bank[7][:, 0:n], ones[:, :], sq[:, KT % 2, 0:n], start=True, stop=False)
            pe.wait_ge(sq_ready, sqm[0])
            plan.done(pe.matmul(bank[7][:, 0:n], ones[:, :], sq[:, (KT - 1) % 2, 0:n], start=False, stop=True), key)

        ysums = [0]
        for m in range(KT):
            i = 3 * HEADS + m // 2
            need_slab(i)
            project(("y", 0, m), i, m % 2, k0=KT - 1 if m < 3 else 0)
        y_square_sum(("ss", 0, 0), T)
        square_sum(("ss2", 0, 0))

        def ffn_pe(l, n, hl_count):
            psum_freed_dve = plan.freed["dve"]
            hi, lo = act_tiles(n)
            fhi, flo = (lambda k: fh[:, k, 0:n]), (lambda k: fl[:, k, 0:n])
            for half in range(2):
                nf = FH[half]
                s0 = slab0[l, half, "up"]
                r0, reads = ffp[l, half, "up"]
                v0 = reads["dve"]
                pairs, v1 = nf // 2, v0
                if half == 0:
                    need_slab(s0)
                    need_slab(s0 + 1)
                    up = lambda u, part: (bank[2 * u + part][:, 0:n], wide_w(s0 + u, part), KT,
                                          lambda ins: ins.then_inc(psum_ready, 1))
                    by_tile(hl_count - KT, [up(0, 0), up(0, 1), up(1, 0)], n)
                    gemm(bank[3][:, 0:n], wide_w(s0 + 1, 1), hi, lo, KT).then_inc(psum_ready, 1)
                    s0, v1, pairs = s0 + 2, v0 + 4, pairs - 1
                with pe.Fori(0, pairs) as i:
                    for u in range(2):
                        s = s0 + u
                        pe.wait_ge(w_lo, i * 2 + (s + 1))
                        for part in range(2):
                            pe.wait_ge(psum_freed_dve, i * 4 + (v1 + 2 * u - 3 + part))
                            w = lambda w, k, s=s, part=part: w[:, s % 2, k * 256 + part * P:k * 256 + part * P + P]
                            gemm(bank[2 * u + part][:, 0:n], w, hi, lo, KT).then_inc(psum_ready, 1)
                plan.passed(fills=2 * nf)
                s0 = slab0[l, half, "down"]
                r0, reads = ffp[l, 0, "down"]

                def need(k, nf=nf, t0=l * FT + half * FH[0]):
                    if k == 0 or k >= nf - 3:
                        pe.wait_ge(fl_ready, t0 + max(k + 1, nf - 3))

                if half == 0:
                    with pe.Fori(0, KT // 2) as i:
                        for u in range(2):
                            s = s0 + u
                            pe.wait_ge(w_lo, i * 2 + (s + 1))
                            pe.wait_ge(plan.freed["act"], i * 2 + (reads["act"] + u - 1))
                            w = lambda w, k, s=s: w[:, s % 2, k * P:(k + 1) * P]
                            gemm(bank[4 + u][:, 0:n], w, fhi, flo, nf, need=need).then_inc(psum_ready, 1)
                    plan.passed(fills=KT)
                else:
                    for m in range(KT):
                        s = s0 + m
                        pe.wait_ge(w_lo, s + 1)
                        key = ("fy", l, m)
                        if m < 2:
                            pe.wait_ge(plan.freed["act"], reads["act"] + KT)
                        plan.wait_free(pe, key)
                        w = lambda w, k, s=s: w[:, s % 2, k * P:(k + 1) * P]
                        plan.done(gemm(bank[plan.bank(key)][:, 0:n], w, fhi, flo, nf, need=need), key)
                    y_square_sum(("ss", l, 1), n)

        ffn_pe(0, T, 2 * KT)
        square_sum(("ss2", 0, 1))

        need_slab(MB0)
        need_slab(MB0 + 1)
        for key in (("dt",), ("xs", 0, 0), ("xs", 0, 1)):
            plan.wait_free(pe, key)
        s = MB0 % 2
        by_tile(2 * KT, [(bank[plan.bank(("dt",))][0:64, :], lambda w, k: w[:, s, k * 64:(k + 1) * 64], KT,
                          lambda ins: plan.done(ins, ("dt",))),
                         (dst(("xs", 0, 0)), wide_w(MB0 + 1, 0), KT, lambda ins: plan.done(ins, ("xs", 0, 0))),
                         (dst(("xs", 0, 1)), wide_w(MB0 + 1, 1), KT, lambda ins: plan.done(ins, ("xs", 0, 1)))])

        def dt_turns():
            pe.wait_ge(dt_dve, 4)
            key = ("tk", 0)
            plan.wait_free(pe, key)
            for i, src in enumerate((dtf, elf)):
                for t in range(4):
                    c = (4 * i + t) * 64
                    ins = pe.transpose(bank[plan.bank(key)][:, c:c + 64], src[:, t * P:(t + 1) * P], ident[0:64, 0:64])
            plan.done(ins, key)
            key = ("tk", 1)
            plan.wait_free(pe, key)
            for t in range(2):
                ins = pe.transpose(bank[plan.bank(key)][:, t * 64:(t + 1) * 64], atf[:, t * P:(t + 1) * P], ident[0:64, 0:64])
            plan.done(ins, key)
            key = ("cd",)
            plan.wait_free(pe, key)
            plan.done(pe.matmul(bank[plan.bank(key)][:, 0:96], ones[0:64, :], dg[:, :], start=True, stop=True), key)

        def turns(key, src):
            plan.wait_free(pe, key)
            for t in range(4):
                r = slice(t * P, (t + 1) * P)
                ins = pe.transpose(bank[plan.bank(key)][:, r], src[:, r], ident[:, :])
            plan.done(ins, key)

        def at_rows(p, d, i):
            key = ("row", p, d, i)
            plan.wait_free(pe, key)
            for jj in range(2):
                r = 32 * d + 4 * p + 2 * i + jj
                for half in (ath, atl):
                    ins = pe.matmul(bank[plan.bank(key)][:, jj * SEQ:(jj + 1) * SEQ], identr[:, r:r + 1].to_broadcast([64, P]),
                                    half[:, :], start=(half is ath), stop=(half is atl))
            plan.done(ins, key)

        flat = lambda x: x[:, :, :].rearrange("p a b -> p (a b)")
        y_tiles = (lambda k: flat(hh)[:, k * SEQ:(k + 1) * SEQ]), (lambda k: flat(hl)[:, k * SEQ:(k + 1) * SEQ])

        def out_w(m):
            return lambda w, k: w[:, (OM0 + m) % 2, k * P:(k + 1) * P]

        def mb_early(ks):
            need_slab(OM0 + 1)
            early(1, [(("y", 1, m), out_w(m)) for m in range(2)], ks, *y_tiles, 2)

        for g in range(MB_GROUPS + 2):
            p, q = g - 1, g - 2
            G, S, Q = g < MB_GROUPS, 0 <= p < MB_GROUPS, q >= 0
            sl = MB0 + 1 + 3 * g
            if G and g:
                need_slab(sl)
                project(("xs", g, 0), sl, 0)
            if S:
                for f in range(2):
                    pe.wait_ge(conv_silu, 4 * p + f + 1)
                    turns(("tx", p, f), xf[:, f, :])
                pe.wait_ge(conv_silu, 4 * p + 4)
                turns(("tb", p), bf[:, p % 2, :])
                key = ("cb", p)
                plan.wait_free(pe, key)
                for t in range(2):
                    r = slice(t * P, (t + 1) * P)
                    ins = pe.matmul(bank[plan.bank(key)][:, r], bf[:, p % 2, r], cf[:, p % 2, r], start=True, stop=True)
                plan.done(ins, key)
            if G and g:
                project(("xs", g, 1), sl, 1)
            if S:
                at_rows(p, 0, 0)
                at_rows(p, 0, 1)
            if G:
                need_slab(sl + 1)
                project(("b", g), sl + 1, 0)
            if g == 0:
                dt_turns()
            if S:
                plan.wait_emptied(pe, ("tb", p))
                for d in range(2):
                    pe.wait_ge(scaled_ready, 7 * p + 2 * d + 2)
                    key = ("st", p, d)
                    plan.wait_free(pe, key)
                    b = bank[plan.bank(key)]
                    pe.matmul(b[:, 0:256], btok[:, 2, :], wx[d][:, 0, :], start=True, stop=False)
                    pe.matmul(b[:, 0:256], btok[:, 3, :], wx[d][:, 1, :], start=False, stop=True)
                    plan.done(pe.matmul(b[:, 256:512], btok[:, d, :], wx[d][:, 2, :], start=True, stop=True), key)
                at_rows(p, 1, 0)
                at_rows(p, 1, 1)
            if g == MB_GROUPS:
                mb_early(range(0, 4))
            if G:
                project(("c", g), sl + 1, 1, SEQ)
            if Q:
                if not S:
                    mb_early(range(12, 14))
                key = ("yt", q)
                pe.wait_ge(yn_ready, q + 1)
                plan.wait_free(pe, key)
                for f in range(2):
                    for t in range(2):
                        ins = pe.transpose(bank[plan.bank(key)][:, f * 256 + t * P:f * 256 + (t + 1) * P],
                                           yg[:, t * 256 + f * P:t * 256 + (f + 1) * P], ident[:, :])
                plan.done(ins, key)
            if S:
                for d in range(2):
                    key = ("off", p, d)
                    plan.wait_emptied(pe, ("st", p, d))
                    plan.wait_free(pe, key)
                    for t in range(2):
                        h = hs if t == d else h1
                        ins = pe.matmul(bank[plan.bank(key)][:, t * 256:(t + 1) * 256], cf[:, p % 2, t * P:(t + 1) * P],
                                        h[:, d, :], start=True, stop=True)
                    plan.done(ins, key)
            if G:
                key = ("z", g)
                need_slab(sl + 2)
                plan.wait_free(pe, key)
                s = (sl + 2) % 2
                for t in range(2):
                    dst, r = bank[plan.bank(key)][:, t * 256:(t + 1) * 256], slice(t * P, (t + 1) * P)
                    for k in range(KT):
                        c = slice(k * 256, (k + 1) * 256)
                        pe.matmul(dst, hh[:, k, r], wh[:, s, c], start=(k == 0), stop=False)
                        pe.matmul(dst, hl[:, k, r], wh[:, s, c], start=False, stop=False)
                        ins = pe.matmul(dst, hh[:, k, r], wl[:, s, c], start=False, stop=(k == KT - 1))
                plan.done(ins, key)
            if g == MB_GROUPS:
                mb_early(range(4, 12))
            if S:
                key = ("dg", p)
                plan.wait_free(pe, key)
                pe.wait_ge(scaled_ready, 7 * p + 6)
                for d in range(2):
                    for j in range(4):
                        if j % 2 == 0:
                            pe.wait_ge(w_ready, 4 * p + 2 * d + j // 2 + 1)
                        for t in range(2):
                            ins = pe.matmul(bank[7][:, t * 256 + j * HD:t * 256 + (j + 1) * HD], wd[d][j // 2][:, j % 2, t, :],
                                            dx[d][:, t, j * HD:(j + 1) * HD], start=(d == 0 and j == 0 and t == 0),
                                            stop=(d == 1 and j == 3 and t == 1), skip_group_check=True)
                plan.done(ins, key)
        pe.wait_ge(yl_ready, 2 * KT)
        for m in range(KT):
            need_slab(OM0 + m)
            key = ("y", 1, m)
            plan.wait_free(pe, key)
            plan.done(gemm(bank[plan.bank(key)][:, 0:SEQ], out_w(m), *y_tiles, 2 * KT, k0=14 if m < 2 else 0), key)
        y_square_sum(("ss", 1, 0), SEQ)
        square_sum(("ss2", 1, 0), SEQ)
        ffn_pe(1, SEQ, 4 * KT)
        for half in range(2):
            pe.wait_ge(x_new, 3 * KT + 4 * half + 4)
            for t in range(2):
                key = ("out", t, half)
                plan.wait_free(pe, key)
                for c in range(4):
                    ins = pe.transpose(bank[plan.bank(key)][:, c * P:(c + 1) * P], xT[:, 4 * half + c, t * P:(t + 1) * P],
                                       ident[:, :])
                plan.done(ins, key)

    ctx.close()


INPUTS = ["x", "c", "ctx", "c_ctx", "ada_w", "ada_b", "pre_norm", "post_norm", "hg_w_in", "hg_w_out", "hg_norm",
          "hg_lb_logits", "mb_w_in", "mb_conv_w", "mb_conv_b", "mb_dt_bias", "mb_a_log", "mb_d", "mb_norm", "mb_w_out",
          "ffn_w_up", "ffn_conv_w", "ffn_conv_b", "ffn_w_down"]


def kernel(**inputs):
    import numpy as _np
    import concourse.bacc as _bacc
    from concourse import mybir as _mybir
    from concourse.bass_utils import run_bass_kernel_spmd as _run

    nc = _bacc.Bacc("TRN2", target_bir_lowering=False, num_devices=1, dynamic_dma_scratch_size=1024)
    arrays, aps = {}, {}
    for name in INPUTS:
        arr = _np.ascontiguousarray(inputs[name])
        arrays[f"in_{name}"] = arr
        aps[name] = nc.dram_tensor(f"in_{name}", arr.shape, _mybir.dt.from_np(arr.dtype), kind="ExternalInput").ap()
    out = nc.dram_tensor("out_x", (1, SEQ, D), _mybir.dt.float32, kind="ExternalOutput").ap()
    program(nc, aps, out)
    r = _run(nc, [arrays], core_ids=[0])
    return r.results[0]["out_x"]
```
